# Optimizing a Trainium2 kernel written in Bass

```python
import math
import jax, jax.numpy as jnp
from jax import lax
import numpy as np

D_MODEL = 1024
BATCH = 1
SEQ = 256
DEPTH = 1

N_HEADS = 8
HEAD_DIM = 128
N_KV_GROUPS = 2
HEADS_PER_GROUP = N_HEADS // N_KV_GROUPS
KV_WIDTH = N_KV_GROUPS * HEAD_DIM
NSA_WIDTH = N_HEADS * HEAD_DIM
N_NSA_BRANCHES = 3
CMP_BLOCK = 32
CMP_STRIDE = 16
CMP_HIDDEN = 256
SEL_BLOCK = 64
N_SELECT = 8
WINDOW = 512
QUERY_BLOCK = 128
SEL_QUERY_CHUNK = 16
ROPE_THETA = 10000.0
LRU_WIDTH = D_MODEL
LRU_BLOCKS = 4
LRU_BLOCK_WIDTH = LRU_WIDTH // LRU_BLOCKS
CONV_WIDTH = 4
LRU_C = 8.0
N_BRANCHES = 2
N_EXPERTS = 32
TOP_K = 4
D_FF = D_MODEL
SWIGLU_LIMIT = 7.0
SWIGLU_ALPHA = 1.702
EXPERT_ROW_BLOCK = 256
RMS_EPS = 1e-6
NEG_INF = -1e30
IN_SPLITS = (NSA_WIDTH, 2 * N_NSA_BRANCHES * KV_WIDTH, N_HEADS * N_NSA_BRANCHES, LRU_WIDTH, LRU_WIDTH, N_BRANCHES * D_MODEL)
D_IN_TOTAL = sum(IN_SPLITS)

kernel_name = "hybrid_nsa_rglru_moe_adaln"

def rms_norm(x, g):
    xf = x.astype(jnp.float32)
    y = xf * lax.rsqrt(jnp.mean(xf * xf, axis=-1, keepdims=True) + RMS_EPS)
    return (y * g.astype(jnp.float32)).astype(x.dtype)

def rope_tables(positions):
    inv = ROPE_THETA ** (-jnp.arange(0, HEAD_DIM, 2, dtype=jnp.float32) / HEAD_DIM)
    ang = positions.astype(jnp.float32)[..., None] * inv
    return jnp.cos(ang), jnp.sin(ang)

def apply_rope(x, cos, sin):
    extra = x.ndim - 3
    shp = cos.shape[:2] + (1,) * extra + cos.shape[-1:]
    cos, sin = cos.reshape(shp), sin.reshape(shp)
    x1, x2 = jnp.split(x.astype(jnp.float32), 2, axis=-1)
    return jnp.concatenate([x1 * cos - x2 * sin, x2 * cos + x1 * sin], axis=-1).astype(x.dtype)

def masked_softmax(s, mask):
    s = jnp.where(mask, s.astype(jnp.float32), NEG_INF)
    return jnp.where(mask, jax.nn.softmax(s, axis=-1), 0.0)

def block_overlap(n_cmp, n_blk):
    cs = np.arange(n_cmp)[:, None] * CMP_STRIDE
    js = np.arange(n_blk)[None, :] * SEL_BLOCK
    m = (cs <= js + SEL_BLOCK - 1) & (cs + CMP_BLOCK - 1 >= js)
    return jnp.asarray(m.astype(np.float32))

def nsa_attention(q, k_cmp, v_cmp, k_slc, v_slc, k_win, v_win, gates, cos, sin,
                  q_norm_g, k_norm_g, cmp_pe_k, cmp_pe_v, cmp_wk1, cmp_wk2, cmp_wv1, cmp_wv2):
    B, S = q.shape[0], q.shape[1]
    scale = HEAD_DIM ** -0.5
    t_pos = jnp.arange(S)
    q = rms_norm(q, q_norm_g)
    q_rot = apply_rope(q, cos, sin)

    n_cmp = (S - CMP_BLOCK) // CMP_STRIDE + 1
    blk_idx = np.arange(n_cmp)[:, None] * CMP_STRIDE + np.arange(CMP_BLOCK)[None, :]

    def compress(t, pe, w1, w2):
        blocks = t[:, blk_idx] + pe[:, None, :]
        blocks = blocks.transpose(0, 1, 3, 2, 4).reshape(B, n_cmp, N_KV_GROUPS, CMP_BLOCK * HEAD_DIM)
        return jax.nn.gelu(blocks @ w1) @ w2

    kc = rms_norm(compress(k_cmp, cmp_pe_k, cmp_wk1, cmp_wk2), k_norm_g[0])
    vc = compress(v_cmp, cmp_pe_v, cmp_wv1, cmp_wv2)
    cmp_end = jnp.arange(n_cmp) * CMP_STRIDE + CMP_BLOCK - 1
    cmp_mask = cmp_end[None, :] <= t_pos[:, None]
    s_cmp = jnp.einsum('bsghd,bcgd->bghsc', q, kc) * scale
    p_cmp = masked_softmax(s_cmp, cmp_mask)
    o_cmp = jnp.einsum('bghsc,bcgd->bsghd', p_cmp.astype(vc.dtype), vc)

    n_blk = S // SEL_BLOCK
    n_sel = min(N_SELECT, n_blk)
    imp = jnp.einsum('bghsc,cj->bgsj', p_cmp, block_overlap(n_cmp, n_blk))
    blk = jnp.arange(n_blk)[None, :]
    cur = (t_pos // SEL_BLOCK)[:, None]
    causal_blk = blk <= cur
    forced = (blk == 0) | (blk == cur) | (blk == cur - 1)
    score = jnp.where(forced, 1e6, jnp.where(causal_blk, imp, -1e6))
    top_val, sel_idx = lax.top_k(score, n_sel)
    sel_ok = top_val > -1.0

    k_sel = rms_norm(k_slc, k_norm_g[1])
    k_sel = apply_rope(k_sel, cos, sin)
    k_blk = k_sel.reshape(B, n_blk, SEL_BLOCK, N_KV_GROUPS, HEAD_DIM).transpose(0, 3, 1, 2, 4)
    v_blk = v_slc.reshape(B, n_blk, SEL_BLOCK, N_KV_GROUPS, HEAD_DIM).transpose(0, 3, 1, 2, 4)
    b_ix = jnp.arange(B)[:, None, None]
    g_ix = jnp.arange(N_KV_GROUPS)[None, :, None]
    qc_len = SEL_QUERY_CHUNK

    def sel_chunk(s0):
        qc = lax.dynamic_slice_in_dim(q_rot, s0, qc_len, axis=1)
        ic = lax.dynamic_slice_in_dim(sel_idx, s0, qc_len, axis=2)
        okc = lax.dynamic_slice_in_dim(sel_ok, s0, qc_len, axis=2)
        flat = ic.reshape(B, N_KV_GROUPS, qc_len * n_sel)
        kg = k_blk[b_ix, g_ix, flat].reshape(B, N_KV_GROUPS, qc_len, n_sel, SEL_BLOCK, HEAD_DIM)
        vg = v_blk[b_ix, g_ix, flat].reshape(B, N_KV_GROUPS, qc_len, n_sel, SEL_BLOCK, HEAD_DIM)
        s = jnp.einsum('bqghd,bgqnkd->bghqnk', qc, kg) * scale
        kpos = ic[..., None] * SEL_BLOCK + jnp.arange(SEL_BLOCK)
        tq = s0 + jnp.arange(qc_len)
        mask = (kpos <= tq[:, None, None]) & okc[..., None]
        mask = mask[:, :, None].reshape(B, N_KV_GROUPS, 1, qc_len, n_sel * SEL_BLOCK)
        p = masked_softmax(s.reshape(B, N_KV_GROUPS, HEADS_PER_GROUP, qc_len, n_sel * SEL_BLOCK), mask)
        p = p.reshape(s.shape).astype(vg.dtype)
        return jnp.einsum('bghqnk,bgqnkd->bqghd', p, vg)

    o_slc = lax.map(sel_chunk, jnp.arange(S // qc_len) * qc_len)
    o_slc = jnp.moveaxis(o_slc, 0, 1).reshape(B, S, N_KV_GROUPS, HEADS_PER_GROUP, HEAD_DIM)

    k_w = apply_rope(rms_norm(k_win, k_norm_g[2]), cos, sin)
    k_pad = jnp.pad(k_w, ((0, 0), (WINDOW, 0), (0, 0), (0, 0)))
    v_pad = jnp.pad(v_win, ((0, 0), (WINDOW, 0), (0, 0), (0, 0)))
    span = WINDOW + QUERY_BLOCK

    def win_block(s0):
        qb = lax.dynamic_slice_in_dim(q_rot, s0, QUERY_BLOCK, axis=1)
        kb = lax.dynamic_slice_in_dim(k_pad, s0, span, axis=1)
        vb = lax.dynamic_slice_in_dim(v_pad, s0, span, axis=1)
        s = jnp.einsum('bqghd,bkgd->bghqk', qb, kb) * scale
        tq = (s0 + jnp.arange(QUERY_BLOCK))[:, None]
        kp = (s0 - WINDOW + jnp.arange(span))[None, :]
        mask = (kp <= tq) & (kp > tq - WINDOW) & (kp >= 0)
        p = masked_softmax(s, mask).astype(vb.dtype)
        return jnp.einsum('bghqk,bkgd->bqghd', p, vb)

    o_win = lax.map(win_block, jnp.arange(S // QUERY_BLOCK) * QUERY_BLOCK)
    o_win = jnp.moveaxis(o_win, 0, 1).reshape(B, S, N_KV_GROUPS, HEADS_PER_GROUP, HEAD_DIM)

    o = gates[..., 0:1] * o_cmp + gates[..., 1:2] * o_slc + gates[..., 2:3] * o_win
    return o.reshape(B, S, NSA_WIDTH)

def linear_combine(left, right):
    a_l, b_l = left
    a_r, b_r = right
    return a_l * a_r, a_r * b_l + b_r

def rg_lru_branch(xb, gb, conv_w, conv_b, lru_wa, lru_ba, lru_wx, lru_bx, lru_lambda):
    B, S = xb.shape[0], xb.shape[1]
    xc = lax.conv_general_dilated(xb, conv_w[:, None, :], window_strides=(1,),
                                  padding=[(CONV_WIDTH - 1, 0)],
                                  dimension_numbers=('NWC', 'WIO', 'NWC'),
                                  feature_group_count=LRU_WIDTH) + conv_b
    xblk = xc.reshape(B, S, LRU_BLOCKS, LRU_BLOCK_WIDTH)
    r = jax.nn.sigmoid(jnp.einsum('bshi,hij->bshj', xblk, lru_wa).reshape(B, S, LRU_WIDTH) + lru_ba)
    i = jax.nn.sigmoid(jnp.einsum('bshi,hij->bshj', xblk, lru_wx).reshape(B, S, LRU_WIDTH) + lru_bx)
    log_a = -LRU_C * r.astype(jnp.float32) * jax.nn.softplus(-lru_lambda.astype(jnp.float32))
    a = jnp.exp(log_a)
    mult = jnp.sqrt(-jnp.expm1(2.0 * log_a))
    u = mult * (i * xc).astype(jnp.float32)
    _, h = lax.associative_scan(linear_combine, (a, u), axis=1)
    return jax.nn.gelu(gb) * h.astype(xb.dtype)

def swiglu_expert(xb, w1, b1, w2, b2):
    hcat = xb @ w1 + b1
    x_glu = jnp.minimum(hcat[:, 0::2], SWIGLU_LIMIT)
    x_lin = jnp.clip(hcat[:, 1::2], -SWIGLU_LIMIT, SWIGLU_LIMIT)
    act = x_glu * jax.nn.sigmoid(SWIGLU_ALPHA * x_glu) * (x_lin + 1)
    return act @ w2 + b2

def moe_ffn(h, router_w, router_b, w1, b1, w2, b2):
    B, S, D = h.shape
    T = B * S
    hf = h.reshape(T, D)
    logits = (hf @ router_w + router_b).astype(jnp.float32)
    top_logit, top_e = lax.top_k(logits, TOP_K)
    top_w = jax.nn.softmax(top_logit, axis=-1)
    n_assign = T * TOP_K
    e_flat = top_e.reshape(-1)
    order = jnp.argsort(e_flat)
    e_sorted = e_flat[order]
    tok_sorted = order // TOP_K
    counts = jnp.zeros((N_EXPERTS,), jnp.int32).at[e_flat].add(1)
    padded = (counts + EXPERT_ROW_BLOCK - 1) // EXPERT_ROW_BLOCK * EXPERT_ROW_BLOCK
    pad_end = jnp.cumsum(padded)
    pad_start = pad_end - padded
    grp_start = jnp.cumsum(counts) - counts
    dest_sorted = pad_start[e_sorted] + jnp.arange(n_assign) - grp_start[e_sorted]
    n_rows = -(-(n_assign + N_EXPERTS * (EXPERT_ROW_BLOCK - 1)) // EXPERT_ROW_BLOCK) * EXPERT_ROW_BLOCK
    n_row_blocks = n_rows // EXPERT_ROW_BLOCK
    src_tok = jnp.zeros((n_rows,), jnp.int32).at[dest_sorted].set(tok_sorted)
    used = jnp.zeros((n_rows,), jnp.bool_).at[dest_sorted].set(True)
    buf = jnp.where(used[:, None], hf[src_tok], 0)
    blk_e = jnp.minimum(jnp.searchsorted(pad_end, jnp.arange(n_row_blocks) * EXPERT_ROW_BLOCK, side='right'),
                        N_EXPERTS - 1)

    def expert_block(args):
        xb, e = args
        return swiglu_expert(xb, w1[e], b1[e], w2[e], b2[e])

    ybuf = lax.map(expert_block, (buf.reshape(n_row_blocks, EXPERT_ROW_BLOCK, D), blk_e)).reshape(n_rows, D)
    dest = jnp.zeros((n_assign,), jnp.int32).at[order].set(dest_sorted).reshape(T, TOP_K)
    out = jnp.einsum('tk,tkd->td', top_w.astype(h.dtype), ybuf[dest])
    return out.reshape(B, S, D)

def hybrid_layer(x, c, cos, sin, ada_w, ada_b, norm1_g, w_in, q_norm_g, k_norm_g,
                 cmp_pe_k, cmp_pe_v, cmp_wk1, cmp_wk2, cmp_wv1, cmp_wv2,
                 conv_w, conv_b, lru_wa, lru_ba, lru_wx, lru_bx, lru_lambda,
                 w_branch_out, w_out, norm2_g, router_w, router_b, moe_w1, moe_b1, moe_w2, moe_b2):
    B, S, D = x.shape
    mod = jnp.einsum('bd,de->be', jax.nn.silu(c), ada_w) + ada_b
    shift1, scale1, gate1, shift2, scale2, gate2 = [m[:, None, :] for m in jnp.split(mod, 6, axis=-1)]

    h = rms_norm(x, norm1_g) * (1 + scale1) + shift1
    proj = h @ w_in
    split_points = np.cumsum(IN_SPLITS)[:-1].tolist()
    q, kv, nsa_g, lru_x, lru_g, merge_g = jnp.split(proj, split_points, axis=-1)
    q = q.reshape(B, S, N_KV_GROUPS, HEADS_PER_GROUP, HEAD_DIM)
    k_cmp, v_cmp, k_slc, v_slc, k_win, v_win = [t.reshape(B, S, N_KV_GROUPS, HEAD_DIM)
                                                 for t in jnp.split(kv, 2 * N_NSA_BRANCHES, axis=-1)]
    nsa_gates = jax.nn.sigmoid(nsa_g.reshape(B, S, N_KV_GROUPS, HEADS_PER_GROUP, N_NSA_BRANCHES))
    o_nsa = nsa_attention(q, k_cmp, v_cmp, k_slc, v_slc, k_win, v_win, nsa_gates, cos, sin,
                          q_norm_g, k_norm_g, cmp_pe_k, cmp_pe_v, cmp_wk1, cmp_wk2, cmp_wv1, cmp_wv2)
    o_lru = rg_lru_branch(lru_x, lru_g, conv_w, conv_b, lru_wa, lru_ba, lru_wx, lru_bx, lru_lambda)
    y_nsa = o_nsa @ w_branch_out[:NSA_WIDTH]
    y_lru = o_lru @ w_branch_out[NSA_WIDTH:]
    g = jax.nn.sigmoid(merge_g).reshape(B, S, N_BRANCHES, D)
    merged = g[:, :, 0] * y_nsa + g[:, :, 1] * y_lru
    x = x + gate1 * (merged @ w_out)

    h2 = rms_norm(x, norm2_g) * (1 + scale2) + shift2
    x = x + gate2 * moe_ffn(h2, router_w, router_b, moe_w1, moe_b1, moe_w2, moe_b2)
    return x

def setup_inputs(seed: int = 0) -> dict:
    key = jax.random.key(seed)
    ks = iter(jax.random.split(key, 40))
    L = DEPTH

    def nrm(shape, scale):
        return jax.random.normal(next(ks), shape, jnp.float32) * scale

    def gain(shape):
        return 1.0 + nrm(shape, 0.02)

    x = nrm((BATCH, SEQ, D_MODEL), 1.0)
    c = nrm((BATCH, D_MODEL), 1.0)
    start = jax.random.randint(next(ks), (BATCH, 1), 0, 4096, dtype=jnp.int32)
    positions = start + jnp.arange(SEQ, dtype=jnp.int32)[None, :]
    u = jax.random.uniform(next(ks), (L, LRU_WIDTH), jnp.float32, minval=0.9, maxval=0.999)
    p = u ** (1.0 / LRU_C)
    lru_lambda = jnp.log(p) - jnp.log1p(-p)
    return {
        "x": x,
        "c": c,
        "positions": positions,
        "ada_w": nrm((L, D_MODEL, 6 * D_MODEL), 0.5 * D_MODEL ** -0.5),
        "ada_b": nrm((L, 6 * D_MODEL), 0.02),
        "norm1_g": gain((L, D_MODEL)),
        "w_in": nrm((L, D_MODEL, D_IN_TOTAL), D_MODEL ** -0.5),
        "q_norm_g": gain((L, HEAD_DIM)),
        "k_norm_g": gain((L, N_NSA_BRANCHES, HEAD_DIM)),
        "cmp_pe_k": nrm((L, CMP_BLOCK, HEAD_DIM), 0.2),
        "cmp_pe_v": nrm((L, CMP_BLOCK, HEAD_DIM), 0.2),
        "cmp_wk1": nrm((L, CMP_BLOCK * HEAD_DIM, CMP_HIDDEN), (CMP_BLOCK * HEAD_DIM) ** -0.5),
        "cmp_wk2": nrm((L, CMP_HIDDEN, HEAD_DIM), CMP_HIDDEN ** -0.5),
        "cmp_wv1": nrm((L, CMP_BLOCK * HEAD_DIM, CMP_HIDDEN), (CMP_BLOCK * HEAD_DIM) ** -0.5),
        "cmp_wv2": nrm((L, CMP_HIDDEN, HEAD_DIM), CMP_HIDDEN ** -0.5),
        "conv_w": nrm((L, CONV_WIDTH, LRU_WIDTH), CONV_WIDTH ** -0.5),
        "conv_b": nrm((L, LRU_WIDTH), 0.02),
        "lru_wa": nrm((L, LRU_BLOCKS, LRU_BLOCK_WIDTH, LRU_BLOCK_WIDTH), LRU_BLOCK_WIDTH ** -0.5),
        "lru_ba": nrm((L, LRU_WIDTH), 0.02),
        "lru_wx": nrm((L, LRU_BLOCKS, LRU_BLOCK_WIDTH, LRU_BLOCK_WIDTH), LRU_BLOCK_WIDTH ** -0.5),
        "lru_bx": nrm((L, LRU_WIDTH), 0.02),
        "lru_lambda": lru_lambda,
        "w_branch_out": nrm((L, NSA_WIDTH + LRU_WIDTH, D_MODEL), NSA_WIDTH ** -0.5),
        "w_out": nrm((L, D_MODEL, D_MODEL), D_MODEL ** -0.5),
        "norm2_g": gain((L, D_MODEL)),
        "router_w": nrm((L, D_MODEL, N_EXPERTS), D_MODEL ** -0.5),
        "router_b": nrm((L, N_EXPERTS), 0.01),
        "moe_w1": nrm((L, N_EXPERTS, D_MODEL, 2 * D_FF), D_MODEL ** -0.5),
        "moe_b1": nrm((L, N_EXPERTS, 2 * D_FF), 0.02),
        "moe_w2": nrm((L, N_EXPERTS, D_FF, D_MODEL), D_FF ** -0.5),
        "moe_b2": nrm((L, N_EXPERTS, D_MODEL), 0.02),
    }

def reference(x, c, positions, ada_w, ada_b, norm1_g, w_in, q_norm_g, k_norm_g,
              cmp_pe_k, cmp_pe_v, cmp_wk1, cmp_wk2, cmp_wv1, cmp_wv2,
              conv_w, conv_b, lru_wa, lru_ba, lru_wx, lru_bx, lru_lambda,
              w_branch_out, w_out, norm2_g, router_w, router_b, moe_w1, moe_b1, moe_w2, moe_b2):
    cos, sin = rope_tables(positions)
    for l in range(DEPTH):
        x = hybrid_layer(x, c, cos, sin, ada_w[l], ada_b[l], norm1_g[l], w_in[l], q_norm_g[l], k_norm_g[l],
                         cmp_pe_k[l], cmp_pe_v[l], cmp_wk1[l], cmp_wk2[l], cmp_wv1[l], cmp_wv2[l],
                         conv_w[l], conv_b[l], lru_wa[l], lru_ba[l], lru_wx[l], lru_bx[l], lru_lambda[l],
                         w_branch_out[l], w_out[l], norm2_g[l], router_w[l], router_b[l],
                         moe_w1[l], moe_b1[l], moe_w2[l], moe_b2[l])
    return x


_drawn_inputs = setup_inputs


def setup_inputs(seed=0):
    import zlib

    import numpy as np

    out = dict(_drawn_inputs(seed))
    spreads = {}
    factors = {'norm1_g': 8.0,
     'q_norm_g': 8.0,
     'k_norm_g': 8.0,
     'cmp_pe_k': 8.0,
     'cmp_pe_v': 17.841,
     'cmp_wk1': 2.928,
     'cmp_wk2': 2.824,
     'conv_b': 3.449,
     'lru_ba': 22.768,
     'lru_bx': 8.0,
     'norm2_g': 10.757,
     'router_b': 27.653,
     'moe_b1': 26.442,
     'moe_b2': 64.0}
    for name, (base, spread) in spreads.items():
        noise = np.random.default_rng([zlib.crc32(name.encode()), seed]).standard_normal(out[name].shape)
        drawn = base * np.exp(spread * noise) if base else spread * noise
        out[name] = __import__('jax').numpy.asarray(drawn.astype(out[name].dtype))
    for name, factor in factors.items():
        out[name] = (out[name] * factor).astype(out[name].dtype)
    return out
```

```python
from contextlib import ExitStack

import numpy as np

import concourse.bass as bass
from concourse import mybir

ALU = mybir.AluOpType
ACT = mybir.ActivationFunctionType
AX = mybir.AxisListType
F32 = mybir.dt.float32
BF16 = mybir.dt.bfloat16
I32 = mybir.dt.int32
U32 = mybir.dt.uint32

P = 128
D = 1024
T = 256
TT = T // P
KD = D // P
NH, DH, NG, HPG = 8, 128, 2, 4
CMP_BLOCK, CMP_STRIDE = 32, 16
N_CMP = (T - CMP_BLOCK) // CMP_STRIDE + 1
CMP_HIDDEN = 256
LRU_C = 8.0
NE = 32
TOPK = 4
FF = 1024
CAP = 64
MORE = T // CAP - 1
XP = (T * TOPK - 1) // CAP
NPASS = NE + XP
LIMIT, ALPHA = 7.0, 1.702
EPS = 1e-6
NEG = -1e30
SCALE = float(DH) ** -0.5

Q_OFF = 0
KCMP_OFF = NH * DH
KSLC_OFF = KCMP_OFF + 2 * NG * DH
KWIN_OFF = KSLC_OFF + 2 * NG * DH
NSAG_OFF = KWIN_OFF + 2 * NG * DH
N_NSAG = NH * 3
LRUX_OFF = NSAG_OFF + N_NSAG
LRUG_OFF = LRUX_OFF + D
MERGE_OFF = LRUG_OFF + D

R_N1, R_CONVW, R_CONVB, R_BA, R_BX, R_LAM, R_N2, R_ADAB = 0, 8, 40, 48, 56, 64, 72, 80
M_SHIFT1, M_SCALE1, M_GATE1, M_SHIFT2, M_SCALE2, M_GATE2 = 0, 8, 16, 24, 32, 40

STREAM = ([("ada", 0, k) for k in range(4)]
          + [("lrux", 0), ("lrux", 1), ("lrug", 0), ("lrug", 1), ("lrugate",)]
          + [("merge", 0), ("ada", 1, 0), ("merge", 1), ("ada", 1, 1), ("merge", 2), ("ada", 1, 2), ("merge", 3), ("ada", 1, 3)]
          + [("kcmp",), ("kslc",), ("cmp", 0), ("cmp", 1), ("cmp", 2), ("cmp", 3)]
          + [("ada", 2, 0), ("kwin",), ("ada", 2, 1), ("q", 0), ("ada", 2, 2), ("q", 1), ("ada", 2, 3)]
          + [("bo", 0, 0), ("bo", 1, 0), ("bo", 0, 1), ("bo", 1, 1), ("wo", 0), ("wo", 1)])
SLOT = {u: n for n, u in enumerate(STREAM)}
NSLOT = 4
assert len(STREAM) % NSLOT == 0 and STREAM[-2:] == [("wo", 0), ("wo", 1)]

JOBS = [("lrux", 0), ("lrux", 1), ("lrug", 0), ("lrug", 1), ("r", 0), ("r", 1), ("i", 0), ("i", 1),
        ("merge", 0), ("merge", 1), ("merge", 2), ("merge", 3), ("kcmp",), ("kslc",), ("kwin",), ("q", 0), ("q", 1)]
JOB = {j: n for n, j in enumerate(JOBS)}
NJOB = len(JOBS)



def read_by(u):
    if u in JOB:
        return "job_full", JOB[u] + 1
    if u[0] == "lrugate":
        return "job_full", JOB[("i", 1)] + 1
    if u[0] == "ada":
        return "ada_used", 4 * u[1] + u[2] + 1
    if u[0] == "cmp":
        return "cmp_used", u[1] + 1
    return "branch", 2 * u[2] + u[1] + 1


UNITS = [(g, t, b) for g in range(NG) for t in range(TT) for b in range(3)]


def build_program(nc, x, c, positions, ada_w, ada_b, norm1_g, w_in, q_norm_g, k_norm_g,
                  cmp_pe_k, cmp_pe_v, cmp_wk1, cmp_wk2, cmp_wv1, cmp_wv2,
                  conv_w, conv_b, lru_wa, lru_ba, lru_wx, lru_bx, lru_lambda,
                  w_branch_out, w_out, norm2_g, router_w, router_b,
                  moe_w1, moe_b1, moe_w2, moe_b2, inv_freq, out):
    with ExitStack() as ctx:
        made = {}

        def sem(name):
            if name not in made:
                made[name] = ctx.enter_context(nc.semaphore(name))
            return made[name]

        def sb(name, shape, dt=F32):
            return ctx.enter_context(nc.sbuf_tensor(name, shape, dt))

        W1 = sb("W1", [P, KD * 2 * FF])
        W2 = sb("W2", [P, KD * D])
        ST = sb("ST", [P, NSLOT * 4096])
        xs = sb("xs", [P, TT, D])
        A1 = sb("A1", [P, KD * T])
        A2 = sb("A2", [P, KD * T])
        gate1 = sb("gate1", [P, D])
        gate2 = sb("gate2", [P, D])
        vtm = sb("vtm", [P, 2, TT, NG * DH])
        b1s = sb("b1s", [96, 2 * FF], BF16)
        ident = sb("ident", [P, P])
        pcol = sb("pcol", [P, P])
        peT = sb("peT", [P, 2 * CMP_BLOCK])
        causal = sb("causal", [P, P])
        cneg = sb("cneg", [P, TT, 16])
        gw = sb("gw", [P, KD, N_NSAG])
        rw = sb("rw", [P, KD, NE])
        rb = sb("rb", [P, NE])
        ng = sb("ng", [P, TT, N_NSAG])
        cs32 = sb("cs32", [P, KD, 32])
        ccol = sb("ccol", [P, 2 * KD])
        G1 = sb("G1", [P, KD])
        S1 = sb("S1", [P, KD])
        G2 = sb("G2", [P, KD])
        S2 = sb("S2", [P, KD])
        m3 = sb("m3", [P, 16])
        spl = sb("spl", [P, 4, KD])
        stat = sb("stat", [P, 96])
        pos_i = sb("pos_i", [P, TT], I32)
        pos_f = sb("pos_f", [P, TT])

        def cut(t, a, *shape):
            n = int(np.prod(shape))
            v = t[:, a:a + n]
            if len(shape) == 2:
                v = v.rearrange("p (a b) -> p a b", a=shape[0])
            if len(shape) == 3:
                v = v.rearrange("p (a b c) -> p a b c", a=shape[0], b=shape[1])
            return v

        hT = cut(A1, 0, KD, T)
        LXW = T + 3
        lx = cut(W1, 0, KD, LXW)
        o = KD * LXW
        xc = cut(W1, o, KD, T)
        rr = cut(W1, o + 2048, KD, T)
        ii = cut(W1, o + 4096, KD, T)
        le = cut(W1, o + 6144, KD, T)
        lt = cut(W1, o + 8192, KD, T)
        o += 10240
        QK = cut(W1, o, TT, 12, DH)
        o += 3072
        gain = cut(W1, o, 4, DH)
        cosT = cut(W1, o + 512, TT, DH // 2)
        sinT = cut(W1, o + 640, TT, DH // 2)
        xn = cut(W1, 2072, TT, D)
        praw = W1[:, 4200:4328]
        peraw = W1[0:2 * CMP_BLOCK, 4328:4456]
        modrow = W1[:, 4456:4968]
        ang = cut(W1, 12312 + 3072 + 768, TT, DH // 2)
        QR = cut(W1, 0, TT, 12, DH)
        kcT = cut(W1, 0, 4, T)
        qT = cut(W1, 3072, NH, T)
        rtmp = cut(W1, 3072, TT, 12, DH // 2)
        qrT = cut(W1, 5120, NH, T)
        kT = cut(W1, 7168, 4, T)
        LV = cut(W1, 8192, CMP_BLOCK, 64)
        LK = cut(A2, 0, CMP_BLOCK, 64)
        Sb = cut(W1, 8192, 2, HPG * T)
        uu = W1[:, 10240:10496]
        uT = cut(W1, 10496, 2, P)
        kcn = W1[0:64, 10752:10880]
        vcs = W1[0:64, 10880:11008]
        kccT = W1[:, 11008:11072]
        ksq = W1[0:64, 11072:11200]
        w2c = cut(W1, 11200, 4, DH)
        PT = cut(W1, 12312, 2, HPG * P)
        Pc = cut(W1, 12312 + 1024, HPG, 64)
        pickt = cut(W1, 12312 + 1280, 4, P)
        mod2 = cut(W1, 12312 + 1792, 2, 512)
        mg = cut(W2, 0, 2 * KD, T)
        oT = cut(W2, 4096, NH, T)
        olT = cut(W2, 6144, KD, T)
        mergedT = cut(A2, 0, KD, T)
        xn2 = cut(A2, 0, TT, D)

        def slot(u):
            n = SLOT[u] % NSLOT
            return ST[:, n * 4096:(n + 1) * 4096]

        mb = [0]

        def mine(n):
            mb[0] += n
            return mb[0] - n

        o = mine(512); xT = cut(ST, o, KD, CAP)
        o = mine(512); actT = cut(ST, o, 4, P)
        o = mine(512); ysb = ST[:, o:o + 512]
        o = mine(TT * CAP); sel = cut(ST, o, TT, CAP)
        o = mine(TT * P); selw = cut(ST, o, TT, P)
        o = mine(TT * P); selT = cut(ST, o, TT, P)
        o = mine(32); ohp = ST[0:96, o:o + 32].bitcast(BF16)
        o = mine(128); iota = ST[:, o:o + 128]
        o = mine(TT * 48); posP = cut(ST, o, TT, 48)
        o = mine(TT * 48); wP = cut(ST, o, TT, 48)
        o = mine(48); oh96 = ST[0:96, o:o + 48]
        o = mine(TT * NE); lg = cut(ST, o, TT, NE)
        o = mine(TT * NE); msk = cut(ST, o, TT, NE)
        o = mine(TT * NE); wts = cut(ST, o, TT, NE)
        o = mine(TT * NE); pos = cut(ST, o, TT, NE)
        o = mine(TT * NE); tmpe = cut(ST, o, TT, NE)
        o = mine(TT * 8); top = cut(ST, o, TT, 8)
        o = mine(TT * 8); topi = cut(ST, o, TT, 8)
        o = mine(TT * 8); topw = cut(ST, o, TT, 8)
        o = mine(8); rs = ST[:, o:o + 8]
        o = mine(NE); iotaE = ST[:, o:o + NE]
        o = mine(P); upper = ST[:, o:o + P]
        o = mine(P); ones = ST[:, o:o + P]
        o = mine(T); wT = ST[0:NE, o:o + T]
        o = mine(T); posT = ST[0:NE, o:o + T]
        o = mine(16); iota16 = ST[:, o:o + 16]
        o = mine(NE); cnt = ST[:, o:o + NE]
        o = mine(NE); xneed = ST[:, o:o + NE]
        o = mine(NE); xend = ST[:, o:o + NE]
        o = mine(NE); ohx = ST[:, o:o + NE]
        o = mine(NE); ohy = ST[:, o:o + NE]
        o = mine(8); xcol = ST[:, o:o + 8]
        o = mine(64); ohT = ST[0:NE, o:o + 64]
        o = mine(P); pick1 = ST[0:8, o:o + P]
        o = mine(16); xe_i = ST[0:1, o:o + 16].bitcast(I32)
        o = mine(2); xn_i = ST[0:1, o:o + 1].bitcast(I32)
        o = mine(D); b2s = ST[0:NE, o:o + D]
        o = mine(16); chk = ST[:, o:o + 16]
        o = mine(2); rcol = ST[:, o:o + 2]
        assert mb[0] <= 2 * 4096
        glu = A1[:, 0:512]
        lin = A1[:, 512:1024]
        sig = A1[:, 1024:1536]
        act = A1[:, 1536:2048]
        w1v = cut(W1, 0, KD, 2 * FF)
        w2v = cut(W2, 0, KD, D)

        ps = ctx.enter_context(nc.psum_tensor("ps", [P, 8, 512], F32))
        PAIR = [ps[:, 0:2, :].rearrange("p a b -> p (a b)"), ps[:, 2:4, :].rearrange("p a b -> p (a b)")]
        Hps = ps[:, 4:6, :].rearrange("p a b -> p (a b)")
        Yps = ps[:, 6, :]
        Gps = ps[:, 7, :]

        block = ctx.enter_context(nc.Block())

        def wk(w, k0, nk, c0, nc_):
            return w[k0 * P:(k0 + nk) * P, c0:c0 + nc_].rearrange("(k p) n -> p k n", p=P)

        @block.sync
        def _(sp):
            IN_COL = {"lrux": LRUX_OFF, "lrug": LRUG_OFF, "merge": MERGE_OFF, "q": Q_OFF}
            ONE_COL = {"kcmp": KCMP_OFF, "kslc": KSLC_OFF, "kwin": KWIN_OFF}
            for n, u in enumerate(STREAM):
                if n >= NSLOT:
                    name, value = read_by(STREAM[n - NSLOT])
                    sp.wait_ge(sem(name), value)
                full = sem(f"stream_full{n % NSLOT}")
                dst = slot(u)
                if u[0] == "ada":
                    sp.dma_start(dst.rearrange("p (k n) -> p k n", k=2), wk(ada_w[0], 2 * u[2], 2, 2048 * u[1], 2048)).then_inc(full, 16)
                elif u[0] in IN_COL:
                    sp.dma_start(dst.rearrange("p (k n) -> p k n", k=KD), wk(w_in[0], 0, KD, IN_COL[u[0]] + 512 * u[1], 512)).then_inc(full, 16)
                elif u[0] in ONE_COL:
                    sp.dma_start(dst.rearrange("p (k n) -> p k n", k=KD), wk(w_in[0], 0, KD, ONE_COL[u[0]], 512)).then_inc(full, 16)
                elif u[0] == "lrugate":
                    for half, w in enumerate((lru_wa, lru_wx)):
                        sp.dma_start(dst[:, 2048 * half:2048 * (half + 1)].rearrange("p (a j) -> p a j", a=8),
                                     w[0].rearrange("h (i p) j -> p (h i) j", p=P)).then_inc(full, 16)
                elif u[0] == "cmp":
                    for half, w in enumerate((cmp_wk1, cmp_wv1)):
                        sp.dma_start(dst[:, 2048 * half:2048 * (half + 1)].rearrange("p (k n) -> p k n", k=8),
                                     wk(w[0], 8 * u[1], 8, 0, CMP_HIDDEN)).then_inc(full, 16)
                elif u[0] == "bo":
                    sp.dma_start(dst.rearrange("p (k n) -> p k n", k=KD), wk(w_branch_out[0], KD * u[1], KD, 512 * u[2], 512)).then_inc(full, 16)
                elif u[0] == "wo":
                    sp.dma_start(dst.rearrange("p (k n) -> p k n", k=KD), wk(w_out[0], 0, KD, 512 * u[1], 512)).then_inc(full, 16)

            def load_w1(e, passes):
                for k in range(KD):
                    if passes is not None:
                        sp.wait_ge(sem("w1_used"), 8 * passes - (KD - 1 - k))
                    sp.dma_start(w1v[:, k, :], moe_w1[0, e, k * P:(k + 1) * P, :] if isinstance(e, int)
                                 else moe_w1[0, bass.ds(e, 1), k * P:(k + 1) * P, :].rearrange("a p n -> p (a n)")).then_inc(sem(f"w1_full{k}"), 16)

            def load_w2(e, passes):
                for s in range(4):
                    if passes is not None:
                        sp.wait_ge(sem("w2_used"), 4 * passes - (3 - s))
                    src = moe_w2[0, e] if isinstance(e, int) else moe_w2[0, bass.ds(e, 1)].rearrange("a f n -> (a f) n")
                    sp.dma_start(w2v[:, 2 * s:2 * s + 2, :], wk(src, 2 * s, 2, 0, D)).then_inc(sem(f"w2_full{s}"), 16)

            sp.wait_ge(sem("att_read"), len(UNITS))
            sp.wait_ge(sem("oT_full"), NG * TT)
            sp.wait_ge(sem("gate_read"), 4)
            load_w1(0, None)
            sp.wait_ge(sem("merged"), 2)
            load_w2(0, None)
            load_w1(1, 1)
            with sp.Fori(2, NE) as q:
                load_w1(q, q)
                load_w2(q - 1, q - 1)
            load_w2(NE - 1, NE - 1)
            sp.wait_ge(sem("xtab"), 1)
            more = sp.value_load(xn_i, min_val=0, max_val=XP)
            with sp.Fori(0, XP) as i:
                with sp.If(more > i):
                    e = sp.value_load(xe_i[0:1, bass.ds(i, 1)], min_val=0, max_val=NE - 1)
                    load_w1(e, i + NE)
                    load_w2(e, i + NE)
            sp.wait_ge(sem("out_ready"), 2)
            for t in range(TT):
                sp.dma_start(out[0, t * P:(t + 1) * P, :], xs[:, t, :]).then_inc(sem("out_stored"), 16)
            sp.wait_ge(sem("out_stored"), 16 * TT)

        @block.gpsimd
        def _(pool):
            chain = [0]

            def link(i):
                chain[0] += 1
                i.then_inc(sem("pool_chain"), 1)
                pool.wait_ge(sem("pool_chain"), chain[0])

            pool.dma_start(peraw[0:CMP_BLOCK, :], cmp_pe_k[0]).then_inc(sem("pe_in"), 16)
            pool.dma_start(peraw[CMP_BLOCK:2 * CMP_BLOCK, :], cmp_pe_v[0]).then_inc(sem("pe_in"), 16)
            for j in range(3):
                pool.dma_start(A2[32 * j:32 * j + 32, :], moe_b1[0]).then_inc(sem("b1_in"), 16)
            pool.dma_start(gw[:, :, :], wk(w_in[0], 0, KD, NSAG_OFF, N_NSAG)).then_inc(sem("small_in"), 16)
            pool.dma_start(rw[:, :, :], wk(router_w[0], 0, KD, 0, NE)).then_inc(sem("small_in"), 16)
            pool.dma_start(rb[:, :], router_b.to_broadcast((P, NE))).then_inc(sem("small_in"), 16)
            pool.dma_start(gate1[:, :], ada_b[:, M_GATE1 * P:(M_GATE1 + 8) * P].to_broadcast((P, D))).then_inc(sem("small_in"), 16)
            pool.dma_start(gate2[:, :], ada_b[:, M_GATE2 * P:(M_GATE2 + 8) * P].to_broadcast((P, D))).then_inc(sem("small_in"), 16)
            pool.dma_start(gain[:, 0, :], q_norm_g.to_broadcast((P, DH))).then_inc(sem("small_in"), 16)
            for j in range(3):
                pool.dma_start(gain[:, 1 + j, :], k_norm_g[0, j:j + 1, :].to_broadcast((P, DH))).then_inc(sem("small_in"), 16)
            pool.dma_start(ang[:, 0, :], inv_freq.to_broadcast((P, DH // 2))).then_inc(sem("small_in"), 16)
            pool.dma_start(ang[:, 1, :], inv_freq.to_broadcast((P, DH // 2))).then_inc(sem("small_in"), 16)
            pool.dma_start(pos_i[:, :], positions[0].rearrange("(t p) -> p t", p=P), allow_slow_non_contiguous=True).then_inc(sem("small_in"), 16)
            link(pool.memset(ident[:, :], 0.0))
            pool.affine_select(out=ident[:, :], in_=ident[:, :], compare_op=ALU.not_equal, fill=1.0, base=0,
                               pattern=[[-1, P]], channel_multiplier=1).then_inc(sem("ident"), 1)
            link(pool.memset(causal[:, :], 0.0))
            link(pool.memset(cneg[:, :, :], 0.0))
            link(pool.affine_select(out=causal[:, :], in_=causal[:, :], compare_op=ALU.is_ge, fill=NEG, base=0,
                                    pattern=[[-1, P]], channel_multiplier=1))
            link(pool.affine_select(out=cneg[:, :, :], in_=cneg[:, :, :], compare_op=ALU.is_ge, fill=NEG, base=1 - CMP_BLOCK,
                                    pattern=[[P, TT], [-CMP_STRIDE, 16]], channel_multiplier=1))
            pool.wait_ge(sem("b1_in"), 48)
            link(pool.tensor_copy(b1s[:, :], A2[0:96, :]))
            link(pool.tensor_tensor(A2[0:96, :], A2[0:96, :], b1s[:, :], ALU.subtract))
            link(pool.tensor_copy(b1s[32:64, :], A2[32:64, :]))
            link(pool.tensor_copy(b1s[64:96, :], A2[64:96, :]))
            link(pool.tensor_tensor(A2[64:96, :], A2[64:96, :], b1s[64:96, :], ALU.subtract))
            link(pool.tensor_copy(b1s[64:96, :], A2[64:96, :]))
            link(pool.memset(LK, 0.0))
            pool.nop().then_inc(sem("pool_masks"), 1)

            pool.wait_ge(sem("lru_done"), 1)
            for w, m in enumerate((cmp_wk2, cmp_wv2)):
                pool.dma_start(w2c[:, 2 * w:2 * w + 2, :], wk(m[0], 0, 2, 0, DH)).then_inc(sem("w2c_in"), 16)

            pool.wait_ge(sem("branch"), 4)
            pool.dma_start(b2s, moe_b2[0]).then_inc(sem("b2_in"), 16)
            for h in range(2):
                link(pool.iota(iota[:, CAP * h:CAP * (h + 1)], [[1, CAP]], base=0, channel_multiplier=0, allow_small_or_imprecise_dtypes=True))
            link(pool.iota(iotaE, [[1, NE]], base=0, channel_multiplier=0, allow_small_or_imprecise_dtypes=True))
            link(pool.iota(iota16, [[1, 16]], base=0, channel_multiplier=0, allow_small_or_imprecise_dtypes=True))
            link(pool.iota(rcol[:, 0:1], [[0, 1]], base=0, channel_multiplier=1, allow_small_or_imprecise_dtypes=True))
            link(pool.memset(ones, 1.0))
            link(pool.memset(oh96, 0.0))
            link(pool.memset(ohT, 0.0))
            link(pool.memset(upper, 1.0))
            link(pool.affine_select(out=upper, in_=upper, compare_op=ALU.is_gt, fill=0.0, base=0,
                                    pattern=[[1, P]], channel_multiplier=-1))
            pool.nop().then_inc(sem("pool_masks"), 1)

        @block.scalar
        def _(act_e):
            a = act_e
            n = [0]

            def link(i):
                n[0] += 1
                i.then_inc(sem("act_chain"), 1)
                a.wait_ge(sem("act_chain"), n[0])

            def root(n, st):
                a.wait_ge(sem("square"), n)
                a.activation(st, st, ACT.Sqrt).then_inc(sem("rsqrt"), 1)

            a.dma_start(ccol[:, 0:KD], c[0].rearrange("(k p) -> p k", p=P), allow_slow_non_contiguous=True).then_inc(sem("c_in"), 16)
            for r0, v in ((R_N1, norm1_g), (R_CONVB, conv_b), (R_BA, lru_ba), (R_BX, lru_bx), (R_LAM, lru_lambda), (R_N2, norm2_g)):
                a.dma_start(praw[r0:r0 + 8, :], v[0].rearrange("(k p) -> k p", p=P)).then_inc(sem("params_in"), 16)
            a.dma_start(praw[R_CONVW:R_CONVW + 32, :], conv_w[0].rearrange("w (k p) -> (w k) p", p=P)).then_inc(sem("params_in"), 16)
            a.dma_start(praw[R_ADAB:R_ADAB + 48, :], ada_b[0].rearrange("(k p) -> k p", p=P)).then_inc(sem("params_in"), 16)
            for t in range(TT):
                a.dma_start(xs[:, t, :], x[0, t * P:(t + 1) * P, :]).then_inc(sem("x_in"), 16)
            a.wait_ge(sem("c_in"), 16)
            a.activation(ccol[:, KD:2 * KD], ccol[:, 0:KD], ACT.Sigmoid).then_inc(sem("sig_c"), 1)
            a.wait_ge(sem("x_in"), 32)
            for t in range(TT):
                link(a.activation(xn[:, t, :], xs[:, t, :], ACT.Square, accum_out=stat[:, t:t + 1]))
            a.nop().then_inc(sem("x_sq"), 1)
            root(1, stat[:, 2:4])

            def wait_job(j):
                a.wait_ge(sem("job_full"), JOB[j] + 1)
                return PAIR[JOB[j] % 2]

            a.wait_ge(sem("lam_abs"), 1)
            a.activation(spl[:, 0, :], spl[:, 0, :], ACT.Exp).then_inc(sem("lam_exp"), 1)
            a.wait_ge(sem("lx_zero"), 1)
            for h in range(2):
                p = wait_job(("lrux", h))
                a.activation(lx[:, 4 * h:4 * h + 4, 3:3 + T], p.rearrange("p (k t) -> p k t", k=4), ACT.Copy).then_inc(sem("job_read"), 1)
            for h in range(2):
                p = wait_job(("lrug", h))
                a.activation(olT[:, 4 * h:4 * h + 4, :], p.rearrange("p (k t) -> p k t", k=4), ACT.Gelu_apprx_tanh).then_inc(sem("job_read"), 1)
            for name, dst, r0 in (("r", rr, R_BA), ("i", ii, R_BX)):
                for h in range(2):
                    p = wait_job((name, h))
                    for k in range(4):
                        q = a.activation(dst[:, 4 * h + k, :], p[:, k * T:(k + 1) * T], ACT.Sigmoid, bias=pcol[:, r0 + 4 * h + k:r0 + 4 * h + k + 1])
                    q.then_inc(sem("job_read"), 1)
            for h in range(4):
                p = wait_job(("merge", h))
                a.activation(mg[:, 4 * h:4 * h + 4, :], p.rearrange("p (k t) -> p k t", k=4), ACT.Sigmoid).then_inc(sem("job_read"), 1)
                if h == 0:
                    a.wait_ge(sem("log_a"), 1)
                    a.activation(le, rr, ACT.Exp).then_inc(sem("lru_exp"), 1)
                    a.activation(lt, rr, ACT.Tanh, scale=0.5).then_inc(sem("lru_exp"), 1)
                if h == 2:
                    a.wait_ge(sem("one_minus_a2"), 1)
                    a.activation(lt, lt, ACT.Sqrt).then_inc(sem("lru_sqrt"), 1)
            a.wait_ge(sem("angles"), 1)
            a.activation(cosT, cosT, ACT.Sin).then_inc(sem("sincos"), 1)
            a.activation(sinT, sinT, ACT.Sin).then_inc(sem("sincos"), 1)
            p = wait_job(("kcmp",))
            a.wait_ge(sem("lru_done"), 1)
            a.activation(kcT, p.rearrange("p (k t) -> p k t", k=4), ACT.Copy).then_inc(sem("job_read"), 1)
            a.wait_ge(sem("ng_full"), 1)
            a.activation(ng[:, :, :], ps[:, 4, 0:TT * N_NSAG].rearrange("p (t n) -> p t n", t=TT), ACT.Sigmoid).then_inc(sem("ng_read"), 1)

            def keys_values(j, b):
                p = wait_job(j).rearrange("p (t n) -> p t n", t=TT)
                link(a.activation(QK[:, :, 8 + 2 * b:10 + 2 * b, :], p[:, :, 0:256].rearrange("p t (g d) -> p t g d", g=2), ACT.Copy))
                a.activation(vtm[:, b, :, :], p[:, :, 256:512], ACT.Copy).then_inc(sem("job_read"), 1)

            keys_values(("kslc",), 0)
            a.wait_ge(sem("cmp_used"), 4)
            a.activation(uu, ps[:, 4, 0:CMP_HIDDEN], ACT.Gelu_apprx_tanh).then_inc(sem("cmp_gelu"), 1)
            keys_values(("kwin",), 1)
            root(2, stat[:, 64:68])
            root(3, stat[:, 64:68])
            a.wait_ge(sem("uT_full"), 1)
            a.activation(uT, ps[:, 6, 0:256].rearrange("p (a b) -> p a b", a=2), ACT.Copy).then_inc(sem("uT_read"), 1)
            for h in range(2):
                p = wait_job(("q", h)).rearrange("p (t g d) -> p t g d", t=TT, g=4)
                a.activation(QK[:, :, 4 * h:4 * h + 4, :], p, ACT.Copy).then_inc(sem("job_read"), 1)
                if h == 0:
                    root(4, stat[:, 64:72])
            root(5, stat[0:64, 80:81])
            root(6, stat[:, 64:72])
            for j in range(10):
                a.wait_ge(sem("qk_turned"), j + 1)
                dst = (qT[:, 2 * j:2 * j + 2, :] if j < 4 else qrT[:, 2 * j - 8:2 * j - 6, :] if j < 8 else kT[:, 2 * j - 16:2 * j - 14, :])
                a.activation(dst, ps[:, j % 4, :].rearrange("p (h t) -> p h t", h=2), ACT.Copy).then_inc(sem("qk_read"), 1)

            def exps(m):
                g, t, b = UNITS[m]
                a.wait_ge(sem("att_max"), m + 1)
                nk = 15 if b == 0 else P * (t + 1)
                for h in range(HPG):
                    src = Sb[:, m % 2, h * T:h * T + nk]
                    dst = Pc[:, h, 32 * g:32 * g + N_CMP] if b == 0 else src
                    i = a.activation(dst, src, ACT.Exp, scale=SCALE, bias=stat[:, 16 + 8 * (m % 2) + h:17 + 8 * (m % 2) + h],
                                     accum_out=stat[:, 32 + 8 * (m % 2) + h:33 + 8 * (m % 2) + h])
                i.then_inc(sem("att_exp"), 1)

            def turned(m):
                g, t, b = UNITS[m]
                a.wait_ge(sem("att_turned"), m + 1)
                if m >= 1:
                    a.wait_ge(sem("att_read"), m)
                if b == 0:
                    a.activation(PT[0:64, 0, :], ps[0:64, 4, :], ACT.Copy).then_inc(sem("att_pT"), 1)
                else:
                    a.activation(PT[:, 0:t + 1, :], ps[:, 4:5 + t, :], ACT.Copy).then_inc(sem("att_pT"), 1)
                if b == 2:
                    a.wait_ge(sem("att_read"), m + 1)
                    a.activation(oT[:, 4 * g:4 * g + 4, t * P:(t + 1) * P], ps[:, 6, :].rearrange("p (h q) -> p h q", h=4), ACT.Copy).then_inc(sem("oT_full"), 1)

            exps(0)
            for m in range(len(UNITS)):
                if m + 1 < len(UNITS):
                    exps(m + 1)
                turned(m)

            def expert_sigmoid(q):
                a.wait_ge(sem("glu"), q + 1)
                a.activation(sig, glu, ACT.Sigmoid, scale=ALPHA).then_inc(sem("sig"), 1)

            def expert_turned(q):
                a.wait_ge(sem("act_turned"), q + 1)
                a.activation(actT, Hps[:, 0:512].rearrange("p (j m) -> p j m", j=4), ACT.Copy).then_inc(sem("actT"), 1)
                a.activation(selT, Hps[:, 512:512 + TT * P].rearrange("p (t m) -> p t m", t=TT), ACT.Copy).then_inc(sem("selT"), 1)

            def expert_y(q):
                a.wait_ge(sem("w2_used"), (q + 1) * 4)
                a.activation(ysb, Yps, ACT.Copy).then_inc(sem("y_read"), 1)

            root(7, stat[:, 50:52])
            for t in range(TT):
                a.wait_ge(sem("top4"), t + 1)
                a.activation(topw[:, t, 0:TOPK], top[:, t, 0:TOPK], ACT.Exp, bias=stat[:, 60 + t:61 + t], accum_out=stat[:, 62 + t:63 + t]).then_inc(sem("top_exp"), 1)
            expert_sigmoid(0)
            expert_turned(0)
            with a.Fori(1, NE) as q:
                expert_sigmoid(q)
                expert_y(q - 1)
                expert_turned(q)
            expert_y(NE - 1)
            a.wait_ge(sem("xtab"), 1)
            more = a.value_load(xn_i, min_val=0, max_val=XP)
            with a.Fori(0, XP) as i:
                with a.If(more > i):
                    expert_sigmoid(i + NE)
                    expert_turned(i + NE)
                    expert_y(i + NE)

        @block.tensor
        def _(pe):
            def full(u, times=1):
                nload = lambda v: 2 if v[0] in ("lrugate", "cmp") else 1
                k = SLOT[u]
                total = sum(nload(STREAM[j]) for j in range(k % NSLOT, k + 1, NSLOT))
                pe.wait_ge(sem(f"stream_full{k % NSLOT}"), 16 * total)
                return slot(u)

            pe.wait_ge(sem("ident"), 1)
            pe.wait_ge(sem("params_in"), 16 * 8)
            pe.transpose(ps[:, 6, 0:P], praw, ident[:, :]).then_inc(sem("params_turned"), 1)
            pe.wait_ge(sem("pe_in"), 32)
            pe.transpose(ps[:, 6, P:P + 64], peraw, ident[0:64, 0:64]).then_inc(sem("params_turned"), 1)

            def ada(third, k2, bank):
                s = full(("ada", third, k2)).rearrange("p (k n) -> p k n", k=2)
                for k in range(2):
                    for g in range(4):
                        i = pe.matmul(ps[32 * g:32 * g + 32, bank, :], cs32[:, 2 * k2 + k, :], s[:, k, 512 * g:512 * g + 512],
                                      start=(k2 == 0 and k == 0), stop=(k2 == 3 and k == 1), skip_group_check=True)
                i.then_inc(sem("ada_used"), 1)

            pe.wait_ge(sem("cs32"), 1)
            for k2 in range(4):
                ada(0, k2, 7)
            pe.wait_ge(sem("params_read"), 1)
            pe.wait_ge(sem("modrow"), 1)
            for j in range(4):
                i = pe.transpose(ps[:, 6, j * P:(j + 1) * P], modrow[:, j * P:(j + 1) * P], ident[:, :])
            i.then_inc(sem("mod_turned"), 1)
            pe.wait_ge(sem("xn"), 1)
            for k in range(KD):
                for t in range(TT):
                    i = pe.transpose(ps[:, k // 2, (k % 2) * T + t * P:(k % 2) * T + (t + 1) * P], xn[:, t, k * P:(k + 1) * P], ident[:, :])
            i.then_inc(sem("x_turned"), 1)
            pe.wait_ge(sem("hT"), 1)

            def job_bank(j):
                n = JOB[j]
                if n >= 2:
                    pe.wait_ge(sem("job_read"), n - 1)
                return PAIR[n % 2]

            def rows_out(u):
                s = full(u).rearrange("p (k n) -> p k n", k=KD)
                p = job_bank(u)
                for j in range(4):
                    for k in range(KD):
                        i = pe.matmul(p[:, j * T:(j + 1) * T], s[:, k, j * P:(j + 1) * P], hT[:, k, :], start=(k == 0), stop=(k == KD - 1))
                i.then_inc(sem("job_full"), 1)

            def tokens_out(u):
                s = full(u).rearrange("p (k n) -> p k n", k=KD)
                p = job_bank(u)
                for t in range(TT):
                    for k in range(KD):
                        i = pe.matmul(p[:, t * 512:(t + 1) * 512], hT[:, k, t * P:(t + 1) * P], s[:, k, :], start=(k == 0), stop=(k == KD - 1))
                i.then_inc(sem("job_full"), 1)

            for u in (("lrux", 0), ("lrux", 1), ("lrug", 0), ("lrug", 1)):
                rows_out(u)
            s = full(("lrugate",)).rearrange("p (w a j) -> p w a j", w=2, a=8)
            pe.wait_ge(sem("conv"), 1)
            for w, name in enumerate(("r", "i")):
                for h in range(2):
                    p = job_bank((name, h))
                    for jj in range(4):
                        j = 4 * h + jj
                        b = j // 2
                        for ic in range(2):
                            i = pe.matmul(p[:, jj * T:(jj + 1) * T], s[:, w, 2 * b + ic, (j % 2) * P:(j % 2 + 1) * P],
                                          xc[:, 2 * b + ic, :], start=(ic == 0), stop=(ic == 1))
                    i.then_inc(sem("job_full"), 1)
            for h in range(4):
                rows_out(("merge", h))
                ada(1, h, 7)
            rows_out(("kcmp",))
            for t in range(TT):
                for k in range(KD):
                    if t == 0 and k == 0:
                        pe.wait_ge(sem("small_in"), 16 * 12)
                    i = pe.matmul(ps[:, 4, t * N_NSAG:(t + 1) * N_NSAG], hT[:, k, t * P:(t + 1) * P], gw[:, k, :], start=(k == 0), stop=(k == KD - 1))
            i.then_inc(sem("ng_full"), 1)
            tokens_out(("kslc",))
            pe.wait_ge(sem("cmp_rows"), 1)
            pe.wait_ge(sem("ng_read"), 1)
            for c4 in range(4):
                s = full(("cmp", c4)).rearrange("p (w l n) -> p w l n", w=2, l=8)
                for l8 in range(8):
                    l = 8 * c4 + l8
                    pe.matmul(ps[0:64, 4, 0:CMP_HIDDEN], LK[:, l, :], s[:, 0, l8, :], start=(l == 0), stop=(l == 31), skip_group_check=True)
                    i = pe.matmul(ps[64:128, 4, 0:CMP_HIDDEN], LV[:, l, :], s[:, 1, l8, :], start=(l == 0), stop=(l == 31), skip_group_check=True)
                i.then_inc(sem("cmp_used"), 1)
            ada(2, 0, 5)
            tokens_out(("kwin",))
            pe.wait_ge(sem("cmp_gelu"), 1)
            pe.wait_ge(sem("mod_read"), 1)
            for j in range(2):
                i = pe.transpose(ps[:, 6, j * P:(j + 1) * P], uu[:, j * P:(j + 1) * P], ident[:, :])
            i.then_inc(sem("uT_full"), 1)
            ada(2, 1, 5)
            tokens_out(("q", 0))
            ada(2, 2, 5)
            pe.wait_ge(sem("uT_read"), 1)
            pe.wait_ge(sem("w2c_in"), 32)
            for w in range(2):
                for j in range(2):
                    i = pe.matmul(ps[0:64, 6, 256 + w * P:256 + (w + 1) * P], uT[:, j, 64 * w:64 * w + 64], w2c[:, 2 * w + j, :],
                                  start=(j == 0), stop=(j == 1))
            i.then_inc(sem("cmp2_full"), 1)
            tokens_out(("q", 1))
            ada(2, 3, 5)
            pe.wait_ge(sem("kcn"), 1)
            pe.transpose(ps[:, 6, 0:64], kcn, ident[0:64, 0:64]).then_inc(sem("kc_turned"), 1)
            pe.wait_ge(sem("roped"), 1)
            pe.wait_ge(sem("job_read"), NJOB)
            for j in range(10):
                if j >= 4:
                    pe.wait_ge(sem("qk_read"), j - 3)
                for h in range(2):
                    for t in range(TT):
                        src = (QK[:, t, 2 * j + h, :] if j < 4 else QR[:, t, 2 * j - 8 + h, :])
                        i = pe.transpose(ps[:, j % 4, h * T + t * P:h * T + (t + 1) * P], src, ident[:, :])
                i.then_inc(sem("qk_turned"), 1)

            def scores(m):
                g, t, b = UNITS[m]
                if m >= 2:
                    pe.wait_ge(sem("att_max"), m - 1)
                for h in range(HPG):
                    hd = HPG * g + h
                    if b == 0:
                        i = pe.matmul(PAIR[m % 2][:, h * 16:h * 16 + N_CMP], qT[:, hd, t * P:(t + 1) * P], kccT[:, 32 * g:32 * g + N_CMP], start=True, stop=True)
                    else:
                        nk = P * (t + 1)
                        i = pe.matmul(PAIR[m % 2][:, h * nk:(h + 1) * nk], qrT[:, hd, t * P:(t + 1) * P], kT[:, 2 * (b - 1) + g, 0:nk], start=True, stop=True)
                i.then_inc(sem("scores"), 1)

            def turn(m):
                g, t, b = UNITS[m]
                pe.wait_ge(sem("att_p"), m + 1)
                if m >= 1:
                    pe.wait_ge(sem("att_pT"), m)
                for h in range(HPG):
                    if b == 0:
                        i = pe.transpose(ps[0:64, 4, h * P:(h + 1) * P], Pc[:, h, :], ident[:, :])
                    else:
                        for kt in range(t + 1):
                            i = pe.transpose(ps[:, 4 + kt, h * P:(h + 1) * P], Sb[:, m % 2, h * T + kt * P:h * T + (kt + 1) * P], ident[:, :])
                i.then_inc(sem("att_turned"), 1)

            def values(m):
                g, t, b = UNITS[m]
                pe.wait_ge(sem("att_pT"), m + 1)
                if b == 0:
                    if m >= 3:
                        pe.wait_ge(sem("oT_full"), m // 3)
                    i = pe.matmul(ps[:, 6, :], vcs, PT[0:64, 0, :], start=True, stop=False, skip_group_check=True)
                else:
                    for kt in range(t + 1):
                        i = pe.matmul(ps[:, 6, :], vtm[:, b - 1, kt, g * DH:(g + 1) * DH], PT[:, kt, :], start=False,
                                      stop=(b == 2 and kt == t), skip_group_check=True)
                i.then_inc(sem("att_read"), 1)

            pe.wait_ge(sem("qk_read"), 10)
            pe.wait_ge(sem("kccT"), 1)
            scores(0)
            for m in range(len(UNITS)):
                if m + 1 < len(UNITS):
                    scores(m + 1)
                turn(m)
                values(m)

            def late_modulations():
                pe.wait_ge(sem("pick"), 1)
                for third in (1, 2):
                    if third == 2:
                        pe.wait_ge(sem("mod_read"), 2)
                    for j in range(4):
                        i = pe.transpose(ps[:, 4, j * P:(j + 1) * P], mod2[:, third - 1, j * P:(j + 1) * P], ident[:, :])
                    i.then_inc(sem("mod2_turned"), 1)
                    for j in range(2):
                        n = 2 * (third - 1) + j
                        if n:
                            pe.wait_ge(sem("gate_read"), n)
                        pe.matmul(ps[:, 6, :], pickt[:, n, :], mod2[:, third - 1, :], start=True, stop=True).then_inc(sem("gate_rows"), 1)

            pe.wait_ge(sem("oT_full"), NG * TT)
            pe.wait_ge(sem("lru_done"), 1)
            for half in range(2):
                for br, src in ((0, oT), (1, olT)):
                    s = full(("bo", br, half)).rearrange("p (k n) -> p k n", k=KD)
                    if half == 1:
                        pe.wait_ge(sem("y_taken"), br + 1)
                    for j in range(4):
                        for k in range(KD):
                            i = pe.matmul(PAIR[br][:, j * T:(j + 1) * T], s[:, k, j * P:(j + 1) * P], src[:, k, :], start=(k == 0), stop=(k == KD - 1))
                    i.then_inc(sem("branch"), 1)
                if half == 0:
                    late_modulations()
            pe.wait_ge(sem("merged"), 2)
            for half in range(2):
                s = full(("wo", half)).rearrange("p (k n) -> p k n", k=KD)
                for t in range(TT):
                    for k in range(KD):
                        i = pe.matmul(PAIR[half][:, t * 512:(t + 1) * 512], mergedT[:, k, t * P:(t + 1) * P], s[:, k, :], start=(k == 0), stop=(k == KD - 1))
                i.then_inc(sem("wo_full"), 1)
            pe.wait_ge(sem("xn2"), 1)
            for k in range(KD):
                for t in range(TT):
                    i = pe.transpose(ps[:, k // 2, (k % 2) * T + t * P:(k % 2) * T + (t + 1) * P], xn2[:, t, k * P:(k + 1) * P], ident[:, :])
            i.then_inc(sem("x2_turned"), 1)
            pe.wait_ge(sem("h2T"), 1)
            for t in range(TT):
                for k in range(KD):
                    i = pe.matmul(ps[:, 4, t * NE:(t + 1) * NE], hT[:, k, t * P:(t + 1) * P], rw[:, k, :], start=(k == 0), stop=(k == KD - 1))
            i.then_inc(sem("logits"), 1)
            pe.wait_ge(sem("mask"), 1)
            pe.wait_ge(sem("pool_masks"), 2)
            pe.matmul(ps[:, 5, 0:NE], upper, msk[:, 0, :], start=True, stop=True)
            pe.matmul(ps[:, 5, NE:2 * NE], ones, msk[:, 0, :], start=True, stop=False)
            pe.matmul(ps[:, 5, NE:2 * NE], upper, msk[:, 1, :], start=False, stop=True)
            pe.matmul(ps[:, 5, 2 * NE:3 * NE], ones, msk[:, 0, :], start=True, stop=False)
            pe.matmul(ps[:, 5, 2 * NE:3 * NE], ones, msk[:, 1, :], start=False, stop=True).then_inc(sem("places"), 1)
            pe.wait_ge(sem("pos"), 1)
            for t in range(TT):
                pe.transpose(ps[0:NE, 6, t * P:(t + 1) * P], wts[:, t, :], ident[:, :])
                i = pe.transpose(ps[0:NE, 7, t * P:(t + 1) * P], pos[:, t, :], ident[:, :])
            i.then_inc(sem("routes_turned"), 1)
            pe.wait_ge(sem("ohx"), 1)
            pe.transpose(ps[0:NE, 4, 0:P], ohx, ident[:, :])
            pe.transpose(ps[0:8, 4, P:2 * P], xcol, ident[:, :]).then_inc(sem("xcols"), 1)
            pe.wait_ge(sem("wT"), 1)
            pe.wait_ge(sem("b2_in"), 16)
            pe.wait_ge(sem("x2_read"), 1)
            for t in range(TT):
                for h in range(2):
                    pe.matmul(ps[:, 2 * t + h, :], wT[:, t * P:(t + 1) * P], b2s[:, h * 512:(h + 1) * 512], start=True, stop=False, skip_group_check=True)
            pe.wait_ge(sem("ohT"), 1)
            for t in range(TT):
                pe.matmul(ps[:, 4, 256 + t * 32:256 + t * 32 + XP], posT[:, t * P:(t + 1) * P], ohT[:, 0:XP], start=True, stop=True)
                pe.matmul(ps[:, 4, 320 + t * 32:320 + t * 32 + XP], wT[:, t * P:(t + 1) * P], ohT[:, 0:XP], start=True, stop=True)
            pe.matmul(ps[:, 4, 384:384 + XP], pick1, chk[0:8, 0:XP], start=True, stop=True).then_inc(sem("xmats"), 1)

            def gather(q):
                pe.wait_ge(sem("sel"), q + 1)
                for k in range(KD):
                    for t in range(TT):
                        i = pe.matmul(Gps[:, k * CAP:(k + 1) * CAP], xn2[:, t, k * P:(k + 1) * P], sel[:, t, :], start=(t == 0), stop=(t == TT - 1))
                i.then_inc(sem("rows"), 1)

            def first(q):
                pe.wait_ge(sem("xT"), q + 1)
                pe.wait_ge(sem("ohp"), q + 1)
                if not (isinstance(q, int) and q == 0):
                    pe.wait_ge(sem("selT"), q)
                parts = [(g, b) for b in range(2) for g in range(2)]
                for g, b in parts:
                    cc = 1024 * g + 512 * b
                    pe.matmul(Hps[64 * g:64 * g + 64, b * 512:(b + 1) * 512], ohp, b1s[:, cc:cc + 512], start=True, stop=False, skip_group_check=True)
                for k in range(KD):
                    pe.wait_ge(sem(f"w1_full{k}"), (q + 1) * 16)
                    for g, b in parts:
                        cc = 1024 * g + 512 * b
                        i = pe.matmul(Hps[64 * g:64 * g + 64, b * 512:(b + 1) * 512], xT[:, k, :], w1v[:, k, cc:cc + 512],
                                      start=False, stop=(k == KD - 1), skip_group_check=True)
                    i.then_inc(sem("w1_used"), 1)

            def turn_act(q):
                pe.wait_ge(sem("act"), q + 1)
                for j in range(4):
                    pe.transpose(Hps[:, j * P:(j + 1) * P], act[:, j * P:(j + 1) * P], ident[:, :])
                pe.wait_ge(sem("selw"), q + 1)
                for t in range(TT):
                    i = pe.transpose(Hps[:, 512 + t * P:512 + (t + 1) * P], selw[:, t, :], ident[:, :])
                i.then_inc(sem("act_turned"), 1)

            def second(q):
                pe.wait_ge(sem("actT"), q + 1)
                for s in range(4):
                    pe.wait_ge(sem(f"w2_full{s}"), (q + 1) * 16)
                    for k in (2 * s, 2 * s + 1):
                        for g in range(2):
                            i = pe.matmul(Yps[64 * g:64 * g + 64, :], actT[:, k % 4, 64 * (k // 4):64 * (k // 4) + 64],
                                          w2v[:, k, g * 512:(g + 1) * 512], start=(k == 0), stop=(k == 7), skip_group_check=True)
                    i.then_inc(sem("w2_used"), 1)

            def scatter(q):
                pe.wait_ge(sem("y_read"), q + 1)
                pe.wait_ge(sem("selT"), q + 1)
                for t in range(TT):
                    for g in range(2):
                        i = pe.matmul(ps[:, 2 * t + g, :], selT[64 * g:64 * g + 64, t, :], ysb[64 * g:64 * g + 64, :], start=False, stop=False, skip_group_check=True)
                i.then_inc(sem("scattered"), 1)

            pe.wait_ge(sem("tables"), 1)
            gather(0)
            first(0)
            gather(1)
            turn_act(0)
            with pe.Fori(1, NE - 1) as q:
                first(q)
                second(q - 1)
                gather(q + 1)
                scatter(q - 1)
                turn_act(q)
            first(NE - 1)
            second(NE - 2)
            scatter(NE - 2)
            turn_act(NE - 1)
            second(NE - 1)
            scatter(NE - 1)
            more = pe.value_load(xn_i, min_val=0, max_val=XP)
            with pe.Fori(0, XP) as i:
                with pe.If(more > i):
                    gather(i + NE)
                    first(i + NE)
                    turn_act(i + NE)
                    second(i + NE)
                    scatter(i + NE)

        @block.vector
        def _(v):
            n = [0]

            def link(i):
                n[0] += 1
                i.then_inc(sem("dve_chain"), 1)
                v.wait_ge(sem("dve_chain"), n[0])

            def done(name):
                v.nop().then_inc(sem(name), 1)

            tt, ts, stt = v.tensor_tensor, v.tensor_scalar, v.scalar_tensor_tensor

            v.wait_ge(sem("sig_c"), 1)
            v.wait_ge(sem("c_in"), 16)
            tt(cs32[:, :, :], ccol[:, 0:KD].unsqueeze(2).to_broadcast((P, KD, 32)), ccol[:, KD:2 * KD].unsqueeze(2).to_broadcast((P, KD, 32)),
               ALU.mult).then_inc(sem("cs32"), 1)
            v.wait_ge(sem("x_sq"), 1)
            link(ts(stat[:, 2:4], stat[:, 0:2], 1.0 / D, EPS, ALU.mult, ALU.add))
            link(v.reciprocal(stat[:, 2:4], stat[:, 2:4]))
            done("square")
            v.wait_ge(sem("rsqrt"), 1)
            for t in range(TT):
                link(ts(xn[:, t, :], xs[:, t, :], stat[:, 2 + t:3 + t], None, ALU.mult))
            done("xn")
            v.wait_ge(sem("params_turned"), 2)
            link(v.tensor_copy(pcol[:, :], ps[:, 6, 0:P]))
            link(v.tensor_copy(peT[:, :], ps[:, 6, P:P + 64]))
            done("params_read")
            v.wait_ge(sem("ada_used"), 4)
            v.tensor_copy(modrow, ps[:, 7, :]).then_inc(sem("modrow"), 1)
            v.wait_ge(sem("mod_turned"), 1)
            mc = ps[:, 6, :].rearrange("p (s g r) -> p g s r", s=4, g=4)[:, :, :, 0]
            m3v = m3[:, :].rearrange("p (g s) -> p g s", g=4)
            link(tt(m3v, mc, pcol[:, R_ADAB:R_ADAB + 16].rearrange("p (g s) -> p g s", g=4), ALU.add))
            done("mod_read")
            link(v.tensor_copy(S1[:, :], m3[:, 0:8]))
            link(stt(G1[:, :], m3[:, 8:16], 1.0, pcol[:, R_N1:R_N1 + 8], ALU.add, ALU.mult))
            v.wait_ge(sem("x_turned"), 1)
            for k in range(KD):
                link(ts(hT[:, k, :], ps[:, k // 2, (k % 2) * T:(k % 2 + 1) * T], G1[:, k:k + 1], S1[:, k:k + 1], ALU.mult, ALU.add))
            done("hT")
            link(v.memset(lx[:, :, 0:3], 0.0))
            done("lx_zero")
            lam = pcol[:, R_LAM:R_LAM + 8]
            z, s_, s2, acc = (spl[:, j, :] for j in range(4))
            link(stt(z, lam, -1.0, lam, ALU.mult, ALU.min))
            done("lam_abs")
            v.wait_ge(sem("lam_exp"), 1)
            link(ts(s_, z, 2.0, None, ALU.add))
            link(v.reciprocal(s_, s_))
            link(tt(s_, s_, z, ALU.mult))
            link(tt(s2, s_, s_, ALU.mult))
            link(ts(acc, s2, 1.0 / 15, 1.0 / 13, ALU.mult, ALU.add))
            for d in (11, 9, 7, 5, 3, 1):
                link(tt(acc, acc, s2, ALU.mult))
                link(ts(acc, acc, 1.0 / d, None, ALU.add))
            link(tt(acc, acc, s_, ALU.mult))
            link(ts(z, lam, -1.0, 0.0, ALU.mult, ALU.max))
            link(stt(acc, acc, 2.0, z, ALU.mult, ALU.add))
            link(ts(acc, acc, -LRU_C, None, ALU.mult))
            spf = acc

            for h in range(2):
                v.wait_ge(sem("job_read"), h + 1)
                for w in range(4):
                    for k in range(4 * h, 4 * h + 4):
                        cw = pcol[:, R_CONVW + 8 * w + k:R_CONVW + 8 * w + k + 1]
                        if w == 0:
                            i = ts(xc[:, k, :], lx[:, k, 0:T], cw, pcol[:, R_CONVB + k:R_CONVB + k + 1], ALU.mult, ALU.add)
                        else:
                            i = stt(xc[:, k, :], lx[:, k, w:w + T], cw, xc[:, k, :], ALU.mult, ALU.add)
                        if k % 4 == 3:
                            link(i)
            done("conv")
            v.wait_ge(sem("small_in"), 16 * 12)
            link(v.tensor_copy(pos_f[:, :], pos_i[:, :]))
            for t in range(TT):
                link(ts(ang[:, t, :], ang[:, t, :], pos_f[:, t:t + 1], None, ALU.mult))
            C1 = 6.28125
            C2 = float(np.float32(np.floor((2 * np.pi - C1) * 2 ** 22) / 2 ** 22))
            C3 = float(2 * np.pi - C1 - C2)
            BIG = 1.5 * 2 ** 23
            link(ts(cosT, ang, 1.0 / (2 * np.pi), BIG, ALU.mult, ALU.add))
            link(ts(cosT, cosT, -BIG, None, ALU.add))
            for cst in (C1, C2, C3):
                link(stt(ang, cosT, -cst, ang, ALU.mult, ALU.add))
            link(ts(sinT, ang, 3.1415925, -3.1415925, ALU.min, ALU.max))
            link(stt(cosT, sinT, -1.0, sinT, ALU.mult, ALU.min))
            link(ts(cosT, cosT, float(np.pi / 2), None, ALU.add))
            done("angles")
            v.wait_ge(sem("job_read"), JOB[("r", 1)] + 1)
            link(tt(rr, rr, spf.unsqueeze(2).to_broadcast((P, KD, T)), ALU.mult))
            done("log_a")
            v.wait_ge(sem("job_read"), JOB[("i", 1)] + 1)
            link(tt(ii, ii, xc, ALU.mult))
            v.wait_ge(sem("lru_exp"), 2)
            link(stt(le, le, 1.0, lt, ALU.add, ALU.mult))
            link(ts(rr, le, 1.0, None, ALU.add))
            link(stt(le, le, 2.0, le, ALU.add, ALU.mult))
            link(ts(lt, le, -1.0, 0.0, ALU.mult, ALU.max))
            done("one_minus_a2")
            v.wait_ge(sem("lru_sqrt"), 1)
            link(tt(ii, ii, lt, ALU.mult))
            for k in range(KD):
                i = v.tensor_tensor_scan(xc[:, k, :], rr[:, k, :], ii[:, k, :], 0.0, ALU.mult, ALU.add)
            link(i)
            link(tt(olT, olT, xc, ALU.mult))
            done("lru_done")
            v.wait_ge(sem("pool_masks"), 1)
            link(v.memset(LV, 0.0))
            v.wait_ge(sem("job_read"), JOB[("kcmp",)] + 1)
            for kv, L in enumerate((LK, LV)):
                for g in range(NG):
                    src = kcT[:, 2 * kv + g, :].rearrange("p (b l) -> p l b", l=16)
                    for h in range(2):
                        e = peT[:, 32 * kv + 16 * h:32 * kv + 16 * h + 16].unsqueeze(2).to_broadcast((P, 16, N_CMP))
                        i = tt(L[:, 16 * h:16 * h + 16, 32 * g:32 * g + N_CMP], src[:, :, h:h + N_CMP], e, ALU.add)
            link(i)
            done("cmp_rows")
            def qk_norm(h0, nh, col, n):
                st = stat[:, 64:64 + TT * nh]
                for t in range(TT):
                    q = QK[:, t, h0:h0 + nh, :]
                    sq = QR[:, t, h0:h0 + nh, :]
                    link(tt(sq, q, q, ALU.mult))
                    link(v.tensor_reduce(stat[:, 64 + nh * t:64 + nh * (t + 1)], sq, AX.X, ALU.add))
                link(ts(st, st, 1.0 / DH, EPS, ALU.mult, ALU.add))
                link(v.reciprocal(st, st))
                done("square")
                v.wait_ge(sem("rsqrt"), n)
                for t in range(TT):
                    q = QK[:, t, h0:h0 + nh, :]
                    link(tt(q, q, stat[:, 64 + nh * t:64 + nh * (t + 1)].unsqueeze(2).to_broadcast((P, nh, DH)), ALU.mult))
                    link(tt(q, q, gain[:, col:col + 1, :].to_broadcast((P, nh, DH)), ALU.mult))

            def rope(h0, nh):
                for t in range(TT):
                    x1, x2 = QK[:, t, h0:h0 + nh, 0:64], QK[:, t, h0:h0 + nh, 64:128]
                    r1, r2 = QR[:, t, h0:h0 + nh, 0:64], QR[:, t, h0:h0 + nh, 64:128]
                    tm = rtmp[:, t, 0:nh, :]
                    cb = cosT[:, t:t + 1, :].to_broadcast((P, nh, 64))
                    sb_ = sinT[:, t:t + 1, :].to_broadcast((P, nh, 64))
                    link(tt(tm, x2, sb_, ALU.mult))
                    link(tt(r1, x1, cb, ALU.mult))
                    link(tt(r1, r1, tm, ALU.subtract))
                    link(tt(tm, x1, sb_, ALU.mult))
                    link(tt(r2, x2, cb, ALU.mult))
                    link(tt(r2, r2, tm, ALU.add))

            v.wait_ge(sem("sincos"), 2)
            v.wait_ge(sem("job_read"), JOB[("kwin",)] + 1)
            qk_norm(8, 2, 2, 2)
            qk_norm(10, 2, 3, 3)
            rope(8, 4)
            v.wait_ge(sem("job_read"), JOB[("q", 0)] + 1)
            qk_norm(0, 4, 0, 4)
            rope(0, 4)
            v.wait_ge(sem("cmp2_full"), 1)
            kp = ps[0:64, 6, 256:384]
            link(v.tensor_copy(vcs, ps[0:64, 6, 384:512]))
            link(v.tensor_copy(kcn, kp))
            link(tt(ksq, kcn, kcn, ALU.mult))
            link(v.tensor_reduce(stat[0:64, 80:81], ksq, AX.X, ALU.add))
            link(ts(stat[0:64, 80:81], stat[0:64, 80:81], 1.0 / DH, EPS, ALU.mult, ALU.add))
            link(v.reciprocal(stat[0:64, 80:81], stat[0:64, 80:81]))
            done("square")
            v.wait_ge(sem("rsqrt"), 5)
            link(ts(kcn, kcn, stat[0:64, 80:81], None, ALU.mult))
            link(tt(kcn, kcn, gain[0:64, 1, :], ALU.mult))
            done("kcn")
            v.wait_ge(sem("job_read"), JOB[("q", 1)] + 1)
            qk_norm(4, 4, 0, 6)
            rope(4, 4)
            done("roped")
            v.wait_ge(sem("kc_turned"), 1)
            link(v.tensor_copy(kccT, ps[:, 6, 0:64]))
            done("kccT")
            def softmax_in(m):
                g, t, b = UNITS[m]
                v.wait_ge(sem("scores"), m + 1)
                if m >= 2:
                    v.wait_ge(sem("att_turned"), m - 1)
                S = Sb[:, m % 2, :].rearrange("p (h k) -> p h k", h=HPG)
                if b == 0:
                    p = PAIR[m % 2][:, 0:64].rearrange("p (h k) -> p h k", h=HPG)
                    nk = N_CMP
                    link(tt(S[:, :, 0:nk], p[:, :, 0:nk], cneg[:, t:t + 1, 0:nk].to_broadcast((P, HPG, nk)), ALU.add))
                    if m >= 3:
                        v.wait_ge(sem("att_turned"), m - 2)
                    link(v.memset(Pc, 0.0))
                else:
                    nk = P * (t + 1)
                    p = PAIR[m % 2][:, 0:HPG * nk].rearrange("p (h k) -> p h k", h=HPG)
                    if t == 1:
                        link(v.tensor_copy(S[:, :, 0:P], p[:, :, 0:P]))
                    link(tt(S[:, :, nk - P:nk], p[:, :, nk - P:nk], causal[:, :].unsqueeze(1).to_broadcast((P, HPG, P)), ALU.add))
                mx = stat[:, 16 + 8 * (m % 2):20 + 8 * (m % 2)]
                link(v.tensor_reduce(mx, S[:, :, 0:nk], AX.X, ALU.max))
                link(ts(mx, mx, NEG * 1e-10, -SCALE, ALU.max, ALU.mult))
                done("att_max")

            def softmax_out(m):
                g, t, b = UNITS[m]
                v.wait_ge(sem("att_exp"), m + 1)
                sm = stat[:, 32 + 8 * (m % 2):36 + 8 * (m % 2)]
                if b == 0:
                    link(ts(sm, sm, 1e-30, None, ALU.max))
                link(v.reciprocal(sm, sm))
                gb = ng[:, t, :].rearrange("p (h b) -> p h b", b=3)[:, HPG * g:HPG * g + HPG, b]
                link(tt(sm, sm, gb, ALU.mult))
                sbc = sm.unsqueeze(2)
                if b == 0:
                    q = Pc[:, :, 32 * g:32 * g + N_CMP]
                    link(tt(q, q, sbc.to_broadcast((P, HPG, N_CMP)), ALU.mult))
                else:
                    nk = P * (t + 1)
                    q = Sb[:, m % 2, :].rearrange("p (h k) -> p h k", h=HPG)[:, :, 0:nk]
                    link(tt(q, q, sbc.to_broadcast((P, HPG, nk)), ALU.mult))
                done("att_p")

            v.wait_ge(sem("qk_turned"), 10)
            v.wait_ge(sem("ada_used"), 12)
            link(v.tensor_copy(mod2[:, 0, :], ps[:, 7, :]))
            link(v.tensor_copy(mod2[:, 1, :], ps[:, 5, :]))
            softmax_in(0)
            for m in range(len(UNITS)):
                if m + 1 < len(UNITS):
                    softmax_in(m + 1)
                softmax_out(m)

            link(v.memset(pickt, 0.0))
            for g in range(4):
                link(v.memset(pickt[32 * g:32 * g + 1, g, :], 1.0))
            done("pick")
            for third in (1, 2):
                v.wait_ge(sem("mod2_turned"), third)
                mc = ps[:, 4, :].rearrange("p (s g r) -> p g s r", s=4, g=4)[:, :, :, 0]
                link(tt(m3v, mc, pcol[:, R_ADAB + 16 * third:R_ADAB + 16 * third + 16].rearrange("p (g s) -> p g s", g=4), ALU.add))
                done("mod_read")
                if third == 1:
                    link(v.tensor_copy(S2[:, :], m3[:, 8:16]))
                else:
                    link(stt(G2[:, :], m3[:, 0:8], 1.0, pcol[:, R_N2:R_N2 + 8], ALU.add, ALU.mult))
                gt = gate1 if third == 1 else gate2
                for j in range(2):
                    v.wait_ge(sem("gate_rows"), 2 * (third - 1) + j + 1)
                    link(tt(gt[:, j * 512:(j + 1) * 512], gt[:, j * 512:(j + 1) * 512], ps[:, 6, :], ALU.add))
                    done("gate_read")

            for half in range(2):
                for br in range(2):
                    v.wait_ge(sem("branch"), 2 * half + br + 1)
                    y = PAIR[br].rearrange("p (k t) -> p k t", k=4)
                    mgv = mg[:, KD * br + 4 * half:KD * br + 4 * half + 4, :]
                    if br == 0:
                        link(tt(mergedT[:, 4 * half:4 * half + 4, :], y, mgv, ALU.mult))
                    else:
                        link(tt(mgv, y, mgv, ALU.mult))
                    done("y_taken")
                link(tt(mergedT[:, 4 * half:4 * half + 4, :], mergedT[:, 4 * half:4 * half + 4, :], mg[:, KD + 4 * half:KD + 4 * half + 4, :], ALU.add))
                done("merged")
            for half in range(2):
                v.wait_ge(sem("wo_full"), half + 1)
                p = PAIR[half].rearrange("p (t n) -> p t n", t=TT)
                tmp = A1[:, half * 1024:(half + 1) * 1024].rearrange("p (t n) -> p t n", t=TT)
                link(tt(tmp, p, gate1[:, half * 512:(half + 1) * 512].unsqueeze(1).to_broadcast((P, TT, 512)), ALU.mult))
                xv = xs[:, :, half * 512:(half + 1) * 512]
                link(tt(xv, xv, tmp, ALU.add))
            for t in range(TT):
                link(stt(A1[:, 0:1024], xs[:, t, :], 1.0, xs[:, t, :], ALU.mult, ALU.mult, accum_out=stat[:, 48 + t:49 + t]))
            link(ts(stat[:, 50:52], stat[:, 48:50], 1.0 / D, EPS, ALU.mult, ALU.add))
            link(v.reciprocal(stat[:, 50:52], stat[:, 50:52]))
            done("square")
            v.wait_ge(sem("rsqrt"), 7)
            for t in range(TT):
                link(ts(xn2[:, t, :], xs[:, t, :], stat[:, 50 + t:51 + t], None, ALU.mult))
            done("xn2")
            v.wait_ge(sem("x2_turned"), 1)
            for k in range(KD):
                link(ts(hT[:, k, :], ps[:, k // 2, (k % 2) * T:(k % 2 + 1) * T], G2[:, k:k + 1], S2[:, k:k + 1], ALU.mult, ALU.add))
            done("h2T")
            done("x2_read")
            v.wait_ge(sem("logits"), 1)
            v.wait_ge(sem("pool_masks"), 2)
            for t in range(TT):
                link(tt(lg[:, t, :], ps[:, 4, t * NE:(t + 1) * NE], rb[:, :], ALU.add))
                link(v.max(top[:, t, :], lg[:, t, :]))
                link(v.max_index(topi[:, t, :].bitcast(U32), top[:, t, :], lg[:, t, :]))
                link(ts(stat[:, 60 + t:61 + t], top[:, t, 0:1], -1.0, None, ALU.mult))
                done("top4")
            for t in range(TT):
                link(v.tensor_copy(topi[:, t, :], topi[:, t, :].bitcast(U32)))
                v.wait_ge(sem("top_exp"), t + 1)
                link(v.reciprocal(stat[:, 62 + t:63 + t], stat[:, 62 + t:63 + t]))
                link(ts(topw[:, t, 0:TOPK], topw[:, t, 0:TOPK], stat[:, 62 + t:63 + t], None, ALU.mult))
                for j in range(TOPK):
                    if j == 0:
                        link(ts(msk[:, t, :], iotaE, topi[:, t, 0:1], None, ALU.is_equal))
                        link(ts(wts[:, t, :], iotaE, topi[:, t, 0:1], topw[:, t, 0:1], ALU.is_equal, ALU.mult))
                    else:
                        link(ts(tmpe[:, t, :], iotaE, topi[:, t, j:j + 1], None, ALU.is_equal))
                        link(tt(msk[:, t, :], msk[:, t, :], tmpe[:, t, :], ALU.add))
                        link(stt(wts[:, t, :], tmpe[:, t, :], topw[:, t, j:j + 1], wts[:, t, :], ALU.mult, ALU.add))
            done("mask")
            v.wait_ge(sem("places"), 1)
            pp = ps[:, 5, 0:2 * NE].rearrange("p (t e) -> p t e", t=TT)
            link(ts(tmpe, msk, -4096.0, 4096.0, ALU.mult, ALU.add))
            link(tt(pos, pp, tmpe, ALU.add))
            link(v.tensor_copy(cnt, ps[:, 5, 2 * NE:3 * NE]))
            done("pos")
            link(ts(xneed, cnt, float(CAP), None, ALU.is_gt))
            for m in range(2, MORE + 1):
                link(stt(xneed, cnt, float(CAP * m), xneed, ALU.is_gt, ALU.add))
            link(v.memset(ohx, 1.0))
            link(v.tensor_tensor_scan(xend, ohx, xneed, 0.0, ALU.mult, ALU.add))
            link(ts(ohy, xend, rcol[:, 0:1], None, ALU.is_le))
            link(v.tensor_reduce(xcol[:, 0:1], ohy, AX.X, ALU.add))
            link(ts(ohx, iotaE, xcol[:, 0:1], None, ALU.is_equal))
            link(tt(ohy, xneed, ohy, ALU.mult))
            link(v.tensor_reduce(xcol[:, 1:2], ohy, AX.X, ALU.add))
            link(tt(xcol[:, 1:2], rcol[:, 0:1], xcol[:, 1:2], ALU.subtract))
            link(ts(xcol[:, 1:2], xcol[:, 1:2], 1.0, float(CAP), ALU.add, ALU.mult))
            link(ts(xcol[:, 0:1], xcol[:, 0:1], float(NE - 1), None, ALU.min))
            link(v.memset(xcol[:, 2:8], 0.0))
            done("ohx")
            v.wait_ge(sem("routes_turned"), 1)
            link(v.tensor_copy(wT, ps[0:NE, 6, 0:T]))
            link(v.tensor_copy(posT, ps[0:NE, 7, 0:T]))
            done("wT")
            v.wait_ge(sem("xcols"), 1)
            link(v.tensor_copy(ohT[:, 0:XP], ps[0:NE, 4, 0:XP]))
            link(v.tensor_copy(xe_i[:, 0:XP], ps[0:1, 4, P:P + XP]))
            link(v.tensor_copy(chk[0:8, 0:XP], ps[0:8, 4, P:P + XP]))
            link(ts(rcol[:, 1:2], rcol[:, 0:1], 1.0, None, ALU.is_equal))
            link(ts(pick1, ones[0:8, :], rcol[0:8, 1:2], None, ALU.mult))
            link(v.tensor_copy(xn_i, xend[0:1, NE - 1:NE]))
            done("xtab")
            for j in range(3):
                link(v.tensor_copy(oh96[32 * j:32 * j + 32, 0:NE], ident[32 * j:32 * j + 32, 32 * j:32 * j + 32]))
                link(v.tensor_copy(oh96[32 * j:32 * j + 32, NE:NE + XP], ps[0:NE, 4, 0:XP]))
            done("ohT")
            v.wait_ge(sem("xmats"), 1)
            for t in range(TT):
                link(v.tensor_copy(posP[:, t, 0:NE], pos[:, t, :]))
                link(v.tensor_copy(wP[:, t, 0:NE], wts[:, t, :]))
                link(v.tensor_copy(posP[:, t, NE:NE + XP], ps[:, 4, 256 + t * 32:256 + t * 32 + XP]))
                link(tt(posP[:, t, NE:NE + XP], posP[:, t, NE:NE + XP], ps[:, 4, 384:384 + XP], ALU.subtract))
                link(v.tensor_copy(wP[:, t, NE:NE + XP], ps[:, 4, 320 + t * 32:320 + t * 32 + XP]))

            def select(q):
                for t in range(TT):
                    i = ts(sel[:, t, :], iota[:, 0:CAP], posP[:, t, bass.ds(q, 1)], None, ALU.is_equal)
                i.then_inc(sem("sel"), 1)

            def select_w(q):
                for t in range(TT):
                    i = ts(selw[:, t, :], iota, posP[:, t, bass.ds(q, 1)], wP[:, t, bass.ds(q, 1)], ALU.is_equal, ALU.mult)
                i.then_inc(sem("selw"), 1)

            def expert_rows(q):
                v.wait_ge(sem("rows"), q + 1)
                g = Gps.rearrange("p (k c) -> p k c", k=KD)
                v.tensor_tensor(xT, g, G2[:, :].unsqueeze(2).to_broadcast((P, KD, CAP)), ALU.mult).then_inc(sem("xT_half"), 1)
                v.tensor_copy(ohp, oh96[:, bass.ds(q, 1)].to_broadcast((96, CAP))).then_inc(sem("ohp"), 1)
                v.wait_ge(sem("xT_half"), q + 1)
                v.tensor_tensor(xT, xT, S2[:, :].unsqueeze(2).to_broadcast((P, KD, CAP)), ALU.add).then_inc(sem("xT"), 1)

            def swiglu(q):
                v.wait_ge(sem("w1_used"), (q + 1) * KD)
                hv = Hps.rearrange("p (f two) -> p two f", two=2)
                ts(glu, hv[:, 0, :], LIMIT, None, ALU.min).then_inc(sem("glu"), 1)
                ts(lin, hv[:, 1, :], LIMIT, -LIMIT, ALU.min, ALU.max).then_inc(sem("lin"), 1)
                v.wait_ge(sem("lin"), q + 1)
                stt(lin, lin, 1.0, glu, ALU.add, ALU.mult).then_inc(sem("lin2"), 1)
                v.wait_ge(sem("lin2"), q + 1)
                v.wait_ge(sem("sig"), q + 1)
                tt(act, lin, sig, ALU.mult).then_inc(sem("act"), 1)

            done("tables")
            select(0)
            expert_rows(0)
            select(1)
            v.wait_ge(sem("w1_used"), KD)
            select_w(0)
            swiglu(0)
            expert_rows(1)
            with v.Fori(1, NE - 1) as q:
                v.wait_ge(sem("rows"), q + 1)
                select(q + 1)
                v.wait_ge(sem("act_turned"), q)
                select_w(q)
                swiglu(q)
                expert_rows(q + 1)
            v.wait_ge(sem("act_turned"), NE - 1)
            select_w(NE - 1)
            swiglu(NE - 1)
            more = v.value_load(xn_i, min_val=0, max_val=XP)
            with v.Fori(0, XP) as i:
                with v.If(more > i):
                    v.wait_ge(sem("act_turned"), i + NE)
                    select(i + NE)
                    expert_rows(i + NE)
                    select_w(i + NE)
                    swiglu(i + NE)
            v.wait_ge(sem("scattered"), more + NE)
            for t in range(TT):
                for h in range(2):
                    tmp = A1[:, t * 1024 + h * 512:t * 1024 + (h + 1) * 512]
                    link(tt(tmp, ps[:, 2 * t + h, :], gate2[:, h * 512:(h + 1) * 512], ALU.mult))
                    link(tt(xs[:, t, h * 512:(h + 1) * 512], xs[:, t, h * 512:(h + 1) * 512], tmp, ALU.add))
                done("out_ready")


_INS = ["x", "c", "positions", "ada_w", "ada_b", "norm1_g", "w_in", "q_norm_g", "k_norm_g",
        "cmp_pe_k", "cmp_pe_v", "cmp_wk1", "cmp_wk2", "cmp_wv1", "cmp_wv2",
        "conv_w", "conv_b", "lru_wa", "lru_ba", "lru_wx", "lru_bx", "lru_lambda",
        "w_branch_out", "w_out", "norm2_g", "router_w", "router_b", "moe_w1", "moe_b1", "moe_w2", "moe_b2"]


def kernel(**inputs):
    import concourse.bacc as bacc
    from concourse.bass_utils import run_bass_kernel_spmd

    nc = bacc.Bacc("TRN2", target_bir_lowering=False, num_devices=1)
    inv = (10000.0 ** (-np.arange(0, DH, 2, dtype=np.float64) / DH)).astype(np.float32)[None, :]
    arrays, args = {}, {}
    for name in _INS + ["inv_freq"]:
        arr = np.ascontiguousarray(inputs[name]) if name in inputs else inv
        arrays[f"in_{name}"] = arr
        args[name] = nc.dram_tensor(f"in_{name}", arr.shape, mybir.dt.from_np(arr.dtype), kind="ExternalInput").ap()
    args["out"] = nc.dram_tensor("out_x", (1, T, D), F32, kind="ExternalOutput").ap()
    build_program(nc, **args)
    r = run_bass_kernel_spmd(nc, [arrays], core_ids=[0])
    return r.results[0]["out_x"]
```

```python
from contextlib import ExitStack

import numpy as np

import concourse.bass as bass
from concourse import mybir

ALU = mybir.AluOpType
ACT = mybir.ActivationFunctionType
AX = mybir.AxisListType
F32 = mybir.dt.float32
BF16 = mybir.dt.bfloat16
I32 = mybir.dt.int32
U32 = mybir.dt.uint32

P = 128
D = 1024
T = 256
TT = T // P
KD = D // P
NH, DH, NG, HPG = 8, 128, 2, 4
CMP_BLOCK, CMP_STRIDE = 32, 16
N_CMP = (T - CMP_BLOCK) // CMP_STRIDE + 1
CMP_HIDDEN = 256
LRU_C = 8.0
NE = 32
TOPK = 4
FF = 1024
CAP = 64
MORE = T // CAP - 1
XP = (T * TOPK - 1) // CAP
NPASS = NE + XP
LIMIT, ALPHA = 7.0, 1.702
EPS = 1e-6
NEG = -1e30
SCALE = float(DH) ** -0.5

Q_OFF = 0
KCMP_OFF = NH * DH
KSLC_OFF = KCMP_OFF + 2 * NG * DH
KWIN_OFF = KSLC_OFF + 2 * NG * DH
NSAG_OFF = KWIN_OFF + 2 * NG * DH
N_NSAG = NH * 3
LRUX_OFF = NSAG_OFF + N_NSAG
LRUG_OFF = LRUX_OFF + D
MERGE_OFF = LRUG_OFF + D

R_N1, R_CONVW, R_CONVB, R_BA, R_BX, R_LAM, R_N2, R_ADAB = 0, 8, 40, 48, 56, 64, 72, 80
M_SHIFT1, M_SCALE1, M_GATE1, M_SHIFT2, M_SCALE2, M_GATE2 = 0, 8, 16, 24, 32, 40

UNITS = [(g, t, b) for g in range(NG) for t in range(TT) for b in range(3)]

JOBS_A = [(("kslc",), 2), (("kwin",), 2), (("q", 0), 2), (("q", 1), 2), (("kcmp",), 4), (("lrux", 0), 4)]
JOBS_B = [(("r", 0), 1), (("i", 0), 1), (("lrug", 0), 4), (("lrug", 1), 4), (("lrux", 1), 4), (("merge", 0), 4),
          (("r", 1), 1), (("i", 1), 1), (("merge", 1), 4), (("merge", 2), 4), (("merge", 3), 4), (("ylru", 0), 4), (("ylru", 1), 4)]
JOBS = [j for j, _ in JOBS_A + JOBS_B]
JOB = {j: n for n, j in enumerate(JOBS)}
EARLY, PER = 4, 3
PIECES = [(j, p, p == n - 1) for j, n in JOBS_B for p in range(n)]
assert len(PIECES) == EARLY + PER * len(UNITS)
LRU_AT = {0: (0, 1), 1: (0, 2), 2: (0, 3), 4: (1, 0), 6: (1, 1), 7: (1, 2), 8: (1, 3)}
ADA_AT = {0: (1, 0), 1: (1, 1), 2: (1, 2), 3: (1, 3), 5: (2, 0), 6: (2, 1), 7: (2, 2), 8: (2, 3)}


def pieces_of(m):
    return PIECES[:EARLY] if m < 0 else PIECES[EARLY + PER * m:EARLY + PER * (m + 1)]


def weights_of(job):
    return {"r": ("lrugate",), "i": ("lrugate",), "ylru": ("bo", 1)}.get(job[0], job[:1]) + job[1:]


STREAM = [("ada", 0, k) for k in range(4)] + [("kslc",), ("kwin",), ("q", 0), ("q", 1), ("kcmp",), ("lrux", 0)] + [("cmp", k) for k in range(4)]
for _m in range(-1, len(UNITS)):
    for _j, _p, _ in pieces_of(_m):
        if _p == 0 and _j[0] != "i":
            STREAM.append(weights_of(_j))
    if _m in ADA_AT:
        STREAM.append(("ada",) + ADA_AT[_m])
STREAM += [("bo", 0, 0), ("bo", 0, 1), ("wo", 0), ("wo", 1)]
SLOT = {u: n for n, u in enumerate(STREAM)}
NSLOT = 4


def read_by(u):
    if u[0] == "lrugate":
        return "job_full", JOB[("i", u[1])] + 1
    if u[:2] == ("bo", 1):
        return "job_full", JOB[("ylru", u[2])] + 1
    if u in JOB:
        return "job_full", JOB[u] + 1
    if u[0] == "ada":
        return "ada_used", 4 * u[1] + u[2] + 1
    if u[0] == "cmp":
        return "cmp_used", u[1] + 1
    return "branch", u[2] + 1


def build_program(nc, x, c, positions, ada_w, ada_b, norm1_g, w_in, q_norm_g, k_norm_g,
                  cmp_pe_k, cmp_pe_v, cmp_wk1, cmp_wk2, cmp_wv1, cmp_wv2,
                  conv_w, conv_b, lru_wa, lru_ba, lru_wx, lru_bx, lru_lambda,
                  w_branch_out, w_out, norm2_g, router_w, router_b,
                  moe_w1, moe_b1, moe_w2, moe_b2, inv_freq, out):
    with ExitStack() as ctx:
        made = {}

        def sem(name):
            if name not in made:
                made[name] = ctx.enter_context(nc.semaphore(name))
            return made[name]

        def sb(name, shape, dt=F32):
            return ctx.enter_context(nc.sbuf_tensor(name, shape, dt))

        W1 = sb("W1", [P, KD * 2 * FF])
        W2 = sb("W2", [P, KD * D])
        ST = sb("ST", [P, NSLOT * 4096])
        xs = sb("xs", [P, TT, D])
        A1 = sb("A1", [P, KD * T])
        A2 = sb("A2", [P, KD * T])
        gate1 = sb("gate1", [P, D])
        gate2 = sb("gate2", [P, D])
        vtm = sb("vtm", [P, 2, TT, NG * DH])
        b1s = sb("b1s", [96, 2 * FF], BF16)
        ident = sb("ident", [P, P])
        pcol = sb("pcol", [P, P])
        peT = sb("peT", [P, 2 * CMP_BLOCK])
        causal = sb("causal", [P, P])
        cneg = sb("cneg", [P, TT, 16])
        gw = sb("gw", [P, KD, N_NSAG])
        rw = sb("rw", [P, KD, NE])
        rb = sb("rb", [P, NE])
        ng = sb("ng", [P, TT, N_NSAG])
        cs32 = sb("cs32", [P, KD, 32])
        ccol = sb("ccol", [P, 2 * KD])
        G1 = sb("G1", [P, KD])
        S1 = sb("S1", [P, KD])
        G2 = sb("G2", [P, KD])
        S2 = sb("S2", [P, KD])
        m3 = sb("m3", [P, 16])
        spl = sb("spl", [P, 4, KD])
        stat = sb("stat", [P, 96])
        pos_i = sb("pos_i", [P, TT], I32)
        pos_f = sb("pos_f", [P, TT])

        def cut(t, a, *shape):
            n = int(np.prod(shape))
            v = t[:, a:a + n]
            if len(shape) == 2:
                v = v.rearrange("p (a b) -> p a b", a=shape[0])
            if len(shape) == 3:
                v = v.rearrange("p (a b c) -> p a b c", a=shape[0], b=shape[1])
            return v

        hT = cut(A1, 0, KD, T)
        QK = cut(W1, 0, TT, 12, DH)
        QR = cut(W1, 3072, TT, 12, DH)
        xn = cut(W1, 3072, TT, D)
        praw = W1[:, 5120:5248]
        peraw = W1[0:2 * CMP_BLOCK, 5248:5376]
        modrow = W1[:, 5376:5888]
        Sb = cut(W1, 0, 2, HPG * T)
        PT = cut(W1, 2048, 2, HPG * P)
        Pc = cut(W1, 3072, HPG, 64)
        pickt = cut(W1, 3328, 4, P)
        mod2 = cut(W1, 3840, 2, 512)
        qT = cut(W1, 6144, NH, T)
        rtmp = cut(W1, 6144, TT, 12, DH // 2)
        qrT = cut(W1, 8192, NH, T)
        LV = cut(W1, 8192, CMP_BLOCK, 64)
        LK = cut(A2, 0, CMP_BLOCK, 64)
        kT = cut(W1, 10240, 4, T)
        kcT = cut(W1, 10240, 4, T)
        uu = W1[:, 11264:11520]
        uT = cut(W1, 11520, 2, P)
        kcn = W1[0:64, 11776:11904]
        vcs = W1[0:64, 11904:12032]
        kccT = W1[:, 12032:12096]
        ksq = W1[0:64, 12096:12224]
        w2c = cut(W1, 12224, 4, DH)
        gain = cut(W1, 12736, 4, DH)
        cosT = cut(W1, 13248, TT, DH // 2)
        sinT = cut(W1, 13376, TT, DH // 2)
        ang = cut(W1, 13504, TT, DH // 2)
        KH = KD // 2
        lx = cut(W1, 13632, KH, T + 3)
        lt = cut(W1, 13632, KH, T)
        xc = cut(W1, 13632 + KH * (T + 3), KH, T)
        rr = cut(A2, 0, KH, T)
        ii = cut(A2, KH * T, KH, T)
        mg = cut(W2, 0, 2 * KD, T)
        oT = cut(W2, 4096, NH, T)
        olT = cut(W2, 6144, KD, T)
        mergedT = cut(A2, 0, KD, T)
        xn2 = cut(A2, 0, TT, D)

        def slot(u):
            n = (SLOT[u] - SLOT[("wo", 0)] + 2) % NSLOT
            return ST[:, n * 4096:(n + 1) * 4096]

        mb = [0]

        def mine(n):
            mb[0] += n
            return mb[0] - n

        o = mine(512); xT = cut(ST, o, KD, CAP)
        o = mine(512); actT = cut(ST, o, 4, P)
        o = mine(512); ysb = ST[:, o:o + 512]
        o = mine(TT * CAP); sel = cut(ST, o, TT, CAP)
        o = mine(TT * P); selw = cut(ST, o, TT, P)
        o = mine(TT * P); selT = cut(ST, o, TT, P)
        o = mine(32); ohp = ST[0:96, o:o + 32].bitcast(BF16)
        o = mine(128); iota = ST[:, o:o + 128]
        o = mine(TT * 48); posP = cut(ST, o, TT, 48)
        o = mine(TT * 48); wP = cut(ST, o, TT, 48)
        o = mine(48); oh96 = ST[0:96, o:o + 48]
        o = mine(TT * NE); lg = cut(ST, o, TT, NE)
        o = mine(TT * NE); msk = cut(ST, o, TT, NE)
        o = mine(TT * NE); wts = cut(ST, o, TT, NE)
        o = mine(TT * NE); pos = cut(ST, o, TT, NE)
        o = mine(TT * NE); tmpe = cut(ST, o, TT, NE)
        o = mine(TT * 8); top = cut(ST, o, TT, 8)
        o = mine(TT * 8); topi = cut(ST, o, TT, 8)
        o = mine(TT * 8); topw = cut(ST, o, TT, 8)
        o = mine(8); rs = ST[:, o:o + 8]
        o = mine(NE); iotaE = ST[:, o:o + NE]
        o = mine(P); upper = ST[:, o:o + P]
        o = mine(P); ones = ST[:, o:o + P]
        o = mine(T); wT = ST[0:NE, o:o + T]
        o = mine(T); posT = ST[0:NE, o:o + T]
        o = mine(16); iota16 = ST[:, o:o + 16]
        o = mine(NE); cnt = ST[:, o:o + NE]
        o = mine(NE); xneed = ST[:, o:o + NE]
        o = mine(NE); xend = ST[:, o:o + NE]
        o = mine(NE); ohx = ST[:, o:o + NE]
        o = mine(NE); ohy = ST[:, o:o + NE]
        o = mine(8); xcol = ST[:, o:o + 8]
        o = mine(64); ohT = ST[0:NE, o:o + 64]
        o = mine(P); pick1 = ST[0:8, o:o + P]
        o = mine(16); xe_i = ST[0:1, o:o + 16].bitcast(I32)
        o = mine(2); xn_i = ST[0:1, o:o + 1].bitcast(I32)
        o = mine(D); b2s = ST[0:NE, o:o + D]
        o = mine(16); chk = ST[:, o:o + 16]
        o = mine(2); rcol = ST[:, o:o + 2]
        assert mb[0] <= 2 * 4096
        glu = A1[:, 0:512]
        lin = A1[:, 512:1024]
        sig = A1[:, 1024:1536]
        act = A1[:, 1536:2048]
        w1v = cut(W1, 0, KD, 2 * FF)
        w2v = cut(W2, 0, KD, D)

        ps = ctx.enter_context(nc.psum_tensor("ps", [P, 8, 512], F32))
        PAIR = [ps[:, 0:2, :].rearrange("p a b -> p (a b)"), ps[:, 2:4, :].rearrange("p a b -> p (a b)")]
        Hps = ps[:, 4:6, :].rearrange("p a b -> p (a b)")
        Yps = ps[:, 6, :]
        Gps = ps[:, 7, :]

        block = ctx.enter_context(nc.Block())

        def wk(w, k0, nk, c0, nc_):
            return w[k0 * P:(k0 + nk) * P, c0:c0 + nc_].rearrange("(k p) n -> p k n", p=P)

        @block.sync
        def _(sp):
            IN_COL = {"lrux": LRUX_OFF, "lrug": LRUG_OFF, "merge": MERGE_OFF, "q": Q_OFF}
            ONE_COL = {"kcmp": KCMP_OFF, "kslc": KSLC_OFF, "kwin": KWIN_OFF}
            for n, u in enumerate(STREAM):
                if n >= NSLOT:
                    name, value = read_by(STREAM[n - NSLOT])
                    sp.wait_ge(sem(name), value)
                full = sem(f"stream_full{n % NSLOT}")
                dst = slot(u)
                if u[0] == "ada":
                    sp.dma_start(dst.rearrange("p (k n) -> p k n", k=2), wk(ada_w[0], 2 * u[2], 2, 2048 * u[1], 2048)).then_inc(full, 16)
                elif u[0] in IN_COL:
                    sp.dma_start(dst.rearrange("p (k n) -> p k n", k=KD), wk(w_in[0], 0, KD, IN_COL[u[0]] + 512 * u[1], 512)).then_inc(full, 16)
                elif u[0] in ONE_COL:
                    sp.dma_start(dst.rearrange("p (k n) -> p k n", k=KD), wk(w_in[0], 0, KD, ONE_COL[u[0]], 512)).then_inc(full, 16)
                elif u[0] == "lrugate":
                    for half, w in enumerate((lru_wa, lru_wx)):
                        sp.dma_start(dst[:, 1024 * half:1024 * (half + 1)].rearrange("p (a j) -> p a j", a=4),
                                     w[0, 2 * u[1]:2 * u[1] + 2].rearrange("h (i p) j -> p (h i) j", p=P)).then_inc(full, 16)
                elif u[0] == "cmp":
                    for half, w in enumerate((cmp_wk1, cmp_wv1)):
                        sp.dma_start(dst[:, 2048 * half:2048 * (half + 1)].rearrange("p (k n) -> p k n", k=8),
                                     wk(w[0], 8 * u[1], 8, 0, CMP_HIDDEN)).then_inc(full, 16)
                elif u[0] == "bo":
                    sp.dma_start(dst.rearrange("p (k n) -> p k n", k=KD), wk(w_branch_out[0], KD * u[1], KD, 512 * u[2], 512)).then_inc(full, 16)
                elif u[0] == "wo":
                    sp.dma_start(dst.rearrange("p (k n) -> p k n", k=KD), wk(w_out[0], 0, KD, 512 * u[1], 512)).then_inc(full, 16)

            def load_w1(e, passes):
                for k in range(KD):
                    if passes is not None:
                        sp.wait_ge(sem("w1_used"), 8 * passes - (KD - 1 - k))
                    sp.dma_start(w1v[:, k, :], moe_w1[0, e, k * P:(k + 1) * P, :] if isinstance(e, int)
                                 else moe_w1[0, bass.ds(e, 1), k * P:(k + 1) * P, :].rearrange("a p n -> p (a n)")).then_inc(sem(f"w1_full{k}"), 16)

            def load_w2(e, passes):
                for s in range(4):
                    if passes is not None:
                        sp.wait_ge(sem("w2_used"), 4 * passes - (3 - s))
                    src = moe_w2[0, e] if isinstance(e, int) else moe_w2[0, bass.ds(e, 1)].rearrange("a f n -> (a f) n")
                    sp.dma_start(w2v[:, 2 * s:2 * s + 2, :], wk(src, 2 * s, 2, 0, D)).then_inc(sem(f"w2_full{s}"), 16)

            sp.wait_ge(sem("att_read"), len(UNITS))
            sp.wait_ge(sem("oT_full"), NG * TT)
            sp.wait_ge(sem("gate_read"), 4)
            load_w1(0, None)
            sp.wait_ge(sem("merged"), 2)
            load_w2(0, None)
            load_w1(1, 1)
            with sp.Fori(2, NE) as q:
                load_w1(q, q)
                load_w2(q - 1, q - 1)
            load_w2(NE - 1, NE - 1)
            sp.wait_ge(sem("xtab"), 1)
            more = sp.value_load(xn_i, min_val=0, max_val=XP)
            with sp.Fori(0, XP) as i:
                with sp.If(more > i):
                    e = sp.value_load(xe_i[0:1, bass.ds(i, 1)], min_val=0, max_val=NE - 1)
                    load_w1(e, i + NE)
                    load_w2(e, i + NE)
            sp.wait_ge(sem("out_ready"), 2)
            for t in range(TT):
                sp.dma_start(out[0, t * P:(t + 1) * P, :], xs[:, t, :]).then_inc(sem("out_stored"), 16)
            sp.wait_ge(sem("out_stored"), 16 * TT)

        @block.gpsimd
        def _(pool):
            chain = [0]

            def link(i):
                chain[0] += 1
                i.then_inc(sem("pool_chain"), 1)
                pool.wait_ge(sem("pool_chain"), chain[0])

            pool.dma_start(peraw[0:CMP_BLOCK, :], cmp_pe_k[0]).then_inc(sem("pe_in"), 16)
            pool.dma_start(peraw[CMP_BLOCK:2 * CMP_BLOCK, :], cmp_pe_v[0]).then_inc(sem("pe_in"), 16)
            for j in range(3):
                pool.dma_start(A2[32 * j:32 * j + 32, :], moe_b1[0]).then_inc(sem("b1_in"), 16)
            pool.dma_start(gw[:, :, :], wk(w_in[0], 0, KD, NSAG_OFF, N_NSAG)).then_inc(sem("small_in"), 16)
            pool.dma_start(rw[:, :, :], wk(router_w[0], 0, KD, 0, NE)).then_inc(sem("small_in"), 16)
            pool.dma_start(rb[:, :], router_b.to_broadcast((P, NE))).then_inc(sem("small_in"), 16)
            pool.dma_start(gate1[:, :], ada_b[:, M_GATE1 * P:(M_GATE1 + 8) * P].to_broadcast((P, D))).then_inc(sem("small_in"), 16)
            pool.dma_start(gate2[:, :], ada_b[:, M_GATE2 * P:(M_GATE2 + 8) * P].to_broadcast((P, D))).then_inc(sem("small_in"), 16)
            pool.dma_start(gain[:, 0, :], q_norm_g.to_broadcast((P, DH))).then_inc(sem("small_in"), 16)
            for j in range(3):
                pool.dma_start(gain[:, 1 + j, :], k_norm_g[0, j:j + 1, :].to_broadcast((P, DH))).then_inc(sem("small_in"), 16)
            pool.dma_start(ang[:, 0, :], inv_freq.to_broadcast((P, DH // 2))).then_inc(sem("small_in"), 16)
            pool.dma_start(ang[:, 1, :], inv_freq.to_broadcast((P, DH // 2))).then_inc(sem("small_in"), 16)
            pool.dma_start(pos_i[:, :], positions[0].rearrange("(t p) -> p t", p=P), allow_slow_non_contiguous=True).then_inc(sem("small_in"), 16)
            for w, m in enumerate((cmp_wk2, cmp_wv2)):
                pool.dma_start(w2c[:, 2 * w:2 * w + 2, :], wk(m[0], 0, 2, 0, DH)).then_inc(sem("w2c_in"), 16)
            link(pool.memset(ident[:, :], 0.0))
            pool.affine_select(out=ident[:, :], in_=ident[:, :], compare_op=ALU.not_equal, fill=1.0, base=0,
                               pattern=[[-1, P]], channel_multiplier=1).then_inc(sem("ident"), 1)
            link(pool.memset(causal[:, :], 0.0))
            link(pool.memset(cneg[:, :, :], 0.0))
            link(pool.affine_select(out=causal[:, :], in_=causal[:, :], compare_op=ALU.is_ge, fill=NEG, base=0,
                                    pattern=[[-1, P]], channel_multiplier=1))
            link(pool.affine_select(out=cneg[:, :, :], in_=cneg[:, :, :], compare_op=ALU.is_ge, fill=NEG, base=1 - CMP_BLOCK,
                                    pattern=[[P, TT], [-CMP_STRIDE, 16]], channel_multiplier=1))
            pool.wait_ge(sem("b1_in"), 48)
            link(pool.tensor_copy(b1s[:, :], A2[0:96, :]))
            link(pool.tensor_tensor(A2[0:96, :], A2[0:96, :], b1s[:, :], ALU.subtract))
            link(pool.tensor_copy(b1s[32:64, :], A2[32:64, :]))
            link(pool.tensor_copy(b1s[64:96, :], A2[64:96, :]))
            link(pool.tensor_tensor(A2[64:96, :], A2[64:96, :], b1s[64:96, :], ALU.subtract))
            link(pool.tensor_copy(b1s[64:96, :], A2[64:96, :]))
            link(pool.memset(LK, 0.0))
            pool.nop().then_inc(sem("pool_masks"), 1)

            pool.wait_ge(sem("branch"), 2)
            pool.dma_start(b2s, moe_b2[0]).then_inc(sem("b2_in"), 16)
            for h in range(2):
                link(pool.iota(iota[:, CAP * h:CAP * (h + 1)], [[1, CAP]], base=0, channel_multiplier=0, allow_small_or_imprecise_dtypes=True))
            link(pool.iota(iotaE, [[1, NE]], base=0, channel_multiplier=0, allow_small_or_imprecise_dtypes=True))
            link(pool.iota(iota16, [[1, 16]], base=0, channel_multiplier=0, allow_small_or_imprecise_dtypes=True))
            link(pool.iota(rcol[:, 0:1], [[0, 1]], base=0, channel_multiplier=1, allow_small_or_imprecise_dtypes=True))
            link(pool.memset(ones, 1.0))
            link(pool.memset(oh96, 0.0))
            link(pool.memset(ohT, 0.0))
            link(pool.memset(upper, 1.0))
            link(pool.affine_select(out=upper, in_=upper, compare_op=ALU.is_gt, fill=0.0, base=0,
                                    pattern=[[1, P]], channel_multiplier=-1))
            pool.nop().then_inc(sem("pool_masks"), 1)

        @block.scalar
        def _(act_e):
            a = act_e
            n = [0]

            def link(i):
                n[0] += 1
                i.then_inc(sem("act_chain"), 1)
                a.wait_ge(sem("act_chain"), n[0])

            def root(n, st):
                a.wait_ge(sem("square"), n)
                a.activation(st, st, ACT.Sqrt).then_inc(sem("rsqrt"), 1)

            a.dma_start(ccol[:, 0:KD], c[0].rearrange("(k p) -> p k", p=P), allow_slow_non_contiguous=True).then_inc(sem("c_in"), 16)
            for r0, v in ((R_N1, norm1_g), (R_CONVB, conv_b), (R_BA, lru_ba), (R_BX, lru_bx), (R_LAM, lru_lambda), (R_N2, norm2_g)):
                a.dma_start(praw[r0:r0 + 8, :], v[0].rearrange("(k p) -> k p", p=P)).then_inc(sem("params_in"), 16)
            a.dma_start(praw[R_CONVW:R_CONVW + 32, :], conv_w[0].rearrange("w (k p) -> (w k) p", p=P)).then_inc(sem("params_in"), 16)
            a.dma_start(praw[R_ADAB:R_ADAB + 48, :], ada_b[0].rearrange("(k p) -> k p", p=P)).then_inc(sem("params_in"), 16)
            for t in range(TT):
                a.dma_start(xs[:, t, :], x[0, t * P:(t + 1) * P, :]).then_inc(sem("x_in"), 16)
            a.wait_ge(sem("c_in"), 16)
            a.activation(ccol[:, KD:2 * KD], ccol[:, 0:KD], ACT.Sigmoid).then_inc(sem("sig_c"), 1)
            a.wait_ge(sem("x_in"), 32)
            for t in range(TT):
                link(a.activation(xn[:, t, :], xs[:, t, :], ACT.Square, accum_out=stat[:, t:t + 1]))
            a.nop().then_inc(sem("x_sq"), 1)
            root(1, stat[:, 2:4])

            def wait_job(j):
                a.wait_ge(sem("job_full"), JOB[j] + 1)
                return PAIR[JOB[j] % 2]

            a.wait_ge(sem("lam_abs"), 1)
            a.activation(spl[:, 0, :], spl[:, 0, :], ACT.Exp).then_inc(sem("lam_exp"), 1)
            def keys_values(j, b):
                p = wait_job(j).rearrange("p (t n) -> p t n", t=TT)
                link(a.activation(QK[:, :, 8 + 2 * b:10 + 2 * b, :], p[:, :, 0:256].rearrange("p t (g d) -> p t g d", g=2), ACT.Copy))
                a.activation(vtm[:, b, :, :], p[:, :, 256:512], ACT.Copy).then_inc(sem("job_read"), 1)

            def evacuate(job):
                name, h = job
                p = wait_job(job)
                p4 = p.rearrange("p (k t) -> p k t", k=4)
                if name == "lrux":
                    a.wait_ge(sem("lx_zero"), h + 1)
                    a.activation(lx[:, :, 3:3 + T], p4, ACT.Copy).then_inc(sem("job_read"), 1)
                elif name == "lrug":
                    a.activation(olT[:, 4 * h:4 * h + 4, :], p4, ACT.Gelu_apprx_tanh).then_inc(sem("job_read"), 1)
                elif name == "merge":
                    a.activation(mg[:, 4 * h:4 * h + 4, :], p4, ACT.Sigmoid).then_inc(sem("job_read"), 1)
                elif name in "ri":
                    dst, r0 = (rr, R_BA) if name == "r" else (ii, R_BX)
                    if h == 1:
                        a.wait_ge(sem("lru_done"), 1)
                    for k in range(4):
                        q = a.activation(dst[:, k, :], p[:, k * T:(k + 1) * T], ACT.Sigmoid, bias=pcol[:, r0 + 4 * h + k:r0 + 4 * h + k + 1])
                    q.then_inc(sem("job_read"), 1)

            keys_values(("kslc",), 0)
            a.wait_ge(sem("angles"), 1)
            a.activation(cosT, cosT, ACT.Sin).then_inc(sem("sincos"), 1)
            a.activation(sinT, sinT, ACT.Sin).then_inc(sem("sincos"), 1)
            keys_values(("kwin",), 1)
            root(2, stat[:, 64:68])
            root(3, stat[:, 64:68])
            for h in range(2):
                p = wait_job(("q", h)).rearrange("p (t g d) -> p t g d", t=TT, g=4)
                a.activation(QK[:, :, 4 * h:4 * h + 4, :], p, ACT.Copy).then_inc(sem("job_read"), 1)
                root(4 + h, stat[:, 64:72])
            p = wait_job(("kcmp",))
            a.activation(kcT, p.rearrange("p (k t) -> p k t", k=4), ACT.Copy).then_inc(sem("job_read"), 1)
            a.wait_ge(sem("ng_full"), 1)
            a.activation(ng[:, :, :], ps[:, 4, 0:TT * N_NSAG].rearrange("p (t n) -> p t n", t=TT), ACT.Sigmoid).then_inc(sem("ng_read"), 1)
            evacuate(("lrux", 0))
            a.wait_ge(sem("cmp_used"), 4)
            a.activation(uu, ps[:, 4, 0:CMP_HIDDEN], ACT.Gelu_apprx_tanh).then_inc(sem("cmp_gelu"), 1)
            for j in range(10):
                a.wait_ge(sem("qk_turned"), j + 1)
                dst = (qT[:, 2 * j:2 * j + 2, :] if j < 4 else qrT[:, 2 * j - 8:2 * j - 6, :] if j < 8 else kT[:, 2 * j - 16:2 * j - 14, :])
                a.activation(dst, ps[:, 4 + j % 2, :].rearrange("p (h t) -> p h t", h=2), ACT.Copy).then_inc(sem("qk_read"), 1)
            a.wait_ge(sem("uT_full"), 1)
            a.activation(uT, ps[:, 6, 0:256].rearrange("p (a b) -> p a b", a=2), ACT.Copy).then_inc(sem("uT_read"), 1)
            for job, _, last in pieces_of(-1):
                if last:
                    evacuate(job)
            root(6, stat[0:64, 80:81])

            def exps(m):
                g, t, b = UNITS[m]
                a.wait_ge(sem("att_max"), m + 1)
                nk = N_CMP if b == 0 else P * (t + 1)
                for h in range(HPG):
                    src = Sb[:, m % 2, h * T:h * T + nk]
                    dst = Pc[:, h, 32 * g:32 * g + N_CMP] if b == 0 else src
                    i = a.activation(dst, src, ACT.Exp, scale=SCALE, bias=stat[:, 16 + 8 * (m % 2) + h:17 + 8 * (m % 2) + h],
                                     accum_out=stat[:, 32 + 8 * (m % 2) + h:33 + 8 * (m % 2) + h])
                i.then_inc(sem("att_exp"), 1)

            def turned(m):
                g, t, b = UNITS[m]
                a.wait_ge(sem("att_turned"), m + 1)
                if m >= 1:
                    a.wait_ge(sem("att_read"), m)
                if b == 0:
                    a.activation(PT[0:64, 0, :], ps[0:64, 4, :], ACT.Copy).then_inc(sem("att_pT"), 1)
                else:
                    a.activation(PT[:, 0:t + 1, :], ps[:, 4:5 + t, :], ACT.Copy).then_inc(sem("att_pT"), 1)

            def head_out(m):
                g, t, b = UNITS[m]
                if b == 2:
                    a.wait_ge(sem("att_read"), m + 1)
                    a.activation(oT[:, 4 * g:4 * g + 4, t * P:(t + 1) * P], ps[:, 6, :].rearrange("p (h q) -> p h q", h=4), ACT.Copy).then_inc(sem("oT_full"), 1)

            def lru_exp(h):
                a.wait_ge(sem("log_a"), h + 1)
                a.activation(xc, rr, ACT.Exp).then_inc(sem("lru_exp"), 1)
                a.activation(lt, rr, ACT.Tanh, scale=0.5).then_inc(sem("lru_exp"), 1)

            def lru_root(h):
                a.wait_ge(sem("one_minus_a2"), h + 1)
                a.activation(xc, xc, ACT.Sqrt).then_inc(sem("lru_sqrt"), 1)

            for m in range(len(UNITS)):
                exps(m)
                if m in LRU_AT:
                    {1: lru_exp, 2: lru_root}.get(LRU_AT[m][1], lambda h: None)(LRU_AT[m][0])
                turned(m)
                head_out(m)
                for job, _, last in pieces_of(m):
                    if last and job[0] != "ylru":
                        evacuate(job)

            def expert_sigmoid(q):
                a.wait_ge(sem("glu"), q + 1)
                a.activation(sig, glu, ACT.Sigmoid, scale=ALPHA).then_inc(sem("sig"), 1)

            def expert_turned(q):
                a.wait_ge(sem("act_turned"), q + 1)
                a.activation(actT, Hps[:, 0:512].rearrange("p (j m) -> p j m", j=4), ACT.Copy).then_inc(sem("actT"), 1)
                a.activation(selT, Hps[:, 512:512 + TT * P].rearrange("p (t m) -> p t m", t=TT), ACT.Copy).then_inc(sem("selT"), 1)

            def expert_y(q):
                a.wait_ge(sem("w2_used"), (q + 1) * 4)
                a.activation(ysb, Yps, ACT.Copy).then_inc(sem("y_read"), 1)

            root(7, stat[:, 50:52])
            for t in range(TT):
                a.wait_ge(sem("top4"), t + 1)
                a.activation(topw[:, t, 0:TOPK], top[:, t, 0:TOPK], ACT.Exp, bias=stat[:, 60 + t:61 + t], accum_out=stat[:, 62 + t:63 + t]).then_inc(sem("top_exp"), 1)
            expert_sigmoid(0)
            expert_turned(0)
            with a.Fori(1, NE) as q:
                expert_sigmoid(q)
                expert_y(q - 1)
                expert_turned(q)
            expert_y(NE - 1)
            a.wait_ge(sem("xtab"), 1)
            more = a.value_load(xn_i, min_val=0, max_val=XP)
            with a.Fori(0, XP) as i:
                with a.If(more > i):
                    expert_sigmoid(i + NE)
                    expert_turned(i + NE)
                    expert_y(i + NE)

        @block.tensor
        def _(pe):
            def full(u, times=1):
                nload = lambda w: 2 if w[0] in ("lrugate", "cmp") else 1
                k = SLOT[u]
                total = sum(nload(STREAM[j]) for j in range(k % NSLOT, k + 1, NSLOT))
                pe.wait_ge(sem(f"stream_full{k % NSLOT}"), 16 * total)
                return slot(u)

            def ada(third, k2, bank):
                s = full(("ada", third, k2)).rearrange("p (k n) -> p k n", k=2)
                for k in range(2):
                    for g in range(4):
                        i = pe.matmul(ps[32 * g:32 * g + 32, bank, :], cs32[:, 2 * k2 + k, :], s[:, k, 512 * g:512 * g + 512],
                                      start=(k2 == 0 and k == 0), stop=(k2 == 3 and k == 1), skip_group_check=True)
                i.then_inc(sem("ada_used"), 1)

            pe.wait_ge(sem("cs32"), 1)
            for k2 in range(4):
                ada(0, k2, 7)
            pe.wait_ge(sem("ident"), 1)
            pe.wait_ge(sem("params_in"), 16 * 8)
            pe.transpose(ps[:, 6, 0:P], praw, ident[:, :]).then_inc(sem("params_turned"), 1)
            pe.wait_ge(sem("pe_in"), 32)
            pe.transpose(ps[:, 6, P:P + 64], peraw, ident[0:64, 0:64]).then_inc(sem("params_turned"), 1)
            pe.wait_ge(sem("xn"), 1)
            for k in range(KD):
                for t in range(TT):
                    i = pe.transpose(ps[:, k // 2, (k % 2) * T + t * P:(k % 2) * T + (t + 1) * P], xn[:, t, k * P:(k + 1) * P], ident[:, :])
            i.then_inc(sem("x_turned"), 1)
            pe.wait_ge(sem("params_read"), 1)
            pe.wait_ge(sem("modrow"), 1)
            for j in range(4):
                i = pe.transpose(ps[:, 6, j * P:(j + 1) * P], modrow[:, j * P:(j + 1) * P], ident[:, :])
            i.then_inc(sem("mod_turned"), 1)
            pe.wait_ge(sem("hT"), 1)

            def job_bank(j):
                n = JOB[j]
                if n >= 2:
                    pe.wait_ge(sem("job_read"), n - 1)
                return PAIR[n % 2]

            def rows_out(u, piece):
                s = full(u).rearrange("p (k n) -> p k n", k=KD)
                if piece == 0:
                    job_bank(u)
                p, j = PAIR[JOB[u] % 2], piece
                for k in range(KD):
                    i = pe.matmul(p[:, j * T:(j + 1) * T], s[:, k, j * P:(j + 1) * P], hT[:, k, :], start=(k == 0), stop=(k == KD - 1))
                if piece == 3:
                    i.then_inc(sem("job_full"), 1)

            def tokens_out(u):
                s = full(u).rearrange("p (k n) -> p k n", k=KD)
                p = job_bank(u)
                for t in range(TT):
                    for k in range(KD):
                        i = pe.matmul(p[:, t * 512:(t + 1) * 512], hT[:, k, t * P:(t + 1) * P], s[:, k, :], start=(k == 0), stop=(k == KD - 1))
                i.then_inc(sem("job_full"), 1)

            def lru_gate(name, h):
                s = full(("lrugate", h))[:, 0:2048].rearrange("p (w a j) -> p w a j", w=2, a=4)
                pe.wait_ge(sem("conv"), h + 1)
                p = job_bank((name, h))
                for j in range(4):
                    for ic in range(2):
                        i = pe.matmul(p[:, j * T:(j + 1) * T], s[:, "ri".index(name), 2 * (j // 2) + ic, (j % 2) * P:(j % 2 + 1) * P],
                                      xc[:, 2 * (j // 2) + ic, :], start=(ic == 0), stop=(ic == 1))
                i.then_inc(sem("job_full"), 1)

            def lru_branch(h, piece):
                s = full(("bo", 1, h)).rearrange("p (k n) -> p k n", k=KD)
                if piece == 0:
                    pe.wait_ge(sem("lru_done"), 2)
                    job_bank(("ylru", h))
                p, j = PAIR[JOB[("ylru", h)] % 2], piece
                for k in range(KD):
                    i = pe.matmul(p[:, j * T:(j + 1) * T], s[:, k, j * P:(j + 1) * P], olT[:, k, :], start=(k == 0), stop=(k == KD - 1))
                if piece == 3:
                    i.then_inc(sem("job_full"), 1)

            def piece_of(job, piece, last):
                if job[0] in ("r", "i"):
                    lru_gate(*job)
                elif job[0] == "ylru":
                    lru_branch(job[1], piece)
                else:
                    rows_out(job, piece)

            for u in (("kslc",), ("kwin",), ("q", 0), ("q", 1)):
                tokens_out(u)
            for piece in range(4):
                rows_out(("kcmp",), piece)
            for t in range(TT):
                for k in range(KD):
                    if t == 0 and k == 0:
                        pe.wait_ge(sem("small_in"), 16 * 12)
                    i = pe.matmul(ps[:, 4, t * N_NSAG:(t + 1) * N_NSAG], hT[:, k, t * P:(t + 1) * P], gw[:, k, :], start=(k == 0), stop=(k == KD - 1))
            i.then_inc(sem("ng_full"), 1)
            for piece in range(4):
                rows_out(("lrux", 0), piece)
            pe.wait_ge(sem("cmp_rows"), 1)
            pe.wait_ge(sem("ng_read"), 1)
            for c4 in range(4):
                s = full(("cmp", c4)).rearrange("p (w l n) -> p w l n", w=2, l=8)
                for l8 in range(8):
                    l = 8 * c4 + l8
                    pe.matmul(ps[0:64, 4, 0:CMP_HIDDEN], LK[:, l, :], s[:, 0, l8, :], start=(l == 0), stop=(l == 31), skip_group_check=True)
                    i = pe.matmul(ps[64:128, 4, 0:CMP_HIDDEN], LV[:, l, :], s[:, 1, l8, :], start=(l == 0), stop=(l == 31), skip_group_check=True)
                i.then_inc(sem("cmp_used"), 1)
            pe.wait_ge(sem("roped"), 1)
            pe.wait_ge(sem("cmp_gelu"), 1)
            for j in range(10):
                if j >= 2:
                    pe.wait_ge(sem("qk_read"), j - 1)
                for h in range(2):
                    for t in range(TT):
                        src = (QK[:, t, 2 * j + h, :] if j < 4 else QR[:, t, 2 * j - 8 + h, :])
                        i = pe.transpose(ps[:, 4 + j % 2, h * T + t * P:h * T + (t + 1) * P], src, ident[:, :])
                i.then_inc(sem("qk_turned"), 1)
            pe.wait_ge(sem("mod_read"), 1)
            for j in range(2):
                i = pe.transpose(ps[:, 6, j * P:(j + 1) * P], uu[:, j * P:(j + 1) * P], ident[:, :])
            i.then_inc(sem("uT_full"), 1)
            early = pieces_of(-1)
            piece_of(*early[0])
            pe.wait_ge(sem("uT_read"), 1)
            pe.wait_ge(sem("w2c_in"), 32)
            for w in range(2):
                for j in range(2):
                    i = pe.matmul(ps[0:64, 6, 256 + w * P:256 + (w + 1) * P], uT[:, j, 64 * w:64 * w + 64], w2c[:, 2 * w + j, :],
                                  start=(j == 0), stop=(j == 1))
            i.then_inc(sem("cmp2_full"), 1)
            for piece in early[1:3]:
                piece_of(*piece)
            pe.wait_ge(sem("kcn"), 1)
            pe.transpose(ps[:, 6, 0:64], kcn, ident[0:64, 0:64]).then_inc(sem("kc_turned"), 1)
            piece_of(*early[3])

            def scores(m):
                g, t, b = UNITS[m]
                if m >= 1:
                    pe.wait_ge(sem("att_pT"), m)
                for h in range(HPG):
                    hd = HPG * g + h
                    if b == 0:
                        i = pe.matmul(Hps[:, h * 16:h * 16 + N_CMP], qT[:, hd, t * P:(t + 1) * P], kccT[:, 32 * g:32 * g + N_CMP], start=True, stop=True)
                    else:
                        nk = P * (t + 1)
                        i = pe.matmul(Hps[:, h * nk:(h + 1) * nk], qrT[:, hd, t * P:(t + 1) * P], kT[:, 2 * (b - 1) + g, 0:nk], start=True, stop=True)
                i.then_inc(sem("scores"), 1)

            def turn(m):
                g, t, b = UNITS[m]
                pe.wait_ge(sem("att_p"), m + 1)
                for h in range(HPG):
                    if b == 0:
                        i = pe.transpose(ps[0:64, 4, h * P:(h + 1) * P], Pc[:, h, :], ident[:, :])
                    else:
                        for kt in range(t + 1):
                            i = pe.transpose(ps[:, 4 + kt, h * P:(h + 1) * P], Sb[:, m % 2, h * T + kt * P:h * T + (kt + 1) * P], ident[:, :])
                i.then_inc(sem("att_turned"), 1)

            def values(m):
                g, t, b = UNITS[m]
                pe.wait_ge(sem("att_pT"), m + 1)
                if b == 0:
                    if m >= 3:
                        pe.wait_ge(sem("oT_full"), m // 3)
                    i = pe.matmul(ps[:, 6, :], vcs, PT[0:64, 0, :], start=True, stop=False, skip_group_check=True)
                else:
                    for kt in range(t + 1):
                        i = pe.matmul(ps[:, 6, :], vtm[:, b - 1, kt, g * DH:(g + 1) * DH], PT[:, kt, :], start=False,
                                      stop=(b == 2 and kt == t), skip_group_check=True)
                i.then_inc(sem("att_read"), 1)

            pe.wait_ge(sem("qk_read"), 10)
            pe.wait_ge(sem("kccT"), 1)
            for m in range(len(UNITS)):
                scores(m)
                for piece in pieces_of(m)[:2]:
                    piece_of(*piece)
                turn(m)
                for piece in pieces_of(m)[2:]:
                    piece_of(*piece)
                if m in ADA_AT:
                    if ADA_AT[m] == (2, 0):
                        pe.wait_ge(sem("mod_rows"), 1)
                    ada(*ADA_AT[m], 7)
                values(m)

            def late_modulations():
                pe.wait_ge(sem("pick"), 1)
                for third in (1, 2):
                    if third == 2:
                        pe.wait_ge(sem("mod_read"), 2)
                    for j in range(4):
                        i = pe.transpose(ps[:, 4, j * P:(j + 1) * P], mod2[:, third - 1, j * P:(j + 1) * P], ident[:, :])
                    i.then_inc(sem("mod2_turned"), 1)
                    for j in range(2):
                        n = 2 * (third - 1) + j
                        if n:
                            pe.wait_ge(sem("gate_read"), n)
                        pe.matmul(ps[:, 6, :], pickt[:, n, :], mod2[:, third - 1, :], start=True, stop=True).then_inc(sem("gate_rows"), 1)

            pe.wait_ge(sem("oT_full"), NG * TT)
            for half in range(2):
                s = full(("bo", 0, half)).rearrange("p (k n) -> p k n", k=KD)
                pe.wait_ge(sem("y_taken"), half + 1)
                p = PAIR[JOB[("ylru", half)] % 2]
                for j in range(4):
                    for k in range(KD):
                        i = pe.matmul(p[:, j * T:(j + 1) * T], s[:, k, j * P:(j + 1) * P], oT[:, k, :], start=(k == 0), stop=(k == KD - 1))
                i.then_inc(sem("branch"), 1)
                if half == 0:
                    late_modulations()
            pe.wait_ge(sem("merged"), 2)
            for half in range(2):
                s = full(("wo", half)).rearrange("p (k n) -> p k n", k=KD)
                for t in range(TT):
                    for k in range(KD):
                        i = pe.matmul(PAIR[half][:, t * 512:(t + 1) * 512], mergedT[:, k, t * P:(t + 1) * P], s[:, k, :], start=(k == 0), stop=(k == KD - 1))
                i.then_inc(sem("wo_full"), 1)
            pe.wait_ge(sem("xn2"), 1)
            for k in range(KD):
                for t in range(TT):
                    i = pe.transpose(ps[:, k // 2, (k % 2) * T + t * P:(k % 2) * T + (t + 1) * P], xn2[:, t, k * P:(k + 1) * P], ident[:, :])
            i.then_inc(sem("x2_turned"), 1)
            pe.wait_ge(sem("h2T"), 1)
            for t in range(TT):
                for k in range(KD):
                    i = pe.matmul(ps[:, 4, t * NE:(t + 1) * NE], hT[:, k, t * P:(t + 1) * P], rw[:, k, :], start=(k == 0), stop=(k == KD - 1))
            i.then_inc(sem("logits"), 1)
            pe.wait_ge(sem("mask"), 1)
            pe.wait_ge(sem("pool_masks"), 2)
            pe.matmul(ps[:, 5, 0:NE], upper, msk[:, 0, :], start=True, stop=True)
            pe.matmul(ps[:, 5, NE:2 * NE], ones, msk[:, 0, :], start=True, stop=False)
            pe.matmul(ps[:, 5, NE:2 * NE], upper, msk[:, 1, :], start=False, stop=True)
            pe.matmul(ps[:, 5, 2 * NE:3 * NE], ones, msk[:, 0, :], start=True, stop=False)
            pe.matmul(ps[:, 5, 2 * NE:3 * NE], ones, msk[:, 1, :], start=False, stop=True).then_inc(sem("places"), 1)
            pe.wait_ge(sem("pos"), 1)
            for t in range(TT):
                pe.transpose(ps[0:NE, 6, t * P:(t + 1) * P], wts[:, t, :], ident[:, :])
                i = pe.transpose(ps[0:NE, 7, t * P:(t + 1) * P], pos[:, t, :], ident[:, :])
            i.then_inc(sem("routes_turned"), 1)
            pe.wait_ge(sem("ohx"), 1)
            pe.transpose(ps[0:NE, 4, 0:P], ohx, ident[:, :])
            pe.transpose(ps[0:8, 4, P:2 * P], xcol, ident[:, :]).then_inc(sem("xcols"), 1)
            pe.wait_ge(sem("wT"), 1)
            pe.wait_ge(sem("b2_in"), 16)
            pe.wait_ge(sem("x2_read"), 1)
            for t in range(TT):
                for h in range(2):
                    pe.matmul(ps[:, 2 * t + h, :], wT[:, t * P:(t + 1) * P], b2s[:, h * 512:(h + 1) * 512], start=True, stop=False, skip_group_check=True)
            pe.wait_ge(sem("ohT"), 1)
            for t in range(TT):
                pe.matmul(ps[:, 4, 256 + t * 32:256 + t * 32 + XP], posT[:, t * P:(t + 1) * P], ohT[:, 0:XP], start=True, stop=True)
                pe.matmul(ps[:, 4, 320 + t * 32:320 + t * 32 + XP], wT[:, t * P:(t + 1) * P], ohT[:, 0:XP], start=True, stop=True)
            pe.matmul(ps[:, 4, 384:384 + XP], pick1, chk[0:8, 0:XP], start=True, stop=True).then_inc(sem("xmats"), 1)

            def gather(q):
                pe.wait_ge(sem("sel"), q + 1)
                for k in range(KD):
                    for t in range(TT):
                        i = pe.matmul(Gps[:, k * CAP:(k + 1) * CAP], xn2[:, t, k * P:(k + 1) * P], sel[:, t, :], start=(t == 0), stop=(t == TT - 1))
                i.then_inc(sem("rows"), 1)

            def first(q):
                pe.wait_ge(sem("xT"), q + 1)
                pe.wait_ge(sem("ohp"), q + 1)
                if not (isinstance(q, int) and q == 0):
                    pe.wait_ge(sem("selT"), q)
                parts = [(g, b) for b in range(2) for g in range(2)]
                for g, b in parts:
                    cc = 1024 * g + 512 * b
                    pe.matmul(Hps[64 * g:64 * g + 64, b * 512:(b + 1) * 512], ohp, b1s[:, cc:cc + 512], start=True, stop=False, skip_group_check=True)
                for k in range(KD):
                    pe.wait_ge(sem(f"w1_full{k}"), (q + 1) * 16)
                    for g, b in parts:
                        cc = 1024 * g + 512 * b
                        i = pe.matmul(Hps[64 * g:64 * g + 64, b * 512:(b + 1) * 512], xT[:, k, :], w1v[:, k, cc:cc + 512],
                                      start=False, stop=(k == KD - 1), skip_group_check=True)
                    i.then_inc(sem("w1_used"), 1)

            def turn_act(q):
                pe.wait_ge(sem("act"), q + 1)
                for j in range(4):
                    pe.transpose(Hps[:, j * P:(j + 1) * P], act[:, j * P:(j + 1) * P], ident[:, :])
                pe.wait_ge(sem("selw"), q + 1)
                for t in range(TT):
                    i = pe.transpose(Hps[:, 512 + t * P:512 + (t + 1) * P], selw[:, t, :], ident[:, :])
                i.then_inc(sem("act_turned"), 1)

            def second(q):
                pe.wait_ge(sem("actT"), q + 1)
                for s in range(4):
                    pe.wait_ge(sem(f"w2_full{s}"), (q + 1) * 16)
                    for k in (2 * s, 2 * s + 1):
                        for g in range(2):
                            i = pe.matmul(Yps[64 * g:64 * g + 64, :], actT[:, k % 4, 64 * (k // 4):64 * (k // 4) + 64],
                                          w2v[:, k, g * 512:(g + 1) * 512], start=(k == 0), stop=(k == 7), skip_group_check=True)
                    i.then_inc(sem("w2_used"), 1)

            def scatter(q):
                pe.wait_ge(sem("y_read"), q + 1)
                pe.wait_ge(sem("selT"), q + 1)
                for t in range(TT):
                    for g in range(2):
                        i = pe.matmul(ps[:, 2 * t + g, :], selT[64 * g:64 * g + 64, t, :], ysb[64 * g:64 * g + 64, :], start=False, stop=False, skip_group_check=True)
                i.then_inc(sem("scattered"), 1)

            pe.wait_ge(sem("tables"), 1)
            gather(0)
            first(0)
            gather(1)
            turn_act(0)
            with pe.Fori(1, NE - 1) as q:
                first(q)
                second(q - 1)
                gather(q + 1)
                scatter(q - 1)
                turn_act(q)
            first(NE - 1)
            second(NE - 2)
            scatter(NE - 2)
            turn_act(NE - 1)
            second(NE - 1)
            scatter(NE - 1)
            more = pe.value_load(xn_i, min_val=0, max_val=XP)
            with pe.Fori(0, XP) as i:
                with pe.If(more > i):
                    gather(i + NE)
                    first(i + NE)
                    turn_act(i + NE)
                    second(i + NE)
                    scatter(i + NE)

        @block.vector
        def _(v):
            n = [0]

            def link(i):
                n[0] += 1
                i.then_inc(sem("dve_chain"), 1)
                v.wait_ge(sem("dve_chain"), n[0])

            def done(name):
                v.nop().then_inc(sem(name), 1)

            tt, ts, stt = v.tensor_tensor, v.tensor_scalar, v.scalar_tensor_tensor

            v.wait_ge(sem("sig_c"), 1)
            v.wait_ge(sem("c_in"), 16)
            tt(cs32[:, :, :], ccol[:, 0:KD].unsqueeze(2).to_broadcast((P, KD, 32)), ccol[:, KD:2 * KD].unsqueeze(2).to_broadcast((P, KD, 32)),
               ALU.mult).then_inc(sem("cs32"), 1)
            v.wait_ge(sem("x_sq"), 1)
            link(ts(stat[:, 2:4], stat[:, 0:2], 1.0 / D, EPS, ALU.mult, ALU.add))
            link(v.reciprocal(stat[:, 2:4], stat[:, 2:4]))
            done("square")
            v.wait_ge(sem("rsqrt"), 1)
            for t in range(TT):
                link(ts(xn[:, t, :], xs[:, t, :], stat[:, 2 + t:3 + t], None, ALU.mult))
            done("xn")
            v.wait_ge(sem("params_turned"), 2)
            link(v.tensor_copy(pcol[:, :], ps[:, 6, 0:P]))
            link(v.tensor_copy(peT[:, :], ps[:, 6, P:P + 64]))
            done("params_read")
            v.wait_ge(sem("ada_used"), 4)
            v.tensor_copy(modrow, ps[:, 7, :]).then_inc(sem("modrow"), 1)
            v.wait_ge(sem("mod_turned"), 1)
            mc = ps[:, 6, :].rearrange("p (s g r) -> p g s r", s=4, g=4)[:, :, :, 0]
            m3v = m3[:, :].rearrange("p (g s) -> p g s", g=4)
            link(tt(m3v, mc, pcol[:, R_ADAB:R_ADAB + 16].rearrange("p (g s) -> p g s", g=4), ALU.add))
            done("mod_read")
            link(v.tensor_copy(S1[:, :], m3[:, 0:8]))
            link(stt(G1[:, :], m3[:, 8:16], 1.0, pcol[:, R_N1:R_N1 + 8], ALU.add, ALU.mult))
            v.wait_ge(sem("x_turned"), 1)
            for k in range(KD):
                link(ts(hT[:, k, :], ps[:, k // 2, (k % 2) * T:(k % 2 + 1) * T], G1[:, k:k + 1], S1[:, k:k + 1], ALU.mult, ALU.add))
            done("hT")
            link(v.memset(lx[:, :, 0:3], 0.0))
            done("lx_zero")
            lam = pcol[:, R_LAM:R_LAM + 8]
            z, s_, s2, acc = (spl[:, j, :] for j in range(4))
            link(stt(z, lam, -1.0, lam, ALU.mult, ALU.min))
            done("lam_abs")
            v.wait_ge(sem("lam_exp"), 1)
            link(ts(s_, z, 2.0, None, ALU.add))
            link(v.reciprocal(s_, s_))
            link(tt(s_, s_, z, ALU.mult))
            link(tt(s2, s_, s_, ALU.mult))
            link(ts(acc, s2, 1.0 / 15, 1.0 / 13, ALU.mult, ALU.add))
            for d in (11, 9, 7, 5, 3, 1):
                link(tt(acc, acc, s2, ALU.mult))
                link(ts(acc, acc, 1.0 / d, None, ALU.add))
            link(tt(acc, acc, s_, ALU.mult))
            link(ts(z, lam, -1.0, 0.0, ALU.mult, ALU.max))
            link(stt(acc, acc, 2.0, z, ALU.mult, ALU.add))
            link(ts(acc, acc, -LRU_C, None, ALU.mult))
            spf = acc

            v.wait_ge(sem("small_in"), 16 * 12)
            link(v.tensor_copy(pos_f[:, :], pos_i[:, :]))
            for t in range(TT):
                link(ts(ang[:, t, :], ang[:, t, :], pos_f[:, t:t + 1], None, ALU.mult))
            C1 = 6.28125
            C2 = float(np.float32(np.floor((2 * np.pi - C1) * 2 ** 22) / 2 ** 22))
            C3 = float(2 * np.pi - C1 - C2)
            BIG = 1.5 * 2 ** 23
            link(ts(cosT, ang, 1.0 / (2 * np.pi), BIG, ALU.mult, ALU.add))
            link(ts(cosT, cosT, -BIG, None, ALU.add))
            for cst in (C1, C2, C3):
                link(stt(ang, cosT, -cst, ang, ALU.mult, ALU.add))
            link(ts(sinT, ang, 3.1415925, -3.1415925, ALU.min, ALU.max))
            link(stt(cosT, sinT, -1.0, sinT, ALU.mult, ALU.min))
            link(ts(cosT, cosT, float(np.pi / 2), None, ALU.add))
            done("angles")
            def convolution(h):
                v.wait_ge(sem("job_read"), JOB[("lrux", h)] + 1)
                for w in range(4):
                    for k in range(KH):
                        kk = 4 * h + k
                        cw = pcol[:, R_CONVW + 8 * w + kk:R_CONVW + 8 * w + kk + 1]
                        if w == 0:
                            i = ts(xc[:, k, :], lx[:, k, 0:T], cw, pcol[:, R_CONVB + kk:R_CONVB + kk + 1], ALU.mult, ALU.add)
                        else:
                            i = stt(xc[:, k, :], lx[:, k, w:w + T], cw, xc[:, k, :], ALU.mult, ALU.add)
                    link(i)
                done("conv")

            def lru_step(h, step):
                if step == 0:
                    convolution(h)
                if step == 1:
                    v.wait_ge(sem("job_read"), JOB[("i", h)] + 1)
                    link(tt(rr, rr, spf[:, 4 * h:4 * h + 4].unsqueeze(2).to_broadcast((P, KH, T)), ALU.mult))
                    link(tt(ii, ii, xc, ALU.mult))
                    done("log_a")
                if step == 2:
                    v.wait_ge(sem("lru_exp"), 2 * h + 2)
                    link(stt(xc, xc, 1.0, lt, ALU.add, ALU.mult))
                    link(ts(rr, xc, 1.0, None, ALU.add))
                    link(stt(xc, xc, 2.0, xc, ALU.add, ALU.mult))
                    link(ts(xc, xc, -1.0, 0.0, ALU.mult, ALU.max))
                    done("one_minus_a2")
                    if h == 0:
                        link(v.memset(lx[:, :, 0:3], 0.0))
                        done("lx_zero")
                if step == 3:
                    v.wait_ge(sem("lru_sqrt"), h + 1)
                    link(tt(ii, ii, xc, ALU.mult))
                    for k in range(KH):
                        i = v.tensor_tensor_scan(xc[:, k, :], rr[:, k, :], ii[:, k, :], 0.0, ALU.mult, ALU.add)
                    link(i)
                    link(tt(olT[:, 4 * h:4 * h + 4, :], olT[:, 4 * h:4 * h + 4, :], xc, ALU.mult))
                    done("lru_done")

            def qk_norm(h0, nh, col, n):
                st = stat[:, 64:64 + TT * nh]
                for t in range(TT):
                    q = QK[:, t, h0:h0 + nh, :]
                    sq = QR[:, t, h0:h0 + nh, :]
                    link(tt(sq, q, q, ALU.mult))
                    link(v.tensor_reduce(stat[:, 64 + nh * t:64 + nh * (t + 1)], sq, AX.X, ALU.add))
                link(ts(st, st, 1.0 / DH, EPS, ALU.mult, ALU.add))
                link(v.reciprocal(st, st))
                done("square")
                v.wait_ge(sem("rsqrt"), n)
                for t in range(TT):
                    q = QK[:, t, h0:h0 + nh, :]
                    link(tt(q, q, stat[:, 64 + nh * t:64 + nh * (t + 1)].unsqueeze(2).to_broadcast((P, nh, DH)), ALU.mult))
                    link(tt(q, q, gain[:, col:col + 1, :].to_broadcast((P, nh, DH)), ALU.mult))

            def rope(h0, nh):
                for t in range(TT):
                    x1, x2 = QK[:, t, h0:h0 + nh, 0:64], QK[:, t, h0:h0 + nh, 64:128]
                    r1, r2 = QR[:, t, h0:h0 + nh, 0:64], QR[:, t, h0:h0 + nh, 64:128]
                    tm = rtmp[:, t, 0:nh, :]
                    cb = cosT[:, t:t + 1, :].to_broadcast((P, nh, 64))
                    sb_ = sinT[:, t:t + 1, :].to_broadcast((P, nh, 64))
                    link(tt(tm, x2, sb_, ALU.mult))
                    link(tt(r1, x1, cb, ALU.mult))
                    link(tt(r1, r1, tm, ALU.subtract))
                    link(tt(tm, x1, sb_, ALU.mult))
                    link(tt(r2, x2, cb, ALU.mult))
                    link(tt(r2, r2, tm, ALU.add))

            v.wait_ge(sem("sincos"), 2)
            v.wait_ge(sem("job_read"), JOB[("kwin",)] + 1)
            qk_norm(8, 2, 2, 2)
            qk_norm(10, 2, 3, 3)
            rope(8, 4)
            for h in range(2):
                v.wait_ge(sem("job_read"), JOB[("q", h)] + 1)
                qk_norm(4 * h, 4, 0, 4 + h)
                rope(4 * h, 4)
            done("roped")
            v.wait_ge(sem("pool_masks"), 1)
            link(v.memset(LV, 0.0))
            v.wait_ge(sem("job_read"), JOB[("kcmp",)] + 1)
            for kv, L in enumerate((LK, LV)):
                for g in range(NG):
                    src = kcT[:, 2 * kv + g, :].rearrange("p (b l) -> p l b", l=16)
                    for h in range(2):
                        e = peT[:, 32 * kv + 16 * h:32 * kv + 16 * h + 16].unsqueeze(2).to_broadcast((P, 16, N_CMP))
                        i = tt(L[:, 16 * h:16 * h + 16, 32 * g:32 * g + N_CMP], src[:, :, h:h + N_CMP], e, ALU.add)
            link(i)
            done("cmp_rows")
            convolution(0)
            v.wait_ge(sem("cmp2_full"), 1)
            kp = ps[0:64, 6, 256:384]
            link(v.tensor_copy(vcs, ps[0:64, 6, 384:512]))
            link(v.tensor_copy(kcn, kp))
            link(tt(ksq, kcn, kcn, ALU.mult))
            link(v.tensor_reduce(stat[0:64, 80:81], ksq, AX.X, ALU.add))
            link(ts(stat[0:64, 80:81], stat[0:64, 80:81], 1.0 / DH, EPS, ALU.mult, ALU.add))
            link(v.reciprocal(stat[0:64, 80:81], stat[0:64, 80:81]))
            done("square")
            v.wait_ge(sem("rsqrt"), 6)
            link(ts(kcn, kcn, stat[0:64, 80:81], None, ALU.mult))
            link(tt(kcn, kcn, gain[0:64, 1, :], ALU.mult))
            done("kcn")
            v.wait_ge(sem("kc_turned"), 1)
            link(v.tensor_copy(kccT, ps[:, 6, 0:64]))
            done("kccT")

            def softmax_in(m):
                g, t, b = UNITS[m]
                v.wait_ge(sem("scores"), m + 1)
                if m >= 2:
                    v.wait_ge(sem("att_turned"), m - 1)
                S = Sb[:, m % 2, :].rearrange("p (h k) -> p h k", h=HPG)
                if b == 0:
                    p = Hps[:, 0:64].rearrange("p (h k) -> p h k", h=HPG)
                    nk = N_CMP
                    link(tt(S[:, :, 0:nk], p[:, :, 0:nk], cneg[:, t:t + 1, 0:nk].to_broadcast((P, HPG, nk)), ALU.add))
                    if m >= 3:
                        v.wait_ge(sem("att_turned"), m - 2)
                    link(v.memset(Pc, 0.0))
                else:
                    nk = P * (t + 1)
                    p = Hps[:, 0:HPG * nk].rearrange("p (h k) -> p h k", h=HPG)
                    if t == 1:
                        link(v.tensor_copy(S[:, :, 0:P], p[:, :, 0:P]))
                    link(tt(S[:, :, nk - P:nk], p[:, :, nk - P:nk], causal[:, :].unsqueeze(1).to_broadcast((P, HPG, P)), ALU.add))
                mx = stat[:, 16 + 8 * (m % 2):20 + 8 * (m % 2)]
                link(v.tensor_reduce(mx, S[:, :, 0:nk], AX.X, ALU.max))
                link(ts(mx, mx, NEG * 1e-10, -SCALE, ALU.max, ALU.mult))
                done("att_max")

            def softmax_out(m):
                g, t, b = UNITS[m]
                v.wait_ge(sem("att_exp"), m + 1)
                sm = stat[:, 32 + 8 * (m % 2):36 + 8 * (m % 2)]
                if b == 0:
                    link(ts(sm, sm, 1e-30, None, ALU.max))
                link(v.reciprocal(sm, sm))
                gb = ng[:, t, :].rearrange("p (h b) -> p h b", b=3)[:, HPG * g:HPG * g + HPG, b]
                link(tt(sm, sm, gb, ALU.mult))
                sbc = sm.unsqueeze(2)
                if b == 0:
                    q = Pc[:, :, 32 * g:32 * g + N_CMP]
                    link(tt(q, q, sbc.to_broadcast((P, HPG, N_CMP)), ALU.mult))
                else:
                    nk = P * (t + 1)
                    q = Sb[:, m % 2, :].rearrange("p (h k) -> p h k", h=HPG)[:, :, 0:nk]
                    link(tt(q, q, sbc.to_broadcast((P, HPG, nk)), ALU.mult))
                done("att_p")

            def lru_branch_gated(h):
                v.wait_ge(sem("job_full"), JOB[("ylru", h)] + 1)
                v.wait_ge(sem("job_read"), JOB[("merge", 3)] + 1)
                y = PAIR[JOB[("ylru", h)] % 2].rearrange("p (k t) -> p k t", k=4)
                mgv = mg[:, KD + 4 * h:KD + 4 * h + 4, :]
                link(tt(mgv, y, mgv, ALU.mult))
                done("y_taken")

            v.wait_ge(sem("qk_turned"), 10)
            for m in range(len(UNITS)):
                softmax_in(m)
                if m in LRU_AT:
                    lru_step(*LRU_AT[m])
                softmax_out(m)
                if m in (4, 9):
                    v.wait_ge(sem("ada_used"), 8 if m == 4 else 12)
                    link(v.tensor_copy(mod2[:, m // 5, :], ps[:, 7, :]))
                    done("mod_rows")
                if m == 11:
                    lru_branch_gated(0)

            def modulations():
                link(v.memset(pickt, 0.0))
                for g in range(4):
                    link(v.memset(pickt[32 * g:32 * g + 1, g, :], 1.0))
                done("pick")
                for third in (1, 2):
                    v.wait_ge(sem("mod2_turned"), third)
                    mc = ps[:, 4, :].rearrange("p (s g r) -> p g s r", s=4, g=4)[:, :, :, 0]
                    link(tt(m3v, mc, pcol[:, R_ADAB + 16 * third:R_ADAB + 16 * third + 16].rearrange("p (g s) -> p g s", g=4), ALU.add))
                    done("mod_read")
                    if third == 1:
                        link(v.tensor_copy(S2[:, :], m3[:, 8:16]))
                    else:
                        link(stt(G2[:, :], m3[:, 0:8], 1.0, pcol[:, R_N2:R_N2 + 8], ALU.add, ALU.mult))
                    gt = gate1 if third == 1 else gate2
                    for j in range(2):
                        v.wait_ge(sem("gate_rows"), 2 * (third - 1) + j + 1)
                        link(tt(gt[:, j * 512:(j + 1) * 512], gt[:, j * 512:(j + 1) * 512], ps[:, 6, :], ALU.add))
                        done("gate_read")

            lru_branch_gated(1)
            modulations()
            for half in range(2):
                v.wait_ge(sem("branch"), half + 1)
                y = PAIR[JOB[("ylru", half)] % 2].rearrange("p (k t) -> p k t", k=4)
                link(tt(mergedT[:, 4 * half:4 * half + 4, :], y, mg[:, 4 * half:4 * half + 4, :], ALU.mult))
                link(tt(mergedT[:, 4 * half:4 * half + 4, :], mergedT[:, 4 * half:4 * half + 4, :], mg[:, KD + 4 * half:KD + 4 * half + 4, :], ALU.add))
                done("merged")
            for half in range(2):
                v.wait_ge(sem("wo_full"), half + 1)
                p = PAIR[half].rearrange("p (t n) -> p t n", t=TT)
                tmp = A1[:, half * 1024:(half + 1) * 1024].rearrange("p (t n) -> p t n", t=TT)
                link(tt(tmp, p, gate1[:, half * 512:(half + 1) * 512].unsqueeze(1).to_broadcast((P, TT, 512)), ALU.mult))
                xv = xs[:, :, half * 512:(half + 1) * 512]
                link(tt(xv, xv, tmp, ALU.add))
            for t in range(TT):
                link(stt(A1[:, 0:1024], xs[:, t, :], 1.0, xs[:, t, :], ALU.mult, ALU.mult, accum_out=stat[:, 48 + t:49 + t]))
            link(ts(stat[:, 50:52], stat[:, 48:50], 1.0 / D, EPS, ALU.mult, ALU.add))
            link(v.reciprocal(stat[:, 50:52], stat[:, 50:52]))
            done("square")
            v.wait_ge(sem("rsqrt"), 7)
            for t in range(TT):
                link(ts(xn2[:, t, :], xs[:, t, :], stat[:, 50 + t:51 + t], None, ALU.mult))
            done("xn2")
            v.wait_ge(sem("x2_turned"), 1)
            for k in range(KD):
                link(ts(hT[:, k, :], ps[:, k // 2, (k % 2) * T:(k % 2 + 1) * T], G2[:, k:k + 1], S2[:, k:k + 1], ALU.mult, ALU.add))
            done("h2T")
            done("x2_read")
            v.wait_ge(sem("logits"), 1)
            v.wait_ge(sem("pool_masks"), 2)
            for t in range(TT):
                link(tt(lg[:, t, :], ps[:, 4, t * NE:(t + 1) * NE], rb[:, :], ALU.add))
                link(v.max(top[:, t, :], lg[:, t, :]))
                link(v.max_index(topi[:, t, :].bitcast(U32), top[:, t, :], lg[:, t, :]))
                link(ts(stat[:, 60 + t:61 + t], top[:, t, 0:1], -1.0, None, ALU.mult))
                done("top4")
            for t in range(TT):
                link(v.tensor_copy(topi[:, t, :], topi[:, t, :].bitcast(U32)))
                v.wait_ge(sem("top_exp"), t + 1)
                link(v.reciprocal(stat[:, 62 + t:63 + t], stat[:, 62 + t:63 + t]))
                link(ts(topw[:, t, 0:TOPK], topw[:, t, 0:TOPK], stat[:, 62 + t:63 + t], None, ALU.mult))
                for j in range(TOPK):
                    if j == 0:
                        link(ts(msk[:, t, :], iotaE, topi[:, t, 0:1], None, ALU.is_equal))
                        link(ts(wts[:, t, :], iotaE, topi[:, t, 0:1], topw[:, t, 0:1], ALU.is_equal, ALU.mult))
                    else:
                        link(ts(tmpe[:, t, :], iotaE, topi[:, t, j:j + 1], None, ALU.is_equal))
                        link(tt(msk[:, t, :], msk[:, t, :], tmpe[:, t, :], ALU.add))
                        link(stt(wts[:, t, :], tmpe[:, t, :], topw[:, t, j:j + 1], wts[:, t, :], ALU.mult, ALU.add))
            done("mask")
            v.wait_ge(sem("places"), 1)
            pp = ps[:, 5, 0:2 * NE].rearrange("p (t e) -> p t e", t=TT)
            link(ts(tmpe, msk, -4096.0, 4096.0, ALU.mult, ALU.add))
            link(tt(pos, pp, tmpe, ALU.add))
            link(v.tensor_copy(cnt, ps[:, 5, 2 * NE:3 * NE]))
            done("pos")
            link(ts(xneed, cnt, float(CAP), None, ALU.is_gt))
            for m in range(2, MORE + 1):
                link(stt(xneed, cnt, float(CAP * m), xneed, ALU.is_gt, ALU.add))
            link(v.memset(ohx, 1.0))
            link(v.tensor_tensor_scan(xend, ohx, xneed, 0.0, ALU.mult, ALU.add))
            link(ts(ohy, xend, rcol[:, 0:1], None, ALU.is_le))
            link(v.tensor_reduce(xcol[:, 0:1], ohy, AX.X, ALU.add))
            link(ts(ohx, iotaE, xcol[:, 0:1], None, ALU.is_equal))
            link(tt(ohy, xneed, ohy, ALU.mult))
            link(v.tensor_reduce(xcol[:, 1:2], ohy, AX.X, ALU.add))
            link(tt(xcol[:, 1:2], rcol[:, 0:1], xcol[:, 1:2], ALU.subtract))
            link(ts(xcol[:, 1:2], xcol[:, 1:2], 1.0, float(CAP), ALU.add, ALU.mult))
            link(ts(xcol[:, 0:1], xcol[:, 0:1], float(NE - 1), None, ALU.min))
            link(v.memset(xcol[:, 2:8], 0.0))
            done("ohx")
            v.wait_ge(sem("routes_turned"), 1)
            link(v.tensor_copy(wT, ps[0:NE, 6, 0:T]))
            link(v.tensor_copy(posT, ps[0:NE, 7, 0:T]))
            done("wT")
            v.wait_ge(sem("xcols"), 1)
            link(v.tensor_copy(ohT[:, 0:XP], ps[0:NE, 4, 0:XP]))
            link(v.tensor_copy(xe_i[:, 0:XP], ps[0:1, 4, P:P + XP]))
            link(v.tensor_copy(chk[0:8, 0:XP], ps[0:8, 4, P:P + XP]))
            link(ts(rcol[:, 1:2], rcol[:, 0:1], 1.0, None, ALU.is_equal))
            link(ts(pick1, ones[0:8, :], rcol[0:8, 1:2], None, ALU.mult))
            link(v.tensor_copy(xn_i, xend[0:1, NE - 1:NE]))
            done("xtab")
            for j in range(3):
                link(v.tensor_copy(oh96[32 * j:32 * j + 32, 0:NE], ident[32 * j:32 * j + 32, 32 * j:32 * j + 32]))
                link(v.tensor_copy(oh96[32 * j:32 * j + 32, NE:NE + XP], ps[0:NE, 4, 0:XP]))
            done("ohT")
            v.wait_ge(sem("xmats"), 1)
            for t in range(TT):
                link(v.tensor_copy(posP[:, t, 0:NE], pos[:, t, :]))
                link(v.tensor_copy(wP[:, t, 0:NE], wts[:, t, :]))
                link(v.tensor_copy(posP[:, t, NE:NE + XP], ps[:, 4, 256 + t * 32:256 + t * 32 + XP]))
                link(tt(posP[:, t, NE:NE + XP], posP[:, t, NE:NE + XP], ps[:, 4, 384:384 + XP], ALU.subtract))
                link(v.tensor_copy(wP[:, t, NE:NE + XP], ps[:, 4, 320 + t * 32:320 + t * 32 + XP]))

            def select(q):
                for t in range(TT):
                    i = ts(sel[:, t, :], iota[:, 0:CAP], posP[:, t, bass.ds(q, 1)], None, ALU.is_equal)
                i.then_inc(sem("sel"), 1)

            def select_w(q):
                for t in range(TT):
                    i = ts(selw[:, t, :], iota, posP[:, t, bass.ds(q, 1)], wP[:, t, bass.ds(q, 1)], ALU.is_equal, ALU.mult)
                i.then_inc(sem("selw"), 1)

            def expert_rows(q):
                v.wait_ge(sem("rows"), q + 1)
                g = Gps.rearrange("p (k c) -> p k c", k=KD)
                v.tensor_tensor(xT, g, G2[:, :].unsqueeze(2).to_broadcast((P, KD, CAP)), ALU.mult).then_inc(sem("xT_half"), 1)
                v.tensor_copy(ohp, oh96[:, bass.ds(q, 1)].to_broadcast((96, CAP))).then_inc(sem("ohp"), 1)
                v.wait_ge(sem("xT_half"), q + 1)
                v.tensor_tensor(xT, xT, S2[:, :].unsqueeze(2).to_broadcast((P, KD, CAP)), ALU.add).then_inc(sem("xT"), 1)

            def swiglu(q):
                v.wait_ge(sem("w1_used"), (q + 1) * KD)
                hv = Hps.rearrange("p (f two) -> p two f", two=2)
                ts(glu, hv[:, 0, :], LIMIT, None, ALU.min).then_inc(sem("glu"), 1)
                ts(lin, hv[:, 1, :], LIMIT, -LIMIT, ALU.min, ALU.max).then_inc(sem("lin"), 1)
                v.wait_ge(sem("lin"), q + 1)
                stt(lin, lin, 1.0, glu, ALU.add, ALU.mult).then_inc(sem("lin2"), 1)
                v.wait_ge(sem("lin2"), q + 1)
                v.wait_ge(sem("sig"), q + 1)
                tt(act, lin, sig, ALU.mult).then_inc(sem("act"), 1)

            done("tables")
            select(0)
            expert_rows(0)
            select(1)
            v.wait_ge(sem("w1_used"), KD)
            select_w(0)
            swiglu(0)
            expert_rows(1)
            with v.Fori(1, NE - 1) as q:
                v.wait_ge(sem("rows"), q + 1)
                select(q + 1)
                v.wait_ge(sem("act_turned"), q)
                select_w(q)
                swiglu(q)
                expert_rows(q + 1)
            v.wait_ge(sem("act_turned"), NE - 1)
            select_w(NE - 1)
            swiglu(NE - 1)
            more = v.value_load(xn_i, min_val=0, max_val=XP)
            with v.Fori(0, XP) as i:
                with v.If(more > i):
                    v.wait_ge(sem("act_turned"), i + NE)
                    select(i + NE)
                    expert_rows(i + NE)
                    select_w(i + NE)
                    swiglu(i + NE)
            v.wait_ge(sem("scattered"), more + NE)
            for t in range(TT):
                for h in range(2):
                    tmp = A1[:, t * 1024 + h * 512:t * 1024 + (h + 1) * 512]
                    link(tt(tmp, ps[:, 2 * t + h, :], gate2[:, h * 512:(h + 1) * 512], ALU.mult))
                    link(tt(xs[:, t, h * 512:(h + 1) * 512], xs[:, t, h * 512:(h + 1) * 512], tmp, ALU.add))
                done("out_ready")


_INS = ["x", "c", "positions", "ada_w", "ada_b", "norm1_g", "w_in", "q_norm_g", "k_norm_g",
        "cmp_pe_k", "cmp_pe_v", "cmp_wk1", "cmp_wk2", "cmp_wv1", "cmp_wv2",
        "conv_w", "conv_b", "lru_wa", "lru_ba", "lru_wx", "lru_bx", "lru_lambda",
        "w_branch_out", "w_out", "norm2_g", "router_w", "router_b", "moe_w1", "moe_b1", "moe_w2", "moe_b2"]


def kernel(**inputs):
    import concourse.bacc as bacc
    from concourse.bass_utils import run_bass_kernel_spmd

    nc = bacc.Bacc("TRN2", target_bir_lowering=False, num_devices=1)
    inv = (10000.0 ** (-np.arange(0, DH, 2, dtype=np.float64) / DH)).astype(np.float32)[None, :]
    arrays, args = {}, {}
    for name in _INS + ["inv_freq"]:
        arr = np.ascontiguousarray(inputs[name]) if name in inputs else inv
        arrays[f"in_{name}"] = arr
        args[name] = nc.dram_tensor(f"in_{name}", arr.shape, mybir.dt.from_np(arr.dtype), kind="ExternalInput").ap()
    args["out"] = nc.dram_tensor("out_x", (1, T, D), F32, kind="ExternalOutput").ap()
    build_program(nc, **args)
    r = run_bass_kernel_spmd(nc, [arrays], core_ids=[0])
    return r.results[0]["out_x"]
```

```python
from contextlib import ExitStack

import numpy as np

import concourse.bass as bass
from concourse import mybir

ALU = mybir.AluOpType
ACT = mybir.ActivationFunctionType
AX = mybir.AxisListType
F32 = mybir.dt.float32
BF16 = mybir.dt.bfloat16
I32 = mybir.dt.int32
U32 = mybir.dt.uint32

P = 128
D = 1024
T = 256
TT = T // P
KD = D // P
NH, DH, NG, HPG = 8, 128, 2, 4
CMP_BLOCK, CMP_STRIDE = 32, 16
N_CMP = (T - CMP_BLOCK) // CMP_STRIDE + 1
CMP_HIDDEN = 256
LRU_C = 8.0
NE = 32
TOPK = 4
FF = 1024
CAP = 64
MORE = T // CAP - 1
XP = (T * TOPK - 1) // CAP
NPASS = NE + XP
LIMIT, ALPHA = 7.0, 1.702
EPS = 1e-6
NEG = -1e30
SCALE = float(DH) ** -0.5

Q_OFF = 0
KCMP_OFF = NH * DH
KSLC_OFF = KCMP_OFF + 2 * NG * DH
KWIN_OFF = KSLC_OFF + 2 * NG * DH
NSAG_OFF = KWIN_OFF + 2 * NG * DH
N_NSAG = NH * 3
LRUX_OFF = NSAG_OFF + N_NSAG
LRUG_OFF = LRUX_OFF + D
MERGE_OFF = LRUG_OFF + D

R_N1, R_CONVW, R_CONVB, R_BA, R_BX, R_LAM, R_N2, R_ADAB = 0, 8, 40, 48, 56, 64, 72, 80
M_SHIFT1, M_SCALE1, M_GATE1, M_SHIFT2, M_SCALE2, M_GATE2 = 0, 8, 16, 24, 32, 40

UNITS = [(g, t, b) for g in range(NG) for t in range(TT) for b in range(3)]

JOBS_A = [(("kslc",), 2), (("kwin",), 2), (("q", 0), 2), (("q", 1), 2), (("kcmp",), 4), (("lrux", 0), 4)]
JOBS_B = [(("r", 0), 1), (("i", 0), 1), (("lrug", 0), 4), (("lrug", 1), 4), (("lrux", 1), 4), (("merge", 0), 4),
          (("r", 1), 1), (("i", 1), 1), (("merge", 1), 4), (("merge", 2), 4), (("merge", 3), 4), (("ylru", 0), 4), (("ylru", 1), 4)]
JOBS = [j for j, _ in JOBS_A + JOBS_B]
JOB = {j: n for n, j in enumerate(JOBS)}
EARLY, PER = 4, 3
PIECES = [(j, p, p == n - 1) for j, n in JOBS_B for p in range(n)]
assert len(PIECES) == EARLY + PER * len(UNITS)
LRU_AT = {0: (0, 1), 1: (0, 2), 2: (0, 3), 4: (1, 0), 6: (1, 1), 7: (1, 2), 8: (1, 3)}
ADA_AT = {0: (1, 0), 1: (1, 1), 2: (1, 2), 3: (1, 3), 5: (2, 0), 6: (2, 1), 7: (2, 2), 8: (2, 3)}


def pieces_of(m):
    return PIECES[:EARLY] if m < 0 else PIECES[EARLY + PER * m:EARLY + PER * (m + 1)]


def weights_of(job):
    return {"r": ("lrugate",), "i": ("lrugate",), "ylru": ("bo", 1)}.get(job[0], job[:1]) + job[1:]


EVEN_BANKS = [k for k in range(KD) if k // 2 % 2 == 0]
ODD_BANKS = [k for k in range(KD) if k // 2 % 2 == 1]


def bank_side(k):
    odd = k // 2 % 2
    return ("_even", "_odd")[odd], (ODD_BANKS if odd else EVEN_BANKS).index(k) + 1


STREAM = [("ada", 0, k) for k in range(4)] + [("kslc",), ("kwin",), ("q", 0), ("q", 1), ("kcmp",), ("lrux", 0)] + [("cmp", k) for k in range(4)]
for _m in range(-1, len(UNITS)):
    for _j, _p, _ in pieces_of(_m):
        if _p == 0 and _j[0] != "i":
            STREAM.append(weights_of(_j))
    if _m in ADA_AT:
        STREAM.append(("ada",) + ADA_AT[_m])
STREAM += [("bo", 0, 0), ("bo", 0, 1), ("wo", 0), ("wo", 1)]
SLOT = {u: n for n, u in enumerate(STREAM)}
NSLOT = 4


def read_by(u):
    if u[0] == "lrugate":
        return "job_full", JOB[("i", u[1])] + 1
    if u[:2] == ("bo", 1):
        return "job_full", JOB[("ylru", u[2])] + 1
    if u in JOB:
        return "job_full", JOB[u] + 1
    if u[0] == "ada":
        return "ada_used", 4 * u[1] + u[2] + 1
    if u[0] == "cmp":
        return "cmp_used", u[1] + 1
    return "branch", u[2] + 1


def build_program(nc, x, c, positions, ada_w, ada_b, norm1_g, w_in, q_norm_g, k_norm_g,
                  cmp_pe_k, cmp_pe_v, cmp_wk1, cmp_wk2, cmp_wv1, cmp_wv2,
                  conv_w, conv_b, lru_wa, lru_ba, lru_wx, lru_bx, lru_lambda,
                  w_branch_out, w_out, norm2_g, router_w, router_b,
                  moe_w1, moe_b1, moe_w2, moe_b2, inv_freq, out):
    with ExitStack() as ctx:
        made = {}

        def sem(name):
            if name not in made:
                made[name] = ctx.enter_context(nc.semaphore(name))
            return made[name]

        def sb(name, shape, dt=F32):
            return ctx.enter_context(nc.sbuf_tensor(name, shape, dt))

        W1 = sb("W1", [P, KD * 2 * FF])
        W2 = sb("W2", [P, KD * D])
        ST = sb("ST", [P, NSLOT * 4096])
        xs = sb("xs", [P, TT, D])
        A1 = sb("A1", [P, KD * T])
        A2 = sb("A2", [P, KD * T])
        gate1 = sb("gate1", [P, D])
        gate2 = sb("gate2", [P, D])
        vtm = sb("vtm", [P, 2, TT, NG * DH])
        b1s = sb("b1s", [96, 2 * FF], BF16)
        ident = sb("ident", [P, P])
        pcol = sb("pcol", [P, P])
        peT = sb("peT", [P, 2 * CMP_BLOCK])
        causal = sb("causal", [P, P])
        cneg = sb("cneg", [P, TT, 16])
        gw = sb("gw", [P, KD, N_NSAG])
        rw = sb("rw", [P, KD, NE])
        rb = sb("rb", [P, NE])
        ng = sb("ng", [P, TT, N_NSAG])
        cs32 = sb("cs32", [P, KD, 32])
        ccol = sb("ccol", [P, 2 * KD])
        G1 = sb("G1", [P, KD])
        S1 = sb("S1", [P, KD])
        G2 = sb("G2", [P, KD])
        S2 = sb("S2", [P, KD])
        m3 = sb("m3", [P, 16])
        spl = sb("spl", [P, 4, KD])
        stat = sb("stat", [P, 96])
        pos_i = sb("pos_i", [P, TT], I32)
        pos_f = sb("pos_f", [P, TT])

        def cut(t, a, *shape):
            n = int(np.prod(shape))
            v = t[:, a:a + n]
            if len(shape) == 2:
                v = v.rearrange("p (a b) -> p a b", a=shape[0])
            if len(shape) == 3:
                v = v.rearrange("p (a b c) -> p a b c", a=shape[0], b=shape[1])
            return v

        hT = cut(A1, 0, KD, T)
        QK = cut(W1, 0, TT, 12, DH)
        QR = cut(W1, 3072, TT, 12, DH)
        xn = cut(W1, 3072, TT, D)
        praw = W1[:, 5120:5248]
        peraw = W1[0:2 * CMP_BLOCK, 5248:5376]
        modrow = W1[:, 5376:5888]
        Sb = cut(W1, 0, 2, HPG * T)
        PT = cut(W1, 2048, 2, HPG * P)
        Pc = cut(W1, 3072, HPG, 64)
        pickt = cut(W1, 3328, 4, P)
        mod2 = cut(W1, 3840, 2, 512)
        qT = cut(W1, 6144, NH, T)
        rtmp = cut(W1, 6144, TT, 12, DH // 2)
        qrT = cut(W1, 8192, NH, T)
        LV = cut(W1, 8192, CMP_BLOCK, 64)
        LK = cut(A2, 0, CMP_BLOCK, 64)
        kT = cut(W1, 10240, 4, T)
        kcT = cut(W1, 10240, 4, T)
        uu = W1[:, 11264:11520]
        uT = cut(W1, 11520, 2, P)
        kcn = W1[0:64, 11776:11904]
        vcs = W1[0:64, 11904:12032]
        kccT = W1[:, 12032:12096]
        ksq = W1[0:64, 12096:12224]
        w2c = cut(W1, 12224, 4, DH)
        gain = cut(W1, 12736, 4, DH)
        cosT = cut(W1, 13248, TT, DH // 2)
        sinT = cut(W1, 13376, TT, DH // 2)
        ang = cut(W1, 13504, TT, DH // 2)
        KH = KD // 2
        lx = cut(W1, 13632, KH, T + 3)
        lt = cut(W1, 13632, KH, T)
        xc = cut(W1, 13632 + KH * (T + 3), KH, T)
        rr = cut(A2, 0, KH, T)
        ii = cut(A2, KH * T, KH, T)
        mg = cut(W2, 0, 2 * KD, T)
        oT = cut(W2, 4096, NH, T)
        olT = cut(W2, 6144, KD, T)
        mergedT = cut(W2, 0, KD, T)
        xn2 = cut(A2, 0, TT, D)

        def slot(u):
            n = (SLOT[u] - SLOT[("wo", 0)] + 2) % NSLOT
            return ST[:, n * 4096:(n + 1) * 4096]

        mb = [0]

        def mine(n):
            mb[0] += n
            return mb[0] - n

        o = mine(512); xT = cut(ST, o, KD, CAP)
        o = mine(512); actT = cut(ST, o, 4, P)
        o = mine(512); ysb = ST[:, o:o + 512]
        o = mine(TT * CAP); sel = cut(ST, o, TT, CAP)
        o = mine(TT * P); selw = cut(ST, o, TT, P)
        o = mine(TT * P); selT = cut(ST, o, TT, P)
        o = mine(32); ohp = ST[0:96, o:o + 32].bitcast(BF16)
        o = mine(128); iota = ST[:, o:o + 128]
        o = mine(TT * 48); posP = cut(ST, o, TT, 48)
        o = mine(TT * 48); wP = cut(ST, o, TT, 48)
        o = mine(48); oh96 = ST[0:96, o:o + 48]
        o = mine(TT * NE); lg = cut(ST, o, TT, NE)
        o = mine(TT * NE); msk = cut(ST, o, TT, NE)
        o = mine(TT * NE); wts = cut(ST, o, TT, NE)
        o = mine(TT * NE); pos = cut(ST, o, TT, NE)
        o = mine(TT * NE); tmpe = cut(ST, o, TT, NE)
        o = mine(TT * 8); top = cut(ST, o, TT, 8)
        o = mine(TT * 8); topi = cut(ST, o, TT, 8)
        o = mine(TT * 8); topw = cut(ST, o, TT, 8)
        o = mine(8); rs = ST[:, o:o + 8]
        o = mine(NE); iotaE = ST[:, o:o + NE]
        o = mine(P); upper = ST[:, o:o + P]
        o = mine(P); ones = ST[:, o:o + P]
        o = mine(T); wT = ST[0:NE, o:o + T]
        o = mine(T); posT = ST[0:NE, o:o + T]
        o = mine(16); iota16 = ST[:, o:o + 16]
        o = mine(NE); cnt = ST[:, o:o + NE]
        o = mine(NE); xneed = ST[:, o:o + NE]
        o = mine(NE); xend = ST[:, o:o + NE]
        o = mine(NE); ohx = ST[:, o:o + NE]
        o = mine(NE); ohy = ST[:, o:o + NE]
        o = mine(8); xcol = ST[:, o:o + 8]
        o = mine(64); ohT = ST[0:NE, o:o + 64]
        o = mine(P); pick1 = ST[0:8, o:o + P]
        o = mine(16); xe_i = ST[0:1, o:o + 16].bitcast(I32)
        o = mine(2); xn_i = ST[0:1, o:o + 1].bitcast(I32)
        o = mine(D); b2s = ST[0:NE, o:o + D]
        o = mine(16); chk = ST[:, o:o + 16]
        o = mine(2); rcol = ST[:, o:o + 2]
        o = mine(TT * NE * TOPK); eq4 = cut(ST, o, TT, NE, TOPK)
        o = mine(TT * NE * TOPK); eq4w = cut(ST, o, TT, NE, TOPK)
        assert 2 * TT * NE * TOPK >= 512
        xg = ST[:, mb[0] - 2 * TT * NE * TOPK:mb[0]]
        assert mb[0] <= 2 * 4096
        ahead = [ST[:, 2 * 4096 + k * 2048:2 * 4096 + (k + 1) * 2048] for k in range(4)]
        w2_ahead = [a.rearrange("p (k n) -> p k n", k=2) for a in ahead]
        if 2 * 4096 - mb[0] >= 2 * FF:
            ahead.append(ST[:, 2 * 4096 - 2 * FF:2 * 4096])
        x1tmp = cut(A1, 0, TT, D)
        glu = A1[:, 0:512]
        lin = A1[:, 512:1024]
        sig = A1[:, 1024:1536]
        act = A1[:, 1536:2048]
        w1v = cut(W1, 0, KD, 2 * FF)
        w2v = cut(W2, 0, KD, D)

        ps = ctx.enter_context(nc.psum_tensor("ps", [P, 8, 512], F32))
        PAIR = [ps[:, 0:2, :].rearrange("p a b -> p (a b)"), ps[:, 2:4, :].rearrange("p a b -> p (a b)")]
        Hps = ps[:, 4:6, :].rearrange("p a b -> p (a b)")
        Yps = ps[:, 6, :]
        Gps = ps[:, 7, :]

        block = ctx.enter_context(nc.Block())

        def wk(w, k0, nk, c0, nc_):
            return w[k0 * P:(k0 + nk) * P, c0:c0 + nc_].rearrange("(k p) n -> p k n", p=P)

        @block.sync
        def _(sp):
            IN_COL = {"lrux": LRUX_OFF, "lrug": LRUG_OFF, "merge": MERGE_OFF, "q": Q_OFF}
            ONE_COL = {"kcmp": KCMP_OFF, "kslc": KSLC_OFF, "kwin": KWIN_OFF}
            for n, u in enumerate(STREAM):
                if n >= NSLOT:
                    name, value = read_by(STREAM[n - NSLOT])
                    sp.wait_ge(sem(name), value)
                full = sem(f"stream_full{n % NSLOT}")
                dst = slot(u)
                if u[0] == "ada":
                    sp.dma_start(dst.rearrange("p (k n) -> p k n", k=2), wk(ada_w[0], 2 * u[2], 2, 2048 * u[1], 2048)).then_inc(full, 16)
                elif u[0] in IN_COL:
                    sp.dma_start(dst.rearrange("p (k n) -> p k n", k=KD), wk(w_in[0], 0, KD, IN_COL[u[0]] + 512 * u[1], 512)).then_inc(full, 16)
                elif u[0] in ONE_COL:
                    sp.dma_start(dst.rearrange("p (k n) -> p k n", k=KD), wk(w_in[0], 0, KD, ONE_COL[u[0]], 512)).then_inc(full, 16)
                elif u[0] == "lrugate":
                    for half, w in enumerate((lru_wa, lru_wx)):
                        sp.dma_start(dst[:, 1024 * half:1024 * (half + 1)].rearrange("p (a j) -> p a j", a=4),
                                     w[0, 2 * u[1]:2 * u[1] + 2].rearrange("h (i p) j -> p (h i) j", p=P)).then_inc(full, 16)
                elif u[0] == "cmp":
                    for half, w in enumerate((cmp_wk1, cmp_wv1)):
                        sp.dma_start(dst[:, 2048 * half:2048 * (half + 1)].rearrange("p (k n) -> p k n", k=8),
                                     wk(w[0], 8 * u[1], 8, 0, CMP_HIDDEN)).then_inc(full, 16)
                elif u[0] == "bo":
                    sp.dma_start(dst.rearrange("p (k n) -> p k n", k=KD), wk(w_branch_out[0], KD * u[1], KD, 512 * u[2], 512)).then_inc(full, 16)
                elif u[0] == "wo":
                    sp.dma_start(dst.rearrange("p (k n) -> p k n", k=KD), wk(w_out[0], 0, KD, 512 * u[1], 512)).then_inc(full, 16)

            def load_w1(e, passes):
                for k in range(KD):
                    if passes is not None:
                        sp.wait_ge(sem("w1_used"), 8 * passes - (KD - 1 - k))
                    sp.dma_start(w1v[:, k, :], moe_w1[0, e, k * P:(k + 1) * P, :] if isinstance(e, int)
                                 else moe_w1[0, bass.ds(e, 1), k * P:(k + 1) * P, :].rearrange("a p n -> p (a n)")).then_inc(sem(f"w1_full{k}"), 16)

            def load_w2(e, passes):
                for s in range(4):
                    if passes is not None:
                        sp.wait_ge(sem("w2_used"), 4 * passes - (3 - s))
                    src = moe_w2[0, e] if isinstance(e, int) else moe_w2[0, bass.ds(e, 1)].rearrange("a f n -> (a f) n")
                    sp.dma_start(w2v[:, 2 * s:2 * s + 2, :], wk(src, 2 * s, 2, 0, D)).then_inc(sem(f"w2_full{s}"), 16)

            sp.wait_ge(sem("att_read"), len(UNITS))
            sp.wait_ge(sem("oT_full"), NG * TT)
            sp.wait_ge(sem("gate_read"), 4)
            load_w1(0, None)
            sp.wait_ge(sem("merged"), 2)
            for s in (1, 2, 3):
                sp.dma_start(w2v[:, 2 * s:2 * s + 2, :], wk(moe_w2[0, 0], 2 * s, 2, 0, D)).then_inc(sem(f"w2_full{s}"), 16)
            sp.wait_ge(sem("wo_full"), 2 * TT)
            sp.dma_start(w2v[:, 0:2, :], wk(moe_w2[0, 0], 0, 2, 0, D)).then_inc(sem("w2_full0"), 16)
            for k, dst in enumerate(ahead):
                sp.dma_start(dst, moe_w1[0, 1, k * P:(k + 1) * P, :]).then_inc(sem(f"w1_early{k}"), 16)
            for k in range(len(ahead)):
                sp.wait_ge(sem("w1_used"), k + 1)
                sp.dma_start(w1v[:, k, :], moe_w1[0, 2, k * P:(k + 1) * P, :]).then_inc(sem(f"w1_full{k}"), 16)
            for k in range(len(ahead), KD):
                sp.wait_ge(sem("w1_used"), k + 1)
                sp.dma_start(w1v[:, k, :], moe_w1[0, 1, k * P:(k + 1) * P, :]).then_inc(sem(f"w1_full{k}"), 16)
            for s in range(4):
                sp.wait_ge(sem("w1_used"), KD + s + 1)
                sp.dma_start(w2_ahead[s], wk(moe_w2[0, 1], 2 * s, 2, 0, D)).then_inc(sem(f"w2_early{s}"), 16)
            for k in range(len(ahead), KD):
                sp.wait_ge(sem("w1_used"), KD + k + 1)
                sp.dma_start(w1v[:, k, :], moe_w1[0, 2, k * P:(k + 1) * P, :]).then_inc(sem(f"w1_full{k}"), 16)
            load_w2(2, 1)
            load_w1(3, 3)
            with sp.Fori(4, NE) as q:
                load_w1(q, q)
                load_w2(q - 1, q - 1)
            load_w2(NE - 1, NE - 1)
            sp.wait_ge(sem("xtab"), 1)
            more = sp.value_load(xn_i, min_val=0, max_val=XP)
            with sp.Fori(0, XP) as i:
                with sp.If(more > i):
                    e = sp.value_load(xe_i[0:1, bass.ds(i, 1)], min_val=0, max_val=NE - 1)
                    load_w1(e, i + NE)
                    load_w2(e, i + NE)
            for t in range(TT):
                for h in range(2):
                    sp.wait_ge(sem("out_ready"), 2 * t + h + 1)
                    sp.dma_start(out[0, t * P:(t + 1) * P, 512 * h:512 * (h + 1)], xs[:, t, 512 * h:512 * (h + 1)]).then_inc(sem("out_stored"), 16)
            sp.wait_ge(sem("out_stored"), 16 * 2 * TT)

        @block.gpsimd
        def _(pool):
            chain = [0]

            def link(i):
                chain[0] += 1
                i.then_inc(sem("pool_chain"), 1)
                pool.wait_ge(sem("pool_chain"), chain[0])

            pool.dma_start(peraw[0:CMP_BLOCK, :], cmp_pe_k[0]).then_inc(sem("pe_in"), 16)
            pool.dma_start(peraw[CMP_BLOCK:2 * CMP_BLOCK, :], cmp_pe_v[0]).then_inc(sem("pe_in"), 16)
            link(pool.memset(ident[:, :], 0.0))
            pool.affine_select(out=ident[:, :], in_=ident[:, :], compare_op=ALU.not_equal, fill=1.0, base=0,
                               pattern=[[-1, P]], channel_multiplier=1).then_inc(sem("ident"), 1)
            pool.wait_ge(sem("ada_used"), 3)
            for j in range(3):
                pool.dma_start(A2[32 * j:32 * j + 32, :], moe_b1[0]).then_inc(sem("b1_in"), 16)
            pool.dma_start(gw[:, :, :], wk(w_in[0], 0, KD, NSAG_OFF, N_NSAG)).then_inc(sem("small_in"), 16)
            pool.dma_start(rw[:, :, :], wk(router_w[0], 0, KD, 0, NE)).then_inc(sem("small_in"), 16)
            pool.dma_start(rb[:, :], router_b.to_broadcast((P, NE))).then_inc(sem("small_in"), 16)
            pool.dma_start(gate1[:, :], ada_b[:, M_GATE1 * P:(M_GATE1 + 8) * P].to_broadcast((P, D))).then_inc(sem("small_in"), 16)
            pool.dma_start(gate2[:, :], ada_b[:, M_GATE2 * P:(M_GATE2 + 8) * P].to_broadcast((P, D))).then_inc(sem("small_in"), 16)
            pool.dma_start(gain[:, 0, :], q_norm_g.to_broadcast((P, DH))).then_inc(sem("small_in"), 16)
            for j in range(3):
                pool.dma_start(gain[:, 1 + j, :], k_norm_g[0, j:j + 1, :].to_broadcast((P, DH))).then_inc(sem("small_in"), 16)
            pool.dma_start(ang[:, 0, :], inv_freq.to_broadcast((P, DH // 2))).then_inc(sem("small_in"), 16)
            pool.dma_start(ang[:, 1, :], inv_freq.to_broadcast((P, DH // 2))).then_inc(sem("small_in"), 16)
            pool.dma_start(pos_i[:, :], positions[0].rearrange("(t p) -> p t", p=P), allow_slow_non_contiguous=True).then_inc(sem("small_in"), 16)
            for w, m in enumerate((cmp_wk2, cmp_wv2)):
                pool.dma_start(w2c[:, 2 * w:2 * w + 2, :], wk(m[0], 0, 2, 0, DH)).then_inc(sem("w2c_in"), 16)
            link(pool.memset(causal[:, :], 0.0))
            link(pool.memset(cneg[:, :, :], 0.0))
            link(pool.affine_select(out=causal[:, :], in_=causal[:, :], compare_op=ALU.is_ge, fill=NEG, base=0,
                                    pattern=[[-1, P]], channel_multiplier=1))
            link(pool.affine_select(out=cneg[:, :, :], in_=cneg[:, :, :], compare_op=ALU.is_ge, fill=NEG, base=1 - CMP_BLOCK,
                                    pattern=[[P, TT], [-CMP_STRIDE, 16]], channel_multiplier=1))
            pool.wait_ge(sem("b1_in"), 48)
            link(pool.tensor_copy(b1s[:, :], A2[0:96, :]))
            link(pool.tensor_tensor(A2[0:96, :], A2[0:96, :], b1s[:, :], ALU.subtract))
            link(pool.tensor_copy(b1s[32:64, :], A2[32:64, :]))
            link(pool.tensor_copy(b1s[64:96, :], A2[64:96, :]))
            link(pool.tensor_tensor(A2[64:96, :], A2[64:96, :], b1s[64:96, :], ALU.subtract))
            link(pool.tensor_copy(b1s[64:96, :], A2[64:96, :]))
            link(pool.memset(LK, 0.0))
            pool.nop().then_inc(sem("pool_masks"), 1)

            pool.wait_ge(sem("branch"), 2)
            pool.dma_start(b2s, moe_b2[0]).then_inc(sem("b2_in"), 16)
            for h in range(2):
                link(pool.iota(iota[:, CAP * h:CAP * (h + 1)], [[1, CAP]], base=0, channel_multiplier=0, allow_small_or_imprecise_dtypes=True))
            link(pool.iota(iotaE, [[1, NE]], base=0, channel_multiplier=0, allow_small_or_imprecise_dtypes=True))
            link(pool.iota(iota16, [[1, 16]], base=0, channel_multiplier=0, allow_small_or_imprecise_dtypes=True))
            link(pool.iota(rcol[:, 0:1], [[0, 1]], base=0, channel_multiplier=1, allow_small_or_imprecise_dtypes=True))
            link(pool.memset(ones, 1.0))
            link(pool.memset(oh96, 0.0))
            link(pool.memset(ohT, 0.0))
            link(pool.memset(upper, 1.0))
            link(pool.affine_select(out=upper, in_=upper, compare_op=ALU.is_gt, fill=0.0, base=0,
                                    pattern=[[1, P]], channel_multiplier=-1))
            pool.nop().then_inc(sem("pool_masks"), 1)

        @block.scalar
        def _(act_e):
            a = act_e
            n = [0]

            def link(i):
                n[0] += 1
                i.then_inc(sem("act_chain"), 1)
                a.wait_ge(sem("act_chain"), n[0])

            def root(n, st):
                a.wait_ge(sem("square"), n)
                a.activation(st, st, ACT.Sqrt).then_inc(sem("rsqrt"), 1)

            a.dma_start(ccol[:, 0:KD], c[0].rearrange("(k p) -> p k", p=P), allow_slow_non_contiguous=True).then_inc(sem("c_in"), 16)
            for t in range(TT):
                a.dma_start(xs[:, t, :], x[0, t * P:(t + 1) * P, :]).then_inc(sem("x_in"), 16)
            for r0, v in ((R_N1, norm1_g), (R_CONVB, conv_b), (R_BA, lru_ba), (R_BX, lru_bx), (R_LAM, lru_lambda), (R_N2, norm2_g)):
                a.dma_start(praw[r0:r0 + 8, :], v[0].rearrange("(k p) -> k p", p=P)).then_inc(sem("params_in"), 16)
            a.dma_start(praw[R_CONVW:R_CONVW + 32, :], conv_w[0].rearrange("w (k p) -> (w k) p", p=P)).then_inc(sem("params_in"), 16)
            a.dma_start(praw[R_ADAB:R_ADAB + 48, :], ada_b[0].rearrange("(k p) -> k p", p=P)).then_inc(sem("params_in"), 16)
            a.wait_ge(sem("c_in"), 16)
            a.activation(ccol[:, KD:2 * KD], ccol[:, 0:KD], ACT.Sigmoid).then_inc(sem("sig_c"), 1)
            a.wait_ge(sem("x_in"), 32)
            for t in range(TT):
                link(a.activation(xn[:, t, :], xs[:, t, :], ACT.Square, accum_out=stat[:, t:t + 1]))
            a.nop().then_inc(sem("x_sq"), 1)
            root(1, stat[:, 2:4])

            def wait_job(j):
                a.wait_ge(sem("job_full"), JOB[j] + 1)
                return PAIR[JOB[j] % 2]

            a.wait_ge(sem("x_turned"), 1)
            a.wait_ge(sem("mod1"), 1)
            for k in ODD_BANKS:
                a.activation(hT[:, k, :], ps[:, k // 2, (k % 2) * T:(k % 2 + 1) * T], ACT.Identity, scale=G1[:, k:k + 1], bias=S1[:, k:k + 1]).then_inc(sem("hT_odd"), 1)
            a.wait_ge(sem("lam_abs"), 1)
            a.activation(spl[:, 0, :], spl[:, 0, :], ACT.Exp).then_inc(sem("lam_exp"), 1)
            def keys_values(j, b):
                p = wait_job(j).rearrange("p (t n) -> p t n", t=TT)
                link(a.activation(QK[:, :, 8 + 2 * b:10 + 2 * b, :], p[:, :, 0:256].rearrange("p t (g d) -> p t g d", g=2), ACT.Copy))
                a.activation(vtm[:, b, :, :], p[:, :, 256:512], ACT.Copy).then_inc(sem("job_read"), 1)

            def evacuate(job):
                name, h = job
                p = wait_job(job)
                p4 = p.rearrange("p (k t) -> p k t", k=4)
                if name == "lrux":
                    a.wait_ge(sem("lx_zero"), h + 1)
                    a.activation(lx[:, :, 3:3 + T], p4, ACT.Copy).then_inc(sem("job_read"), 1)
                elif name == "lrug":
                    a.activation(olT[:, 4 * h:4 * h + 4, :], p4, ACT.Gelu_apprx_tanh).then_inc(sem("job_read"), 1)
                elif name == "merge":
                    a.activation(mg[:, 4 * h:4 * h + 4, :], p4, ACT.Sigmoid).then_inc(sem("job_read"), 1)
                elif name in "ri":
                    dst, r0 = (rr, R_BA) if name == "r" else (ii, R_BX)
                    if h == 1:
                        a.wait_ge(sem("lru_done"), 1)
                    for k in range(4):
                        q = a.activation(dst[:, k, :], p[:, k * T:(k + 1) * T], ACT.Sigmoid, bias=pcol[:, r0 + 4 * h + k:r0 + 4 * h + k + 1])
                    q.then_inc(sem("job_read"), 1)

            keys_values(("kslc",), 0)
            a.wait_ge(sem("angles"), 1)
            a.activation(cosT, cosT, ACT.Sin).then_inc(sem("sincos"), 1)
            a.activation(sinT, sinT, ACT.Sin).then_inc(sem("sincos"), 1)
            keys_values(("kwin",), 1)
            root(2, stat[:, 64:68])
            root(3, stat[:, 64:68])
            for h in range(2):
                p = wait_job(("q", h)).rearrange("p (t g d) -> p t g d", t=TT, g=4)
                a.activation(QK[:, :, 4 * h:4 * h + 4, :], p, ACT.Copy).then_inc(sem("job_read"), 1)
                root(4 + h, stat[:, 64:72])
            p = wait_job(("kcmp",))
            a.activation(kcT, p.rearrange("p (k t) -> p k t", k=4), ACT.Copy).then_inc(sem("job_read"), 1)
            a.wait_ge(sem("ng_full"), 1)
            a.activation(ng[:, :, :], ps[:, 4, 0:TT * N_NSAG].rearrange("p (t n) -> p t n", t=TT), ACT.Sigmoid).then_inc(sem("ng_read"), 1)
            evacuate(("lrux", 0))
            a.wait_ge(sem("cmp_used"), 4)
            a.activation(uu, ps[:, 4, 0:CMP_HIDDEN], ACT.Gelu_apprx_tanh).then_inc(sem("cmp_gelu"), 1)
            for j in range(10):
                a.wait_ge(sem("qk_turned"), j + 1)
                dst = (qT[:, 2 * j:2 * j + 2, :] if j < 4 else qrT[:, 2 * j - 8:2 * j - 6, :] if j < 8 else kT[:, 2 * j - 16:2 * j - 14, :])
                a.activation(dst, ps[:, 4 + j % 2, :].rearrange("p (h t) -> p h t", h=2), ACT.Copy).then_inc(sem("qk_read"), 1)
            a.wait_ge(sem("uT_full"), 1)
            a.activation(uT, ps[:, 6, 0:256].rearrange("p (a b) -> p a b", a=2), ACT.Copy).then_inc(sem("uT_read"), 1)
            for job, _, last in pieces_of(-1):
                if last:
                    evacuate(job)
            root(6, stat[0:64, 80:81])

            def exps(m):
                g, t, b = UNITS[m]
                a.wait_ge(sem("att_max"), m + 1)
                nk = N_CMP if b == 0 else P * (t + 1)
                for h in range(HPG):
                    src = Sb[:, m % 2, h * T:h * T + nk]
                    dst = Pc[:, h, 32 * g:32 * g + N_CMP] if b == 0 else src
                    i = a.activation(dst, src, ACT.Exp, scale=SCALE, bias=stat[:, 16 + 8 * (m % 2) + h:17 + 8 * (m % 2) + h],
                                     accum_out=stat[:, 32 + 8 * (m % 2) + h:33 + 8 * (m % 2) + h])
                i.then_inc(sem("att_exp"), 1)

            def turned(m):
                g, t, b = UNITS[m]
                a.wait_ge(sem("att_turned"), m + 1)
                if m >= 1:
                    a.wait_ge(sem("att_read"), m)
                if b == 0:
                    a.activation(PT[0:64, 0, :], ps[0:64, 4, :], ACT.Copy).then_inc(sem("att_pT"), 1)
                else:
                    a.activation(PT[:, 0:t + 1, :], ps[:, 4:5 + t, :], ACT.Copy).then_inc(sem("att_pT"), 1)

            def head_out(m):
                g, t, b = UNITS[m]
                if b == 2:
                    a.wait_ge(sem("att_read"), m + 1)
                    a.activation(oT[:, 4 * g:4 * g + 4, t * P:(t + 1) * P], ps[:, 6, :].rearrange("p (h q) -> p h q", h=4), ACT.Copy).then_inc(sem("oT_full"), 1)

            def lru_exp(h):
                a.wait_ge(sem("log_a"), h + 1)
                a.activation(xc, rr, ACT.Exp).then_inc(sem("lru_exp"), 1)
                a.activation(lt, rr, ACT.Tanh, scale=0.5).then_inc(sem("lru_exp"), 1)

            def lru_root(h):
                a.wait_ge(sem("one_minus_a2"), h + 1)
                a.activation(xc, xc, ACT.Sqrt).then_inc(sem("lru_sqrt"), 1)

            for m in range(len(UNITS)):
                exps(m)
                if m in LRU_AT:
                    {1: lru_exp, 2: lru_root}.get(LRU_AT[m][1], lambda h: None)(LRU_AT[m][0])
                turned(m)
                head_out(m)
                for job, _, last in pieces_of(m):
                    if last and job[0] != "ylru":
                        evacuate(job)

            def expert_sigmoid(q):
                a.wait_ge(sem("glu"), q + 1)
                a.activation(sig, glu, ACT.Sigmoid, scale=ALPHA).then_inc(sem("sig"), 1)

            def expert_turned(q):
                a.wait_ge(sem("act_turned"), q + 1)
                a.activation(actT, Hps[:, 0:512].rearrange("p (j m) -> p j m", j=4), ACT.Copy).then_inc(sem("actT"), 1)
                a.activation(selT, Hps[:, 512:512 + TT * P].rearrange("p (t m) -> p t m", t=TT), ACT.Copy).then_inc(sem("selT"), 1)

            def expert_rows_out(q):
                a.wait_ge(sem("rows"), q + 1)
                a.activation(xg, Gps, ACT.Copy).then_inc(sem("rows_read"), 1)

            def expert_y(q):
                a.wait_ge(sem("w2_used"), (q + 1) * 4)
                a.activation(ysb, Yps, ACT.Copy).then_inc(sem("y_read"), 1)

            for t in range(TT):
                root(7 + t, stat[:, 50 + t:51 + t])
                a.wait_ge(sem("rsqrt"), 7 + t)
                a.activation(xn2[:, t, 512:1024], xs[:, t, 512:1024], ACT.Copy, scale=stat[:, 50 + t:51 + t]).then_inc(sem("xn2b"), 1)
            for k in ODD_BANKS:
                a.wait_ge(sem("x2_turned"), k // 2 + 1)
                a.activation(hT[:, k, :], ps[:, 4 + k // 2, (k % 2) * T:(k % 2 + 1) * T], ACT.Identity, scale=G2[:, k:k + 1], bias=S2[:, k:k + 1]).then_inc(sem("h2T_odd"), 1)
            for t in range(TT):
                a.wait_ge(sem("top4"), t + 1)
                a.activation(topw[:, t, 0:TOPK], top[:, t, 0:TOPK], ACT.Exp, bias=stat[:, 60 + t:61 + t], accum_out=stat[:, 62 + t:63 + t]).then_inc(sem("top_exp"), 1)
            expert_rows_out(0)
            expert_rows_out(1)
            expert_sigmoid(0)
            expert_turned(0)
            with a.Fori(1, NE - 1) as q:
                expert_sigmoid(q)
                expert_y(q - 1)
                expert_rows_out(q + 1)
                expert_turned(q)
            expert_sigmoid(NE - 1)
            expert_y(NE - 2)
            expert_turned(NE - 1)
            expert_y(NE - 1)
            a.wait_ge(sem("xtab"), 1)
            more = a.value_load(xn_i, min_val=0, max_val=XP)
            with a.Fori(0, XP) as i:
                with a.If(more > i):
                    expert_rows_out(i + NE)
                    expert_sigmoid(i + NE)
                    expert_turned(i + NE)
                    expert_y(i + NE)

        @block.tensor
        def _(pe):
            def full(u, times=1):
                nload = lambda w: 2 if w[0] in ("lrugate", "cmp") else 1
                k = SLOT[u]
                total = sum(nload(STREAM[j]) for j in range(k % NSLOT, k + 1, NSLOT))
                pe.wait_ge(sem(f"stream_full{k % NSLOT}"), 16 * total)
                return slot(u)

            def ada(third, k2, bank):
                s = full(("ada", third, k2)).rearrange("p (k n) -> p k n", k=2)
                for k in range(2):
                    for g in range(4):
                        i = pe.matmul(ps[32 * g:32 * g + 32, bank, :], cs32[:, 2 * k2 + k, :], s[:, k, 512 * g:512 * g + 512],
                                      start=(k2 == 0 and k == 0), stop=(k2 == 3 and k == 1), skip_group_check=True)
                i.then_inc(sem("ada_used"), 1)

            pe.wait_ge(sem("cs32"), 1)
            for k2 in range(4):
                ada(0, k2, 7)
            pe.wait_ge(sem("ident"), 1)
            pe.wait_ge(sem("params_in"), 16 * 8)
            pe.transpose(ps[:, 6, 0:P], praw, ident[:, :]).then_inc(sem("params_turned"), 1)
            pe.wait_ge(sem("pe_in"), 32)
            pe.transpose(ps[:, 6, P:P + 64], peraw, ident[0:64, 0:64]).then_inc(sem("params_turned"), 1)
            pe.wait_ge(sem("xn"), 1)
            for k in range(KD):
                for t in range(TT):
                    i = pe.transpose(ps[:, k // 2, (k % 2) * T + t * P:(k % 2) * T + (t + 1) * P], xn[:, t, k * P:(k + 1) * P], ident[:, :])
            i.then_inc(sem("x_turned"), 1)
            pe.wait_ge(sem("params_read"), 1)
            pe.wait_ge(sem("modrow"), 1)
            for j in range(4):
                i = pe.transpose(ps[:, 6, j * P:(j + 1) * P], modrow[:, j * P:(j + 1) * P], ident[:, :])
            i.then_inc(sem("mod_turned"), 1)

            def job_bank(j):
                n = JOB[j]
                if n >= 2:
                    pe.wait_ge(sem("job_read"), n - 1)
                return PAIR[n % 2]

            def rows_out(u, piece):
                s = full(u).rearrange("p (k n) -> p k n", k=KD)
                if piece == 0:
                    job_bank(u)
                p, j = PAIR[JOB[u] % 2], piece
                for k in range(KD):
                    i = pe.matmul(p[:, j * T:(j + 1) * T], s[:, k, j * P:(j + 1) * P], hT[:, k, :], start=(k == 0), stop=(k == KD - 1))
                if piece == 3:
                    i.then_inc(sem("job_full"), 1)

            def tokens_out(u):
                s = full(u).rearrange("p (k n) -> p k n", k=KD)
                p = job_bank(u)
                if u == ("kslc",):
                    pe.wait_ge(sem("hT_even"), 2)
                    pe.wait_ge(sem("hT_odd"), 2)
                for t in range(TT):
                    for k in range(KD):
                        if u == ("kslc",) and t == 0 and k >= 4:
                            pe.wait_ge(sem("hT" + bank_side(k)[0]), bank_side(k)[1])
                        i = pe.matmul(p[:, t * 512:(t + 1) * 512], hT[:, k, t * P:(t + 1) * P], s[:, k, :], start=(k == 0), stop=(k == KD - 1))
                i.then_inc(sem("job_full"), 1)

            def lru_gate(name, h):
                s = full(("lrugate", h))[:, 0:2048].rearrange("p (w a j) -> p w a j", w=2, a=4)
                pe.wait_ge(sem("conv"), h + 1)
                p = job_bank((name, h))
                for j in range(4):
                    for ic in range(2):
                        i = pe.matmul(p[:, j * T:(j + 1) * T], s[:, "ri".index(name), 2 * (j // 2) + ic, (j % 2) * P:(j % 2 + 1) * P],
                                      xc[:, 2 * (j // 2) + ic, :], start=(ic == 0), stop=(ic == 1))
                i.then_inc(sem("job_full"), 1)

            def lru_branch(h, piece):
                s = full(("bo", 1, h)).rearrange("p (k n) -> p k n", k=KD)
                if piece == 0:
                    pe.wait_ge(sem("lru_done"), 2)
                    job_bank(("ylru", h))
                p, j = PAIR[JOB[("ylru", h)] % 2], piece
                for k in range(KD):
                    i = pe.matmul(p[:, j * T:(j + 1) * T], s[:, k, j * P:(j + 1) * P], olT[:, k, :], start=(k == 0), stop=(k == KD - 1))
                if piece == 3:
                    i.then_inc(sem("job_full"), 1)

            def piece_of(job, piece, last):
                if job[0] in ("r", "i"):
                    lru_gate(*job)
                elif job[0] == "ylru":
                    lru_branch(job[1], piece)
                else:
                    rows_out(job, piece)

            for u in (("kslc",), ("kwin",), ("q", 0), ("q", 1)):
                tokens_out(u)
            for piece in range(4):
                rows_out(("kcmp",), piece)
            for t in range(TT):
                for k in range(KD):
                    if t == 0 and k == 0:
                        pe.wait_ge(sem("small_in"), 16 * 12)
                    i = pe.matmul(ps[:, 4, t * N_NSAG:(t + 1) * N_NSAG], hT[:, k, t * P:(t + 1) * P], gw[:, k, :], start=(k == 0), stop=(k == KD - 1))
            i.then_inc(sem("ng_full"), 1)
            for piece in range(4):
                rows_out(("lrux", 0), piece)
            pe.wait_ge(sem("cmp_rows"), 1)
            pe.wait_ge(sem("ng_read"), 1)
            for c4 in range(4):
                s = full(("cmp", c4)).rearrange("p (w l n) -> p w l n", w=2, l=8)
                for l8 in range(8):
                    l = 8 * c4 + l8
                    pe.matmul(ps[0:64, 4, 0:CMP_HIDDEN], LK[:, l, :], s[:, 0, l8, :], start=(l == 0), stop=(l == 31), skip_group_check=True)
                    i = pe.matmul(ps[64:128, 4, 0:CMP_HIDDEN], LV[:, l, :], s[:, 1, l8, :], start=(l == 0), stop=(l == 31), skip_group_check=True)
                i.then_inc(sem("cmp_used"), 1)
            pe.wait_ge(sem("roped"), 1)
            pe.wait_ge(sem("cmp_gelu"), 1)
            for j in range(10):
                if j >= 2:
                    pe.wait_ge(sem("qk_read"), j - 1)
                for h in range(2):
                    for t in range(TT):
                        src = (QK[:, t, 2 * j + h, :] if j < 4 else QR[:, t, 2 * j - 8 + h, :])
                        i = pe.transpose(ps[:, 4 + j % 2, h * T + t * P:h * T + (t + 1) * P], src, ident[:, :])
                i.then_inc(sem("qk_turned"), 1)
            pe.wait_ge(sem("mod_read"), 1)
            for j in range(2):
                i = pe.transpose(ps[:, 6, j * P:(j + 1) * P], uu[:, j * P:(j + 1) * P], ident[:, :])
            i.then_inc(sem("uT_full"), 1)
            early = pieces_of(-1)
            piece_of(*early[0])
            pe.wait_ge(sem("uT_read"), 1)
            pe.wait_ge(sem("w2c_in"), 32)
            for w in range(2):
                for j in range(2):
                    i = pe.matmul(ps[0:64, 6, 256 + w * P:256 + (w + 1) * P], uT[:, j, 64 * w:64 * w + 64], w2c[:, 2 * w + j, :],
                                  start=(j == 0), stop=(j == 1))
            i.then_inc(sem("cmp2_full"), 1)
            for piece in early[1:3]:
                piece_of(*piece)
            pe.wait_ge(sem("kcn"), 1)
            pe.transpose(ps[:, 6, 0:64], kcn, ident[0:64, 0:64]).then_inc(sem("kc_turned"), 1)
            piece_of(*early[3])

            def scores(m):
                g, t, b = UNITS[m]
                if m >= 1:
                    pe.wait_ge(sem("att_pT"), m)
                for h in range(HPG):
                    hd = HPG * g + h
                    if b == 0:
                        i = pe.matmul(Hps[:, h * 16:h * 16 + N_CMP], qT[:, hd, t * P:(t + 1) * P], kccT[:, 32 * g:32 * g + N_CMP], start=True, stop=True)
                    else:
                        nk = P * (t + 1)
                        i = pe.matmul(Hps[:, h * nk:(h + 1) * nk], qrT[:, hd, t * P:(t + 1) * P], kT[:, 2 * (b - 1) + g, 0:nk], start=True, stop=True)
                i.then_inc(sem("scores"), 1)

            def turn(m):
                g, t, b = UNITS[m]
                pe.wait_ge(sem("att_p"), m + 1)
                for h in range(HPG):
                    if b == 0:
                        i = pe.transpose(ps[0:64, 4, h * P:(h + 1) * P], Pc[:, h, :], ident[:, :])
                    else:
                        for kt in range(t + 1):
                            i = pe.transpose(ps[:, 4 + kt, h * P:(h + 1) * P], Sb[:, m % 2, h * T + kt * P:h * T + (kt + 1) * P], ident[:, :])
                i.then_inc(sem("att_turned"), 1)

            def values(m):
                g, t, b = UNITS[m]
                pe.wait_ge(sem("att_pT"), m + 1)
                if b == 0:
                    if m >= 3:
                        pe.wait_ge(sem("oT_full"), m // 3)
                    i = pe.matmul(ps[:, 6, :], vcs, PT[0:64, 0, :], start=True, stop=False, skip_group_check=True)
                else:
                    for kt in range(t + 1):
                        i = pe.matmul(ps[:, 6, :], vtm[:, b - 1, kt, g * DH:(g + 1) * DH], PT[:, kt, :], start=False,
                                      stop=(b == 2 and kt == t), skip_group_check=True)
                i.then_inc(sem("att_read"), 1)

            pe.wait_ge(sem("qk_read"), 10)
            pe.wait_ge(sem("kccT"), 1)
            for m in range(len(UNITS)):
                scores(m)
                for piece in pieces_of(m)[:2]:
                    piece_of(*piece)
                turn(m)
                for piece in pieces_of(m)[2:]:
                    piece_of(*piece)
                if m in ADA_AT:
                    if ADA_AT[m] == (2, 0):
                        pe.wait_ge(sem("mod_rows"), 1)
                    ada(*ADA_AT[m], 7)
                values(m)

            def late_columns():
                for third in (1, 2):
                    for j in range(4):
                        i = pe.transpose(ps[:, 3 + third, j * P:(j + 1) * P], mod2[:, third - 1, j * P:(j + 1) * P], ident[:, :])
                    i.then_inc(sem("mod2_turned"), 1)

            def gate_rows(third):
                pe.wait_ge(sem("pick"), 1)
                for j in range(2):
                    n = 2 * (third - 1) + j
                    if third == 2:
                        pe.wait_ge(sem("gate_read"), j + 1)
                    pe.matmul(ps[:, 6 + j, :], pickt[:, n, :], mod2[:, third - 1, :], start=True, stop=True).then_inc(sem("gate_rows"), 1)

            pe.wait_ge(sem("oT_full"), NG * TT)
            for half in range(2):
                s = full(("bo", 0, half)).rearrange("p (k n) -> p k n", k=KD)
                pe.wait_ge(sem("y_taken"), half + 1)
                p = PAIR[JOB[("ylru", half)] % 2]
                for j in range(4):
                    for k in range(KD):
                        i = pe.matmul(p[:, j * T:(j + 1) * T], s[:, k, j * P:(j + 1) * P], oT[:, k, :], start=(k == 0), stop=(k == KD - 1))
                i.then_inc(sem("branch"), 1)
                if half == 0:
                    late_columns()
                    gate_rows(1)
                else:
                    gate_rows(2)
            pe.wait_ge(sem("merged"), 2)
            for half in range(2):
                s = full(("wo", half)).rearrange("p (k n) -> p k n", k=KD)
                for t in range(TT):
                    for k in range(KD):
                        i = pe.matmul(PAIR[half][:, t * 512:(t + 1) * 512], mergedT[:, k, t * P:(t + 1) * P], s[:, k, :], start=(k == 0), stop=(k == KD - 1))
                    i.then_inc(sem("wo_full"), 1)
            pe.wait_ge(sem("gate_read"), 4)
            for t in range(TT):
                for k in range(KD):
                    if k % 4 == 0:
                        pe.wait_ge(sem(("xn2", "xn2b")[k // 4]), t + 1)
                    i = pe.transpose(ps[:, 4 + k // 2, (k % 2) * T + t * P:(k % 2) * T + (t + 1) * P], xn2[:, t, k * P:(k + 1) * P], ident[:, :])
                    if k % 2 and t == TT - 1:
                        i.then_inc(sem("x2_turned"), 1)
            for k in range(KD):
                pe.wait_ge(sem("h2T" + bank_side(k)[0]), bank_side(k)[1])
                for t in range(TT):
                    i = pe.matmul(ps[:, t, 0:NE], hT[:, k, t * P:(t + 1) * P], rw[:, k, :], start=(k == 0), stop=(k == KD - 1))
            i.then_inc(sem("logits"), 1)
            pe.wait_ge(sem("mask"), 1)
            pe.wait_ge(sem("pool_masks"), 2)
            pe.matmul(ps[:, 5, 0:NE], upper, msk[:, 0, :], start=True, stop=True)
            pe.matmul(ps[:, 5, NE:2 * NE], ones, msk[:, 0, :], start=True, stop=False)
            pe.matmul(ps[:, 5, NE:2 * NE], upper, msk[:, 1, :], start=False, stop=True)
            pe.matmul(ps[:, 5, 2 * NE:3 * NE], ones, msk[:, 0, :], start=True, stop=False)
            pe.matmul(ps[:, 5, 2 * NE:3 * NE], ones, msk[:, 1, :], start=False, stop=True).then_inc(sem("places"), 1)

            def tables_turned():
                pe.wait_ge(sem("pos"), 1)
                for t in range(TT):
                    pe.transpose(ps[0:NE, 6, t * P:(t + 1) * P], wts[:, t, :], ident[:, :])
                    i = pe.transpose(ps[0:NE, 6, T + t * P:T + (t + 1) * P], pos[:, t, :], ident[:, :])
                i.then_inc(sem("routes_turned"), 1)
                pe.wait_ge(sem("ohx"), 1)
                pe.transpose(ps[0:NE, 0, 0:P], ohx, ident[:, :])
                pe.transpose(ps[0:8, 0, P:2 * P], xcol, ident[:, :]).then_inc(sem("xcols"), 1)

            def tables_products():
                pe.wait_ge(sem("b2_in"), 16)
                for t in range(TT):
                    for h in range(2):
                        pe.matmul(ps[:, 2 * t + h, :], wT[:, t * P:(t + 1) * P], b2s[:, h * 512:(h + 1) * 512], start=False, stop=False, skip_group_check=True)
                for t in range(TT):
                    pe.matmul(ps[:, 6, t * 32:t * 32 + XP], posT[:, t * P:(t + 1) * P], ohT[:, 0:XP], start=True, stop=True)
                    pe.matmul(ps[:, 6, 64 + t * 32:64 + t * 32 + XP], wT[:, t * P:(t + 1) * P], ohT[:, 0:XP], start=True, stop=True)
                pe.matmul(ps[:, 6, 128:128 + XP], pick1, chk[0:8, 0:XP], start=True, stop=True).then_inc(sem("xmats"), 1)

            def gather(q):
                pe.wait_ge(sem("sel"), q + 1)
                for t in range(TT):
                    for g in range(2):
                        i = pe.matmul(Gps[64 * g:64 * g + 64, :], sel[:, t, :], xn2[:, t, g * 512:(g + 1) * 512],
                                      start=(t == 0), stop=(t == TT - 1), skip_group_check=True)
                i.then_inc(sem("rows"), 1)

            def turn_rows(q):
                pe.wait_ge(sem("rows_read"), q + 1)
                for j in range(4):
                    i = pe.transpose(Gps[:, j * P:(j + 1) * P], xg[:, j * P:(j + 1) * P], ident[:, :])
                i.then_inc(sem("rows_turned"), 1)

            def first(q, early=(), halfway=None):
                pe.wait_ge(sem("xT"), q + 1)
                pe.wait_ge(sem("ohp"), q + 1)
                if not (isinstance(q, int) and q == 0):
                    pe.wait_ge(sem("selT"), q)
                parts = [(g, b) for b in range(2) for g in range(2)]
                for g, b in parts:
                    cc = 1024 * g + 512 * b
                    pe.matmul(Hps[64 * g:64 * g + 64, b * 512:(b + 1) * 512], ohp, b1s[:, cc:cc + 512], start=True, stop=False, skip_group_check=True)
                for k in range(KD):
                    if k < len(early):
                        pe.wait_ge(sem(f"w1_early{k}"), 16)
                    elif k < len(ahead) and not (isinstance(q, int) and q == 0):
                        pe.wait_ge(sem(f"w1_full{k}"), q * 16)
                    else:
                        pe.wait_ge(sem(f"w1_full{k}"), (q + 1) * 16)
                    w = early[k] if k < len(early) else w1v[:, k, :]
                    for g, b in parts:
                        cc = 1024 * g + 512 * b
                        i = pe.matmul(Hps[64 * g:64 * g + 64, b * 512:(b + 1) * 512], xT[:, k, :], w[:, cc:cc + 512],
                                      start=False, stop=(k == KD - 1), skip_group_check=True)
                    i.then_inc(sem("w1_used"), 1)
                    if k == 3 and halfway:
                        halfway()

            def turn_act(q):
                pe.wait_ge(sem("act"), q + 1)
                for j in range(4):
                    pe.transpose(Hps[:, j * P:(j + 1) * P], act[:, j * P:(j + 1) * P], ident[:, :])
                pe.wait_ge(sem("selw"), q + 1)
                for t in range(TT):
                    i = pe.transpose(Hps[:, 512 + t * P:512 + (t + 1) * P], selw[:, t, :], ident[:, :])
                i.then_inc(sem("act_turned"), 1)

            def second(q, early=()):
                pe.wait_ge(sem("actT"), q + 1)
                for s in range(4):
                    if early:
                        pe.wait_ge(sem(f"w2_early{s}"), 16)
                    elif isinstance(q, int) and q == 0:
                        pe.wait_ge(sem(f"w2_full{s}"), 16)
                    else:
                        pe.wait_ge(sem(f"w2_full{s}"), q * 16)
                    for k in (2 * s, 2 * s + 1):
                        w = early[s][:, k % 2, :] if early else w2v[:, k, :]
                        for g in range(2):
                            i = pe.matmul(Yps[64 * g:64 * g + 64, :], actT[:, k % 4, 64 * (k // 4):64 * (k // 4) + 64],
                                          w[:, g * 512:(g + 1) * 512], start=(k == 0), stop=(k == 7), skip_group_check=True)
                    i.then_inc(sem("w2_used"), 1)

            def scatter(q, opens=False):
                pe.wait_ge(sem("y_read"), q + 1)
                pe.wait_ge(sem("selT"), q + 1)
                for t in range(TT):
                    for g in range(2):
                        pe.matmul(ps[:, 2 * t + g, :], selT[64 * g:64 * g + 64, t, :], ysb[64 * g:64 * g + 64, :],
                                  start=opens, stop=False, skip_group_check=True).then_inc(sem("scattered"), 1)

            gather(0)
            turn_rows(0)
            first(0, halfway=tables_turned)
            gather(1)
            turn_rows(1)
            turn_act(0)
            first(1, ahead)
            pe.wait_ge(sem("ohT"), 1)
            second(0)
            gather(2)
            scatter(0, opens=True)
            turn_rows(2)
            turn_act(1)
            first(2)
            second(1, w2_ahead)
            gather(3)
            scatter(1)
            turn_rows(3)
            turn_act(2)
            with pe.Fori(3, NE - 1) as q:
                first(q)
                second(q - 1)
                gather(q + 1)
                scatter(q - 1)
                turn_rows(q + 1)
                turn_act(q)
            tables_products()
            first(NE - 1)
            pe.wait_ge(sem("tables"), 1)
            second(NE - 2)
            scatter(NE - 2)
            turn_act(NE - 1)
            second(NE - 1)
            scatter(NE - 1)
            more = pe.value_load(xn_i, min_val=0, max_val=XP)
            with pe.Fori(0, XP) as i:
                with pe.If(more > i):
                    gather(i + NE)
                    turn_rows(i + NE)
                    first(i + NE)
                    turn_act(i + NE)
                    second(i + NE)
                    scatter(i + NE)

        @block.vector
        def _(v):
            n = [0]

            def link(i):
                n[0] += 1
                i.then_inc(sem("dve_chain"), 1)
                v.wait_ge(sem("dve_chain"), n[0])

            def done(name):
                v.nop().then_inc(sem(name), 1)

            tt, ts, stt = v.tensor_tensor, v.tensor_scalar, v.scalar_tensor_tensor

            v.wait_ge(sem("sig_c"), 1)
            v.wait_ge(sem("c_in"), 16)
            tt(cs32[:, :, :], ccol[:, 0:KD].unsqueeze(2).to_broadcast((P, KD, 32)), ccol[:, KD:2 * KD].unsqueeze(2).to_broadcast((P, KD, 32)),
               ALU.mult).then_inc(sem("cs32"), 1)
            v.wait_ge(sem("x_sq"), 1)
            link(ts(stat[:, 2:4], stat[:, 0:2], 1.0 / D, EPS, ALU.mult, ALU.add))
            link(v.reciprocal(stat[:, 2:4], stat[:, 2:4]))
            done("square")
            v.wait_ge(sem("rsqrt"), 1)
            for t in range(TT):
                link(ts(xn[:, t, :], xs[:, t, :], stat[:, 2 + t:3 + t], None, ALU.mult))
            done("xn")
            v.wait_ge(sem("params_turned"), 2)
            link(v.tensor_copy(pcol[:, :], ps[:, 6, 0:P]))
            link(v.tensor_copy(peT[:, :], ps[:, 6, P:P + 64]))
            done("params_read")
            v.wait_ge(sem("ada_used"), 4)
            v.tensor_copy(modrow, ps[:, 7, :]).then_inc(sem("modrow"), 1)
            v.wait_ge(sem("mod_turned"), 1)
            mc = ps[:, 6, :].rearrange("p (s g r) -> p g s r", s=4, g=4)[:, :, :, 0]
            m3v = m3[:, :].rearrange("p (g s) -> p g s", g=4)
            link(tt(m3v, mc, pcol[:, R_ADAB:R_ADAB + 16].rearrange("p (g s) -> p g s", g=4), ALU.add))
            done("mod_read")
            link(v.tensor_copy(S1[:, :], m3[:, 0:8]))
            link(stt(G1[:, :], m3[:, 8:16], 1.0, pcol[:, R_N1:R_N1 + 8], ALU.add, ALU.mult))
            v.wait_ge(sem("x_turned"), 1)
            done("mod1")
            for k in EVEN_BANKS:
                ts(hT[:, k, :], ps[:, k // 2, (k % 2) * T:(k % 2 + 1) * T], G1[:, k:k + 1], S1[:, k:k + 1], ALU.mult, ALU.add).then_inc(sem("hT_even"), 1)
            link(v.memset(lx[:, :, 0:3], 0.0))
            done("lx_zero")
            lam = pcol[:, R_LAM:R_LAM + 8]
            z, s_, s2, acc = (spl[:, j, :] for j in range(4))
            link(stt(z, lam, -1.0, lam, ALU.mult, ALU.min))
            done("lam_abs")
            v.wait_ge(sem("lam_exp"), 1)
            link(ts(s_, z, 2.0, None, ALU.add))
            link(v.reciprocal(s_, s_))
            link(tt(s_, s_, z, ALU.mult))
            link(tt(s2, s_, s_, ALU.mult))
            link(ts(acc, s2, 1.0 / 15, 1.0 / 13, ALU.mult, ALU.add))
            for d in (11, 9, 7, 5, 3, 1):
                link(tt(acc, acc, s2, ALU.mult))
                link(ts(acc, acc, 1.0 / d, None, ALU.add))
            link(tt(acc, acc, s_, ALU.mult))
            link(ts(z, lam, -1.0, 0.0, ALU.mult, ALU.max))
            link(stt(acc, acc, 2.0, z, ALU.mult, ALU.add))
            link(ts(acc, acc, -LRU_C, None, ALU.mult))
            spf = acc

            v.wait_ge(sem("small_in"), 16 * 12)
            link(v.tensor_copy(pos_f[:, :], pos_i[:, :]))
            for t in range(TT):
                link(ts(ang[:, t, :], ang[:, t, :], pos_f[:, t:t + 1], None, ALU.mult))
            C1 = 6.28125
            C2 = float(np.float32(np.floor((2 * np.pi - C1) * 2 ** 22) / 2 ** 22))
            C3 = float(2 * np.pi - C1 - C2)
            BIG = 1.5 * 2 ** 23
            link(ts(cosT, ang, 1.0 / (2 * np.pi), BIG, ALU.mult, ALU.add))
            link(ts(cosT, cosT, -BIG, None, ALU.add))
            for cst in (C1, C2, C3):
                link(stt(ang, cosT, -cst, ang, ALU.mult, ALU.add))
            link(ts(sinT, ang, 3.1415925, -3.1415925, ALU.min, ALU.max))
            link(stt(cosT, sinT, -1.0, sinT, ALU.mult, ALU.min))
            link(ts(cosT, cosT, float(np.pi / 2), None, ALU.add))
            done("angles")
            def convolution(h):
                v.wait_ge(sem("job_read"), JOB[("lrux", h)] + 1)
                for w in range(4):
                    for k in range(KH):
                        kk = 4 * h + k
                        cw = pcol[:, R_CONVW + 8 * w + kk:R_CONVW + 8 * w + kk + 1]
                        if w == 0:
                            i = ts(xc[:, k, :], lx[:, k, 0:T], cw, pcol[:, R_CONVB + kk:R_CONVB + kk + 1], ALU.mult, ALU.add)
                        else:
                            i = stt(xc[:, k, :], lx[:, k, w:w + T], cw, xc[:, k, :], ALU.mult, ALU.add)
                    link(i)
                done("conv")

            def lru_step(h, step):
                if step == 1:
                    v.wait_ge(sem("job_read"), JOB[("i", h)] + 1)
                    link(tt(rr, rr, spf[:, 4 * h:4 * h + 4].unsqueeze(2).to_broadcast((P, KH, T)), ALU.mult))
                    link(tt(ii, ii, xc, ALU.mult))
                    done("log_a")
                if step == 2:
                    v.wait_ge(sem("lru_exp"), 2 * h + 2)
                    link(stt(xc, xc, 1.0, lt, ALU.add, ALU.mult))
                    link(ts(rr, xc, 1.0, None, ALU.add))
                    link(stt(xc, xc, 2.0, xc, ALU.add, ALU.mult))
                    link(ts(xc, xc, -1.0, 0.0, ALU.mult, ALU.max))
                    done("one_minus_a2")
                    if h == 0:
                        link(v.memset(lx[:, :, 0:3], 0.0))
                        done("lx_zero")
                if step == 3:
                    v.wait_ge(sem("lru_sqrt"), h + 1)
                    link(tt(ii, ii, xc, ALU.mult))
                    for k in range(KH):
                        i = v.tensor_tensor_scan(xc[:, k, :], rr[:, k, :], ii[:, k, :], 0.0, ALU.mult, ALU.add)
                    link(i)
                    link(tt(olT[:, 4 * h:4 * h + 4, :], olT[:, 4 * h:4 * h + 4, :], xc, ALU.mult))
                    done("lru_done")

            def qk_norm(h0, nh, col, n):
                st = stat[:, 64:64 + TT * nh]
                for t in range(TT):
                    q = QK[:, t, h0:h0 + nh, :]
                    sq = QR[:, t, h0:h0 + nh, :]
                    link(tt(sq, q, q, ALU.mult))
                    link(v.tensor_reduce(stat[:, 64 + nh * t:64 + nh * (t + 1)], sq, AX.X, ALU.add))
                link(ts(st, st, 1.0 / DH, EPS, ALU.mult, ALU.add))
                link(v.reciprocal(st, st))
                done("square")
                v.wait_ge(sem("rsqrt"), n)
                for t in range(TT):
                    q = QK[:, t, h0:h0 + nh, :]
                    link(tt(q, q, stat[:, 64 + nh * t:64 + nh * (t + 1)].unsqueeze(2).to_broadcast((P, nh, DH)), ALU.mult))
                    link(tt(q, q, gain[:, col:col + 1, :].to_broadcast((P, nh, DH)), ALU.mult))

            def rope(h0, nh):
                for t in range(TT):
                    x1, x2 = QK[:, t, h0:h0 + nh, 0:64], QK[:, t, h0:h0 + nh, 64:128]
                    r1, r2 = QR[:, t, h0:h0 + nh, 0:64], QR[:, t, h0:h0 + nh, 64:128]
                    tm = rtmp[:, t, 0:nh, :]
                    cb = cosT[:, t:t + 1, :].to_broadcast((P, nh, 64))
                    sb_ = sinT[:, t:t + 1, :].to_broadcast((P, nh, 64))
                    link(tt(tm, x2, sb_, ALU.mult))
                    link(tt(r1, x1, cb, ALU.mult))
                    link(tt(r1, r1, tm, ALU.subtract))
                    link(tt(tm, x1, sb_, ALU.mult))
                    link(tt(r2, x2, cb, ALU.mult))
                    link(tt(r2, r2, tm, ALU.add))

            v.wait_ge(sem("sincos"), 2)
            v.wait_ge(sem("job_read"), JOB[("kwin",)] + 1)
            qk_norm(8, 2, 2, 2)
            qk_norm(10, 2, 3, 3)
            rope(8, 4)
            for h in range(2):
                v.wait_ge(sem("job_read"), JOB[("q", h)] + 1)
                qk_norm(4 * h, 4, 0, 4 + h)
                rope(4 * h, 4)
            done("roped")
            v.wait_ge(sem("pool_masks"), 1)
            link(v.memset(LV, 0.0))
            v.wait_ge(sem("job_read"), JOB[("kcmp",)] + 1)
            for kv, L in enumerate((LK, LV)):
                for g in range(NG):
                    src = kcT[:, 2 * kv + g, :].rearrange("p (b l) -> p l b", l=16)
                    for h in range(2):
                        e = peT[:, 32 * kv + 16 * h:32 * kv + 16 * h + 16].unsqueeze(2).to_broadcast((P, 16, N_CMP))
                        i = tt(L[:, 16 * h:16 * h + 16, 32 * g:32 * g + N_CMP], src[:, :, h:h + N_CMP], e, ALU.add)
            link(i)
            done("cmp_rows")
            convolution(0)
            v.wait_ge(sem("cmp2_full"), 1)
            kp = ps[0:64, 6, 256:384]
            link(v.tensor_copy(vcs, ps[0:64, 6, 384:512]))
            link(v.tensor_copy(kcn, kp))
            link(tt(ksq, kcn, kcn, ALU.mult))
            link(v.tensor_reduce(stat[0:64, 80:81], ksq, AX.X, ALU.add))
            link(ts(stat[0:64, 80:81], stat[0:64, 80:81], 1.0 / DH, EPS, ALU.mult, ALU.add))
            link(v.reciprocal(stat[0:64, 80:81], stat[0:64, 80:81]))
            done("square")
            v.wait_ge(sem("rsqrt"), 6)
            link(ts(kcn, kcn, stat[0:64, 80:81], None, ALU.mult))
            link(tt(kcn, kcn, gain[0:64, 1, :], ALU.mult))
            done("kcn")
            v.wait_ge(sem("kc_turned"), 1)
            link(v.tensor_copy(kccT, ps[:, 6, 0:64]))
            done("kccT")

            def softmax_in(m):
                g, t, b = UNITS[m]
                v.wait_ge(sem("scores"), m + 1)
                if m >= 2:
                    v.wait_ge(sem("att_turned"), m - 1)
                S = Sb[:, m % 2, :].rearrange("p (h k) -> p h k", h=HPG)
                if b == 0:
                    p = Hps[:, 0:64].rearrange("p (h k) -> p h k", h=HPG)
                    nk = N_CMP
                    link(tt(S[:, :, 0:nk], p[:, :, 0:nk], cneg[:, t:t + 1, 0:nk].to_broadcast((P, HPG, nk)), ALU.add))
                    if m >= 3:
                        v.wait_ge(sem("att_turned"), m - 2)
                    link(v.memset(Pc, 0.0))
                else:
                    nk = P * (t + 1)
                    p = Hps[:, 0:HPG * nk].rearrange("p (h k) -> p h k", h=HPG)
                    if t == 1:
                        link(v.tensor_copy(S[:, :, 0:P], p[:, :, 0:P]))
                    link(tt(S[:, :, nk - P:nk], p[:, :, nk - P:nk], causal[:, :].unsqueeze(1).to_broadcast((P, HPG, P)), ALU.add))
                mx = stat[:, 16 + 8 * (m % 2):20 + 8 * (m % 2)]
                link(v.tensor_reduce(mx, S[:, :, 0:nk], AX.X, ALU.max))
                link(ts(mx, mx, NEG * 1e-10, -SCALE, ALU.max, ALU.mult))
                done("att_max")

            def softmax_out(m):
                g, t, b = UNITS[m]
                v.wait_ge(sem("att_exp"), m + 1)
                sm = stat[:, 32 + 8 * (m % 2):36 + 8 * (m % 2)]
                if b == 0:
                    link(ts(sm, sm, 1e-30, None, ALU.max))
                link(v.reciprocal(sm, sm))
                gb = ng[:, t, :].rearrange("p (h b) -> p h b", b=3)[:, HPG * g:HPG * g + HPG, b]
                link(tt(sm, sm, gb, ALU.mult))
                sbc = sm.unsqueeze(2)
                if b == 0:
                    q = Pc[:, :, 32 * g:32 * g + N_CMP]
                    link(tt(q, q, sbc.to_broadcast((P, HPG, N_CMP)), ALU.mult))
                else:
                    nk = P * (t + 1)
                    q = Sb[:, m % 2, :].rearrange("p (h k) -> p h k", h=HPG)[:, :, 0:nk]
                    link(tt(q, q, sbc.to_broadcast((P, HPG, nk)), ALU.mult))
                done("att_p")

            def lru_branch_gated(h):
                v.wait_ge(sem("job_full"), JOB[("ylru", h)] + 1)
                v.wait_ge(sem("job_read"), JOB[("merge", 3)] + 1)
                y = PAIR[JOB[("ylru", h)] % 2].rearrange("p (k t) -> p k t", k=4)
                mgv = mg[:, KD + 4 * h:KD + 4 * h + 4, :]
                link(tt(mgv, y, mgv, ALU.mult))
                done("y_taken")

            v.wait_ge(sem("qk_turned"), 10)
            for m in range(len(UNITS)):
                if LRU_AT.get(m, (0, 1))[1] == 0:
                    convolution(LRU_AT[m][0])
                softmax_in(m)
                if m in LRU_AT:
                    lru_step(*LRU_AT[m])
                softmax_out(m)
                if m in (4, 9):
                    v.wait_ge(sem("ada_used"), 8 if m == 4 else 12)
                    link(v.tensor_copy(mod2[:, m // 5, :], ps[:, 7, :]))
                    done("mod_rows")
                if m == 11:
                    lru_branch_gated(0)

            def modulations():
                link(v.memset(pickt, 0.0))
                for g in range(4):
                    link(v.memset(pickt[32 * g:32 * g + 1, g, :], 1.0))
                done("pick")
                for third in (1, 2):
                    v.wait_ge(sem("mod2_turned"), third)
                    mc = ps[:, 3 + third, :].rearrange("p (s g r) -> p g s r", s=4, g=4)[:, :, :, 0]
                    link(tt(m3v, mc, pcol[:, R_ADAB + 16 * third:R_ADAB + 16 * third + 16].rearrange("p (g s) -> p g s", g=4), ALU.add))
                    done("mod_read")
                    if third == 1:
                        link(v.tensor_copy(S2[:, :], m3[:, 8:16]))
                    else:
                        link(stt(G2[:, :], m3[:, 0:8], 1.0, pcol[:, R_N2:R_N2 + 8], ALU.add, ALU.mult))

            def add_gate_rows(third):
                gt = gate1 if third == 1 else gate2
                for j in range(2):
                    v.wait_ge(sem("gate_rows"), 2 * (third - 1) + j + 1)
                    link(tt(gt[:, j * 512:(j + 1) * 512], gt[:, j * 512:(j + 1) * 512], ps[:, 6 + j, :], ALU.add))
                    done("gate_read")

            lru_branch_gated(1)
            modulations()
            add_gate_rows(1)
            for half in range(2):
                v.wait_ge(sem("branch"), half + 1)
                y = PAIR[JOB[("ylru", half)] % 2].rearrange("p (k t) -> p k t", k=4)
                link(tt(mergedT[:, 4 * half:4 * half + 4, :], y, mg[:, 4 * half:4 * half + 4, :], ALU.mult))
                link(tt(mergedT[:, 4 * half:4 * half + 4, :], mergedT[:, 4 * half:4 * half + 4, :], mg[:, KD + 4 * half:KD + 4 * half + 4, :], ALU.add))
                done("merged")
            add_gate_rows(2)
            for half in range(2):
                for t in range(TT):
                    v.wait_ge(sem("wo_full"), 2 * half + t + 1)
                    tmp = x1tmp[:, t, half * 512:(half + 1) * 512]
                    link(tt(tmp, PAIR[half][:, t * 512:(t + 1) * 512], gate1[:, half * 512:(half + 1) * 512], ALU.mult))
                    xv = xs[:, t, half * 512:(half + 1) * 512]
                    link(tt(xv, xv, tmp, ALU.add))
                    link(stt(tmp, xv, 1.0, xv, ALU.mult, ALU.mult, accum_out=stat[:, 84 + 2 * half + t:85 + 2 * half + t]))
                    if half == 1:
                        rms = stat[:, 50 + t:51 + t]
                        link(tt(rms, stat[:, 84 + t:85 + t], stat[:, 86 + t:87 + t], ALU.add))
                        link(ts(rms, rms, 1.0 / D, EPS, ALU.mult, ALU.add))
                        link(v.reciprocal(rms, rms))
                        done("square")
                        v.wait_ge(sem("rsqrt"), 7 + t)
                        ts(xn2[:, t, 0:512], xs[:, t, 0:512], rms, None, ALU.mult).then_inc(sem("xn2"), 1)
            for k in EVEN_BANKS:
                v.wait_ge(sem("x2_turned"), k // 2 + 1)
                ts(hT[:, k, :], ps[:, 4 + k // 2, (k % 2) * T:(k % 2 + 1) * T], G2[:, k:k + 1], S2[:, k:k + 1], ALU.mult, ALU.add).then_inc(sem("h2T_even"), 1)
            def select(q):
                for t in range(TT):
                    i = ts(sel[:, t, :], iota[:, 0:CAP], posP[:, t, bass.ds(q, 1)], None, ALU.is_equal)
                i.then_inc(sem("sel"), 1)

            def select_w(q):
                for t in range(TT):
                    i = ts(selw[:, t, :], iota, posP[:, t, bass.ds(q, 1)], wP[:, t, bass.ds(q, 1)], ALU.is_equal, ALU.mult)
                i.then_inc(sem("selw"), 1)

            def expert_rows(q):
                v.wait_ge(sem("rows_turned"), q + 1)
                g = Gps.rearrange("p (j h c) -> p h j c", j=4, h=2)
                v.tensor_tensor(xT.rearrange("p (h j) c -> p h j c", h=2), g,
                                G2[:, :].rearrange("p (h j) -> p h j", h=2).unsqueeze(3).to_broadcast((P, 2, 4, CAP)), ALU.mult).then_inc(sem("xT_half"), 1)
                v.tensor_copy(ohp, oh96[:, bass.ds(q, 1)].to_broadcast((96, CAP))).then_inc(sem("ohp"), 1)
                v.wait_ge(sem("xT_half"), q + 1)
                v.tensor_tensor(xT, xT, S2[:, :].unsqueeze(2).to_broadcast((P, KD, CAP)), ALU.add).then_inc(sem("xT"), 1)

            def swiglu(q):
                v.wait_ge(sem("w1_used"), (q + 1) * KD)
                hv = Hps.rearrange("p (f two) -> p two f", two=2)
                ts(glu, hv[:, 0, :], LIMIT, None, ALU.min).then_inc(sem("glu"), 1)
                ts(lin, hv[:, 1, :], LIMIT, -LIMIT, ALU.min, ALU.max).then_inc(sem("lin"), 1)
                v.wait_ge(sem("lin"), q + 1)
                stt(lin, lin, 1.0, glu, ALU.add, ALU.mult).then_inc(sem("lin2"), 1)
                v.wait_ge(sem("lin2"), q + 1)
                v.wait_ge(sem("sig"), q + 1)
                tt(act, lin, sig, ALU.mult).then_inc(sem("act"), 1)

            v.wait_ge(sem("pool_masks"), 2)
            for j in range(3):
                link(v.tensor_copy(oh96[32 * j:32 * j + 32, 0:NE], ident[32 * j:32 * j + 32, 32 * j:32 * j + 32]))
            v.wait_ge(sem("logits"), 1)
            link(tt(lg, ps[:, 0:2, 0:NE], rb[:, :].unsqueeze(1).to_broadcast((P, TT, NE)), ALU.add))
            for t in range(TT):
                link(v.max(top[:, t, :], lg[:, t, :]))
                ts(stat[:, 60 + t:61 + t], top[:, t, 0:1], -1.0, None, ALU.mult).then_inc(sem("top4"), 1)
            for t in range(TT):
                link(v.max_index(topi[:, t, :].bitcast(U32), top[:, t, :], lg[:, t, :]))
            link(v.tensor_copy(topi, topi.bitcast(U32)))
            link(tt(eq4, iotaE.unsqueeze(1).unsqueeze(3).to_broadcast((P, TT, NE, TOPK)),
                    topi[:, :, 0:TOPK].unsqueeze(2).to_broadcast((P, TT, NE, TOPK)), ALU.is_equal))
            link(v.tensor_reduce(msk, eq4, AX.X, ALU.add))
            done("mask")
            v.wait_ge(sem("top_exp"), TT)
            link(v.reciprocal(stat[:, 62:64], stat[:, 62:64]))
            link(tt(topw[:, :, 0:TOPK], topw[:, :, 0:TOPK], stat[:, 62:64].unsqueeze(2).to_broadcast((P, TT, TOPK)), ALU.mult))
            link(tt(eq4w, eq4, topw[:, :, 0:TOPK].unsqueeze(2).to_broadcast((P, TT, NE, TOPK)), ALU.mult))
            link(v.tensor_reduce(wts, eq4w, AX.X, ALU.add))
            link(v.tensor_copy(wP[:, :, 0:NE], wts))
            link(ts(tmpe, msk, -4096.0, 4096.0, ALU.mult, ALU.add))
            v.wait_ge(sem("places"), 1)
            pp = ps[:, 5, 0:2 * NE].rearrange("p (t e) -> p t e", t=TT)
            link(tt(posP[:, :, 0:NE], pp, tmpe, ALU.add))
            select(0)
            link(v.tensor_copy(pos, posP[:, :, 0:NE]))
            link(v.tensor_copy(cnt, ps[:, 5, 2 * NE:3 * NE]))
            done("pos")
            expert_rows(0)
            link(ts(xneed, cnt, float(CAP), None, ALU.is_gt))
            for m in range(2, MORE + 1):
                link(stt(xneed, cnt, float(CAP * m), xneed, ALU.is_gt, ALU.add))
            link(v.memset(ohx, 1.0))
            link(v.tensor_tensor_scan(xend, ohx, xneed, 0.0, ALU.mult, ALU.add))
            link(ts(ohy, xend, rcol[:, 0:1], None, ALU.is_le))
            link(v.tensor_reduce(xcol[:, 0:1], ohy, AX.X, ALU.add))
            link(ts(ohx, iotaE, xcol[:, 0:1], None, ALU.is_equal))
            link(tt(ohy, xneed, ohy, ALU.mult))
            link(v.tensor_reduce(xcol[:, 1:2], ohy, AX.X, ALU.add))
            link(tt(xcol[:, 1:2], rcol[:, 0:1], xcol[:, 1:2], ALU.subtract))
            link(ts(xcol[:, 1:2], xcol[:, 1:2], 1.0, float(CAP), ALU.add, ALU.mult))
            link(ts(xcol[:, 0:1], xcol[:, 0:1], float(NE - 1), None, ALU.min))
            link(v.memset(xcol[:, 2:8], 0.0))
            done("ohx")
            v.wait_ge(sem("routes_turned"), 1)
            link(v.tensor_copy(wT, ps[0:NE, 6, 0:T]))
            link(v.tensor_copy(posT, ps[0:NE, 6, T:2 * T]))
            done("wT")
            v.wait_ge(sem("xcols"), 1)
            link(v.tensor_copy(ohT[:, 0:XP], ps[0:NE, 0, 0:XP]))
            link(v.tensor_copy(xe_i[:, 0:XP], ps[0:1, 0, P:P + XP]))
            link(v.tensor_copy(chk[0:8, 0:XP], ps[0:8, 0, P:P + XP]))
            link(ts(rcol[:, 1:2], rcol[:, 0:1], 1.0, None, ALU.is_equal))
            link(ts(pick1, ones[0:8, :], rcol[0:8, 1:2], None, ALU.mult))
            link(v.tensor_copy(xn_i, xend[0:1, NE - 1:NE]))
            for j in range(3):
                link(v.tensor_copy(oh96[32 * j:32 * j + 32, NE:NE + XP], ps[0:NE, 0, 0:XP]))
            done("xtab")
            done("ohT")

            v.wait_ge(sem("rows"), 1)
            select(1)
            select_w(0)
            swiglu(0)
            expert_rows(1)
            with v.Fori(1, NE - 1) as q:
                v.wait_ge(sem("rows"), q + 1)
                select(q + 1)
                v.wait_ge(sem("act_turned"), q)
                select_w(q)
                swiglu(q)
                expert_rows(q + 1)
            v.wait_ge(sem("xmats"), 1)
            for t in range(TT):
                link(v.tensor_copy(posP[:, t, NE:NE + XP], ps[:, 6, t * 32:t * 32 + XP]))
                link(tt(posP[:, t, NE:NE + XP], posP[:, t, NE:NE + XP], ps[:, 6, 128:128 + XP], ALU.subtract))
                link(v.tensor_copy(wP[:, t, NE:NE + XP], ps[:, 6, 64 + t * 32:64 + t * 32 + XP]))
            done("tables")
            v.wait_ge(sem("act_turned"), NE - 1)
            select_w(NE - 1)
            swiglu(NE - 1)
            more = v.value_load(xn_i, min_val=0, max_val=XP)
            with v.Fori(0, XP) as i:
                with v.If(more > i):
                    v.wait_ge(sem("act_turned"), i + NE)
                    select(i + NE)
                    expert_rows(i + NE)
                    select_w(i + NE)
                    swiglu(i + NE)
            for t in range(TT):
                for h in range(2):
                    v.wait_ge(sem("scattered"), more * (2 * TT) + (2 * TT * (NE - 1) + 2 * t + h + 1))
                    tmp = A1[:, t * 1024 + h * 512:t * 1024 + (h + 1) * 512]
                    link(tt(tmp, ps[:, 2 * t + h, :], gate2[:, h * 512:(h + 1) * 512], ALU.mult))
                    tt(xs[:, t, h * 512:(h + 1) * 512], xs[:, t, h * 512:(h + 1) * 512], tmp, ALU.add).then_inc(sem("out_ready"), 1)


_INS = ["x", "c", "positions", "ada_w", "ada_b", "norm1_g", "w_in", "q_norm_g", "k_norm_g",
        "cmp_pe_k", "cmp_pe_v", "cmp_wk1", "cmp_wk2", "cmp_wv1", "cmp_wv2",
        "conv_w", "conv_b", "lru_wa", "lru_ba", "lru_wx", "lru_bx", "lru_lambda",
        "w_branch_out", "w_out", "norm2_g", "router_w", "router_b", "moe_w1", "moe_b1", "moe_w2", "moe_b2"]


def kernel(**inputs):
    import concourse.bacc as bacc
    from concourse.bass_utils import run_bass_kernel_spmd

    nc = bacc.Bacc("TRN2", target_bir_lowering=False, num_devices=1)
    inv = (10000.0 ** (-np.arange(0, DH, 2, dtype=np.float64) / DH)).astype(np.float32)[None, :]
    arrays, args = {}, {}
    for name in _INS + ["inv_freq"]:
        arr = np.ascontiguousarray(inputs[name]) if name in inputs else inv
        arrays[f"in_{name}"] = arr
        args[name] = nc.dram_tensor(f"in_{name}", arr.shape, mybir.dt.from_np(arr.dtype), kind="ExternalInput").ap()
    args["out"] = nc.dram_tensor("out_x", (1, T, D), F32, kind="ExternalOutput").ap()
    build_program(nc, **args)
    r = run_bass_kernel_spmd(nc, [arrays], core_ids=[0])
    return r.results[0]["out_x"]
```
